# Optimizing a Trainium2 kernel written in Bass

```python
import jax, jax.numpy as jnp
from jax import lax
import numpy as np

D_MODEL = 1024
BATCH = 1
SEQ = 1024
DEPTH = 1

N_META = 16
BLOCK = 128
SB_HEADS = 8
SB_HEAD_DIM = 64
SB_WIDTH = SB_HEADS * SB_HEAD_DIM
HG_HEADS = 4
HG_EXPAND = 128
HG_HEAD_DIM = 128
HG_F_WIDTH = HG_HEADS * HG_EXPAND
HG_WIDTH = HG_HEADS * HG_HEAD_DIM
MIX_WIDTH = SB_WIDTH + HG_WIDTH
IN_WIDTH = 3 * SB_WIDTH + 2 * HG_F_WIDTH + 2 * HG_WIDTH
D_FF = -(-8 * D_MODEL // (3 * 256)) * 256
RMS_EPS = 1e-6

kernel_name = "hymba_stickbreak_hgrn2_hybrid"

def rmsnorm(x, g):
    xf = x.astype(jnp.float32)
    y = xf * lax.rsqrt(jnp.mean(xf * xf, axis=-1, keepdims=True) + RMS_EPS)
    return (y * g.astype(jnp.float32)).astype(x.dtype)

def group_rmsnorm(o, g, n_heads):
    B, L, W = o.shape
    of = o.astype(jnp.float32).reshape(B, L, n_heads, W // n_heads)
    of = of * lax.rsqrt(jnp.mean(of * of, axis=-1, keepdims=True) + RMS_EPS)
    return of.reshape(B, L, W) * g.astype(jnp.float32)

def split_heads(a, n_heads):
    B, L, W = a.shape
    return a.reshape(B, L, n_heads, W // n_heads).transpose(0, 2, 1, 3)

def merge_heads(a):
    B, H, L, d = a.shape
    return a.transpose(0, 2, 1, 3).reshape(B, L, H * d)

def stick_breaking_attention(q, k, v, key_valid):
    B, H, L, Dh = q.shape
    nb = L // BLOCK
    scale = Dh ** -0.5
    q_blocks = q.reshape(B, H, nb, BLOCK, Dh).transpose(2, 0, 1, 3, 4)
    key_pos = jnp.arange(L)

    def one_block(args):
        blk, qb = args
        q_pos = blk * BLOCK + jnp.arange(BLOCK)
        z = jnp.einsum('bhqd,bhkd->bhqk', qb, k).astype(jnp.float32) * scale
        visible = (key_pos[None, :] < q_pos[:, None]) & key_valid[None, :]
        log_beta = jax.nn.log_sigmoid(z)
        log_one_minus = jnp.where(visible, jax.nn.log_sigmoid(-z), 0.0)
        later = lax.cumsum(log_one_minus, axis=3, reverse=True) - log_one_minus
        w = jnp.where(visible, jnp.exp(log_beta + later), 0.0)
        return jnp.einsum('bhqk,bhkd->bhqd', w.astype(v.dtype), v)

    out = lax.map(one_block, (jnp.arange(nb), q_blocks))
    return out.transpose(1, 2, 0, 3, 4).reshape(B, H, L, Dh)

def hgrn2_chunkwise(q, k, v, log_f):
    B, H, L, Dk = q.shape
    Dv = v.shape[-1]
    nc = L // BLOCK

    def to_chunks(a):
        return a.astype(jnp.float32).reshape(B, H, nc, BLOCK, a.shape[-1]).transpose(2, 0, 1, 3, 4)

    causal = jnp.tril(jnp.ones((BLOCK, BLOCK), dtype=bool))

    def step(S, inp):
        qc, kc, vc, gc = inp
        b = jnp.cumsum(gc, axis=2)
        diff = b[:, :, :, None, :] - b[:, :, None, :, :]
        decay = jnp.exp(jnp.where(causal[:, :, None], diff, -jnp.inf))
        scores = jnp.einsum('bhtsk,bhsk->bhts', qc[:, :, :, None, :] * decay, kc)
        o = (jnp.einsum('bhts,bhsv->bhtv', scores, vc)
             + jnp.einsum('bhtk,bhkv->bhtv', qc * jnp.exp(b), S))
        b_last = b[:, :, -1:, :]
        S = (S * jnp.exp(b_last[:, :, 0, :, None])
             + jnp.einsum('bhsk,bhsv->bhkv', kc * jnp.exp(b_last - b), vc))
        return S, o

    S0 = jnp.zeros((B, H, Dk, Dv), jnp.float32)
    _, o = lax.scan(step, S0, (to_chunks(q), to_chunks(k), to_chunks(v), to_chunks(log_f)))
    return o.transpose(1, 2, 0, 3, 4).reshape(B, H, L, Dv)

def hybrid_layer(h, key_valid, lower_bound, norm1_g, w_in, sb_norm_g, hg_norm_g, w_out,
                 norm2_g, w_gate, w_up, w_down):
    dt = h.dtype
    u = rmsnorm(h, norm1_g)
    proj = u @ w_in
    cuts = np.cumsum([SB_WIDTH, SB_WIDTH, SB_WIDTH, HG_F_WIDTH, HG_F_WIDTH, HG_WIDTH])
    sb_q, sb_k, sb_v, hg_q, hg_f, hg_i, hg_g = jnp.split(proj, cuts, axis=-1)

    o_sb = stick_breaking_attention(split_heads(sb_q, SB_HEADS), split_heads(sb_k, SB_HEADS),
                                    split_heads(sb_v, SB_HEADS), key_valid)
    o_sb = group_rmsnorm(merge_heads(o_sb), sb_norm_g, SB_HEADS)

    lb = lower_bound.astype(jnp.float32)
    log_f = jnp.logaddexp(jnp.log(lb), jnp.log1p(-lb) + jax.nn.log_sigmoid(hg_f.astype(jnp.float32)))
    hg_k = -jnp.expm1(log_f)
    valid = key_valid[None, :, None]
    log_f = jnp.where(valid, log_f, 0.0)
    hg_k = jnp.where(valid, hg_k, 0.0)
    o_hg = hgrn2_chunkwise(split_heads(hg_q, HG_HEADS), split_heads(hg_k, HG_HEADS),
                           split_heads(hg_i, HG_HEADS), split_heads(log_f, HG_HEADS))
    o_hg = group_rmsnorm(merge_heads(o_hg), hg_norm_g, HG_HEADS) * jax.nn.silu(hg_g.astype(jnp.float32))

    mix = jnp.concatenate([o_sb, o_hg], axis=-1).astype(dt) @ w_out
    h = h + mix

    u2 = rmsnorm(h, norm2_g)
    ffn = (jax.nn.silu(u2 @ w_gate) * (u2 @ w_up)) @ w_down
    return h + ffn

def setup_inputs(seed: int = 0) -> dict:
    key = jax.random.key(seed)
    ks = jax.random.split(key, 16)
    f32 = jnp.float32
    nrm = lambda k, shape, s: jax.random.normal(k, shape, f32) * s
    return {
        "x": nrm(ks[0], (BATCH, SEQ, D_MODEL), 1.0),
        "meta_tokens": nrm(ks[1], (N_META, D_MODEL), 1.0),
        "norm1_g": 1.0 + nrm(ks[2], (DEPTH, D_MODEL), 0.02),
        "w_in": nrm(ks[3], (DEPTH, D_MODEL, IN_WIDTH), D_MODEL ** -0.5),
        "sb_norm_g": 1.0 + nrm(ks[4], (DEPTH, SB_WIDTH), 0.02),
        "hg_norm_g": 1.0 + nrm(ks[5], (DEPTH, HG_WIDTH), 0.02),
        "hg_lb_logits": nrm(ks[6], (DEPTH + 1, HG_F_WIDTH), 0.5),
        "w_out": nrm(ks[7], (DEPTH, MIX_WIDTH, D_MODEL), MIX_WIDTH ** -0.5),
        "norm2_g": 1.0 + nrm(ks[8], (DEPTH, D_MODEL), 0.02),
        "w_gate": nrm(ks[9], (DEPTH, D_MODEL, D_FF), D_MODEL ** -0.5),
        "w_up": nrm(ks[10], (DEPTH, D_MODEL, D_FF), D_MODEL ** -0.5),
        "w_down": nrm(ks[11], (DEPTH, D_FF, D_MODEL), D_FF ** -0.5),
        "final_norm_g": 1.0 + nrm(ks[12], (D_MODEL,), 0.02),
    }

def reference(x, meta_tokens, norm1_g, w_in, sb_norm_g, hg_norm_g, hg_lb_logits, w_out,
              norm2_g, w_gate, w_up, w_down, final_norm_g):
    B = x.shape[0]
    pad = jnp.zeros((B, BLOCK - N_META, D_MODEL), x.dtype)
    meta = jnp.broadcast_to(meta_tokens.astype(x.dtype)[None], (B, N_META, D_MODEL))
    h = jnp.concatenate([pad, meta, x], axis=1)
    L = h.shape[1]
    key_valid = jnp.arange(L) >= (BLOCK - N_META)
    lower_bounds = jnp.cumsum(jax.nn.softmax(hg_lb_logits.astype(jnp.float32), axis=0), axis=0)
    for layer in range(DEPTH):
        h = hybrid_layer(h, key_valid, lower_bounds[layer], norm1_g[layer], w_in[layer],
                         sb_norm_g[layer], hg_norm_g[layer], w_out[layer], norm2_g[layer],
                         w_gate[layer], w_up[layer], w_down[layer])
    h = rmsnorm(h, final_norm_g)
    return h[:, BLOCK:, :]


_drawn_inputs = setup_inputs


def setup_inputs(seed=0):
    import zlib

    import numpy as np

    out = dict(_drawn_inputs(seed))
    spreads = {}
    factors = {'sb_norm_g': 4.888, 'hg_norm_g': 7.726, 'norm2_g': 4.975, 'final_norm_g': 2.889}
    for name, (base, spread) in spreads.items():
        noise = np.random.default_rng([zlib.crc32(name.encode()), seed]).standard_normal(out[name].shape)
        drawn = base * np.exp(spread * noise) if base else spread * noise
        out[name] = __import__('jax').numpy.asarray(drawn.astype(out[name].dtype))
    for name, factor in factors.items():
        out[name] = (out[name] * factor).astype(out[name].dtype)
    return out
```

```python
import concourse.bass as bass
from concourse import mybir
from contextlib import ExitStack

F32 = mybir.dt.float32
F32R = mybir.dt.float32r
BF16 = mybir.dt.bfloat16
I32 = mybir.dt.int32
ALU = mybir.AluOpType
ACT = mybir.ActivationFunctionType

P = 128
D = 1024
SEQ = 1024
META = 16
L = SEQ + META
KT = D // P
TT = SEQ // P
SB_HEADS, SB_DIM = 8, 64
HG_HEADS, HG_DIM = 4, 128
SB_WIDTH = SB_HEADS * SB_DIM
HG_WIDTH = HG_HEADS * HG_DIM
SBQ, SBK, SBV, HGQ, HGF, HGI, HGG = (512 * n for n in range(7))
D_FF = -(-8 * D // (3 * 256)) * 256
FG = D_FF // 256
EPS = 1e-6
SB_SCALE = SB_DIM ** -0.5
MASKED = -1e30
CW = 256
CHUNK = KT * CW
HALF = 512
UNIT = 4
LEVELS = [1, 2, 4, 8, 16, 32, 64]


class Signal:

    def __init__(self, sem, per=0, credit=0):
        self.sem, self.per, self.credit = sem, per, credit

    def done(self, i, n):
        return i * self.per + (self.credit + n)

    def free(self, i, n):
        return i * self.per + n


def key_tiles(lo, hi):
    tiles = [(0, META, TT)] if lo == 0 else []
    return tiles + [(META + P * j, P, j) for j in range(TT) if lo <= META + P * j < hi]


def attention_pieces():
    out, unit = [], 0
    for pair in range(2):
        for blk in range(TT):
            width = META + P * (blk + 1)
            cuts = [(0, width)] if width <= 2 * HALF else [(META + HALF, width), (0, META + HALF)]
            for par in range(2):
                out += [(pair, blk, par, lo, hi, width, unit % 2) for lo, hi in cuts]
                unit += 1
    return out


PIECES = attention_pieces()
GROUPS = []
for _n, (_pair, _blk, _par, _lo, _hi, _w, _u) in enumerate(PIECES):
    _t = key_tiles(_lo, _hi)
    _t = _t[1:] + _t[:1] if _lo == 0 else _t
    for _a in range(0, len(_t), 4):
        GROUPS.append((_n, _t[_a:_a + 4], _hi == _w and _a == 0, _lo == 0 and _a + 4 >= len(_t)))
GROUPS_OF = [[g for g, x in enumerate(GROUPS) if x[0] == n] for n in range(len(PIECES))]


def hybrid_layer(nc, x, meta, norm1_g, w_in, sb_g, hg_g, lb_logits, w_out, norm2_g,
                 w_gate, w_up, w_down, final_g, out):
    x2 = x[0]
    out2 = out[0]
    w_in_v = w_in[0].rearrange("(k p) n -> p k n", p=P)
    w_out_v = w_out[0].rearrange("(k p) n -> p k n", p=P)
    w_gate_v = w_gate[0].rearrange("(k p) n -> p k n", p=P)
    w_up_v = w_up[0].rearrange("(k p) n -> p k n", p=P)
    w_down_v = w_down[0].rearrange("(f p) n -> p f n", p=P)

    ctx = ExitStack()
    with ctx:
        def sb(name, shape, dt=F32, stack=ctx):
            return stack.enter_context(nc.sbuf_tensor(name, shape, dt))

        def signal(name, per=0, credit=0):
            return Signal(ctx.enter_context(nc.semaphore(name)), per, credit)

        ident = sb("ident", [P, P])
        ident_bf = sb("ident_bf", [P, P], BF16)
        hidden_bf = sb("hidden_bf", [P, P], BF16)
        ones = sb("ones", [P, P])
        ones_pair = sb("ones_pair", [P, P])
        level_mask = sb("level_mask", [P, len(LEVELS), P // 2])
        gain = sb("gain", [P, D])
        small = sb("small", [P, 64])
        sbg, hgg = small[:, 0:4], small[:, 4:8]
        logit0, logit1 = small[:, 8:12], small[:, 12:16]
        lower, one_minus = small[:, 16:20], small[:, 20:24]
        lower_x, one_x = small[:, 24:28], small[:, 28:32]
        ssq, std, rstd = small[:, 32:34], small[:, 34:36], small[:, 36:38]
        eps = small[:, 38:39]
        meta_decay = sb("meta_decay", [P, 2 * META])
        act_hi = sb("act_hi", [P, KT, L], F32R)
        act_lo = sb("act_lo", [P, KT, L], F32R)
        w_raw = sb("w_raw", [P, CHUNK])
        w_hi = sb("w_hi", [P, 2, CHUNK], F32R)
        w_lo = sb("w_lo", [P, 2, CHUNK], F32R)

        heads = ExitStack()
        mixed = sb("mixed", [P, KT, SEQ], stack=heads)
        U = UNIT * P
        with ExitStack() as hg:
            hq = sb("hq", [P, 2, SEQ], stack=hg)
            hf = sb("hf", [P, 2, L], stack=hg)
            hk = sb("hk", [P, 2, L], stack=hg)
            hv = sb("hv", [P, TT + 1, CW], stack=hg)
            kd = {h: sb(f"kd{h}", [P, U], stack=hg) for h in (8, 16, 32, 64, 128)}
            qd = {h: sb(f"qd{h}", [P, U], stack=hg) for h in (64, 128)}
            spare = mixed[:, 0:4, :].rearrange("p a b -> p (a b)")
            for n, h in enumerate((2, 4)):
                kd[h] = spare[:, n * U:(n + 1) * U]
            for n, h in enumerate((1, 2, 4, 8, 16, 32)):
                qd[h] = spare[:, (2 + n) * U:(3 + n) * U]
            masked = spare[:, 0:4 * U]
            fac = {h: sb(f"fac{h}", [P, U // (2 * h), 4], stack=hg) for h in LEVELS[1:]}
            total = sb("total", [P, UNIT], stack=hg)
            scores = sb("scores", [P, U], stack=hg)
            kd_nat = sb("kd_nat", [P, U], stack=hg)
            state = sb("state", [P, UNIT + 1, P], stack=hg)
            gate_sig = sb("gate_sig", [P, HALF], stack=hg)
        with ExitStack() as at:
            sq = sb("sq", [P, 2, SEQ], stack=at)
            sk = sb("sk", [P, 2, L], stack=at)
            sv = sb("sv", [P, TT + 1, CW], stack=at)
            beta = sb("beta", [P, 2, L], stack=at)
            later = sb("later", [P, 2, L], stack=at)
            probs = sb("probs", [P, 2, L], stack=at)
            probs_t = sb("probs_t", [P, 2, HALF], stack=at)
        with ExitStack() as first:
            x_in = sb("x_in", [P, 2, D], stack=first)
            x_norm = sb("x_norm", [P, 2, D], stack=first)
        heads.close()
        with ExitStack() as ff:
            h_res = sb("h_res", [P, TT, D], stack=ff)
            with ExitStack() as ff2:
                f_hi = sb("f_hi", [P, 2, 2, SEQ], F32R, stack=ff2)
                f_lo = sb("f_lo", [P, 2, 2, SEQ], F32R, stack=ff2)
                d_hi = sb("d_hi", [P, CHUNK], F32R, stack=ff2)
                d_lo = sb("d_lo", [P, CHUNK], F32R, stack=ff2)
                silu = sb("silu", [P, 2, HALF], stack=ff2)
            h_norm = sb("h_norm", [P, 2, D], stack=ff)
            h_sq = sb("h_sq", [P, 2, D], stack=ff)

        ps = ctx.enter_context(nc.psum_tensor("ps", [P, 8 * HALF], F32))

        def bank(n, w=HALF, rows=P):
            return ps[0:rows, n * HALF:n * HALF + w]

        def three(psum, w_parts, a_parts, k, weights_stay):
            wh, wl = w_parts
            ah, al = a_parts
            order = ((wh, ah), (wh, al), (wl, ah)) if weights_stay else ((ah, wh), (ah, wl), (al, wh))
            for n, (stay, move) in enumerate(order):
                last = nc.tensor.matmul(psum, stay, move, start=k == 0 and n == 0, stop=k == KT - 1 and n == 2)
            return last

        class Norm:
            def __init__(self, name, src, dst, square, with_meta):
                self.src, self.dst, self.square, self.with_meta = src, dst, square, with_meta
                self.summed = signal(name + "_summed", 2)
                self.rooted = signal(name + "_rooted", 2)
                self.inverted = signal(name + "_inverted", 2)
                self.normed = signal(name + "_normed", 2, 2)
                self.turned = signal(name + "_turned", 2, 2)
                self.hi = signal(name + "_hi", 4)
                self.lo = signal(name + "_lo", 4, 4)

            def on_scalar(self, act, arrived):
                N = self

                def stats(r, s, rows):
                    arrived(r, s, rows)
                    act.wait_ge(N.turned.sem, N.turned.free(r, s + 1))
                    nc.scalar.activation(N.square[0:rows, s], N.src(r, s, rows), ACT.Square,
                                         accum_out=ssq[0:rows, s:s + 1]).then_inc(N.summed.sem, 1)
                    act.wait_ge(N.summed.sem, N.summed.done(r, s + 1))
                    nc.scalar.activation(std[0:rows, s:s + 1], ssq[0:rows, s:s + 1], ACT.Sqrt,
                                         scale=1.0 / D, bias=eps[0:rows]).then_inc(N.rooted.sem, 1)

                def high(r, s, rows):
                    act.wait_ge(N.turned.sem, N.turned.done(r, s + 1))
                    cols = slice(SEQ, L) if rows == META else bass.ts(2 * r + s, P)
                    for b in range(2):
                        src = bank(2 * s + b).rearrange("p (k t) -> p k t", k=4)[:, :, 0:rows]
                        nc.scalar.activation(act_hi[:, 4 * b:4 * b + 4, cols], src, ACT.Copy).then_inc(N.hi.sem, 1)

                with act.Fori(0, TT // 2) as r:
                    for s in range(2):
                        stats(r, s, P)
                    for s in range(2):
                        high(r, s, P)
                if N.with_meta:
                    stats(TT // 2, 0, META)
                    high(TT // 2, 0, META)

            def on_vector(self, dve):
                N = self

                def scale(r, s, rows):
                    dve.wait_ge(N.rooted.sem, N.rooted.done(r, s + 1))
                    nc.vector.reciprocal(rstd[0:rows, s:s + 1], std[0:rows, s:s + 1]).then_inc(N.inverted.sem, 1)
                    dve.wait_ge(N.inverted.sem, N.inverted.done(r, s + 1))
                    nc.vector.scalar_tensor_tensor(N.dst[0:rows, s], N.src(r, s, rows), rstd[0:rows, s:s + 1],
                                                   gain[0:rows], ALU.mult, ALU.mult).then_inc(N.normed.sem, 1)

                def low(r, s, rows):
                    cols = slice(SEQ, L) if rows == META else bass.ts(2 * r + s, P)
                    for b in range(2):
                        dve.wait_ge(N.hi.sem, N.hi.done(r, 2 * s + b + 1))
                        src = bank(2 * s + b).rearrange("p (k t) -> p k t", k=4)[:, :, 0:rows]
                        nc.vector.tensor_tensor(act_lo[:, 4 * b:4 * b + 4, cols], src,
                                                act_hi[:, 4 * b:4 * b + 4, cols].bitcast(F32),
                                                ALU.subtract).then_inc(N.lo.sem, 1)

                dve.sem_inc(N.normed.sem, 2)
                dve.sem_inc(N.lo.sem, 4)
                with dve.Fori(0, TT // 2) as r:
                    for s in range(2):
                        scale(r, s, P)
                    for s in range(2):
                        low(r, s, P)
                if N.with_meta:
                    scale(TT // 2, 0, META)
                    low(TT // 2, 0, META)

            def on_tensor(self, pe):
                N = self

                def transposes(r, s, rows):
                    pe.wait_ge(N.normed.sem, N.normed.done(r, s + 1))
                    pe.wait_ge(N.lo.sem, N.lo.free(r, 2 * s + 2))
                    for k in range(KT):
                        last = nc.tensor.transpose(bank(2 * s + k // 4)[:, (k % 4) * P:(k % 4) * P + rows],
                                                   N.dst[0:rows, s, k * P:(k + 1) * P], ident[0:rows, 0:rows])
                    last.then_inc(N.turned.sem, 1)

                pe.sem_inc(N.turned.sem, 2)
                with pe.Fori(0, TT // 2) as r:
                    for s in range(2):
                        transposes(r, s, P)
                if N.with_meta:
                    transposes(TT // 2, 0, META)

        consts, gain1, filled = signal("consts"), signal("gain1"), signal("filled")
        eps_set, bounds = signal("eps_set"), signal("bounds")
        x_came = [signal("x_came0", 16), signal("x_came1", 16)]
        n1 = Norm("n1", lambda r, s, rows: x_in[0:rows, s], x_norm, x_norm, True)

        with nc.Block() as blk:
            @blk.sync
            def _(sp):
                with sp.Fori(0, TT // 2) as r:
                    for s in range(2):
                        sp.wait_ge(n1.normed.sem, n1.normed.free(r, s + 1))
                        sp.dma_start(x_in[:, s], x2[bass.ts(2 * r + s, P), :]).then_inc(x_came[s].sem, 16)
                sp.wait_ge(n1.normed.sem, n1.normed.free(TT // 2, 1))
                sp.dma_start(x_in[0:META, 0], meta).then_inc(x_came[0].sem, 16)

            @blk.gpsimd
            def _(pool):
                pool.dma_start(gain[:], norm1_g[0:1, :].to_broadcast([P, D])).then_inc(gain1.sem, 16)
                with nc.allow_non_contiguous_dma(reason="a gain for each partition"):
                    for dst, src in ((sbg, sb_g[0]), (hgg, hg_g[0]), (logit0, lb_logits[0]), (logit1, lb_logits[1])):
                        pool.dma_start(dst, src.rearrange("(t p) -> p t", p=P)).then_inc(consts.sem, 16)
                nc.gpsimd.memset(ident[:], 0.0)
                nc.gpsimd.memset(ones[:], 1.0)
                nc.gpsimd.memset(ones_pair[:], 1.0)
                nc.gpsimd.memset(level_mask[:], 1.0)
                nc.gpsimd.memset(hidden_bf[:], 0.0).then_inc(filled.sem, 1)
                pool.wait_ge(filled.sem, 1)
                nc.gpsimd.affine_select(out=ident[:], in_=ident[:], compare_op=ALU.not_equal, fill=1.0,
                                        base=0, pattern=[[-1, P]], channel_multiplier=1).then_inc(filled.sem, 1)
                nc.gpsimd.affine_select(out=ones_pair[:, 0:64], in_=ones_pair[:, 0:64], compare_op=ALU.is_ge,
                                        fill=0.0, base=63, pattern=[[0, 64]], channel_multiplier=-1)
                nc.gpsimd.affine_select(out=ones_pair[:, 64:P], in_=ones_pair[:, 64:P], compare_op=ALU.is_ge,
                                        fill=0.0, base=-64, pattern=[[0, 64]], channel_multiplier=1)
                nc.gpsimd.affine_select(out=hidden_bf[:], in_=hidden_bf[:], compare_op=ALU.is_gt, fill=MASKED,
                                        base=0, pattern=[[-1, P]], channel_multiplier=1)
                for n, h in enumerate(LEVELS):
                    m = level_mask[:, n, :].rearrange("p (b j) -> p b j", j=h)
                    nc.gpsimd.affine_select(out=m, in_=m, compare_op=ALU.is_ge, fill=0.0, base=0,
                                            pattern=[[-2 * h, P // (2 * h)], [0, h]], channel_multiplier=1)\
                        .then_inc(filled.sem, 1)
                    pool.wait_ge(filled.sem, 3 + 2 * n)
                    nc.gpsimd.affine_select(out=m, in_=m, compare_op=ALU.is_ge, fill=0.0, base=h - 1,
                                            pattern=[[2 * h, P // (2 * h)], [0, h]], channel_multiplier=-1)\
                        .then_inc(filled.sem, 1)

            @blk.scalar
            def _(act):
                act.wait_ge(eps_set.sem, 1)
                n1.on_scalar(act, lambda r, s, rows: act.wait_ge(x_came[s].sem, x_came[s].done(r, 16)))
                act.wait_ge(bounds.sem, 2)
                nc.scalar.activation(lower, lower_x, ACT.Sigmoid)
                nc.scalar.activation(one_minus, one_x, ACT.Sigmoid).then_inc(bounds.sem, 1)

            @blk.vector
            def _(dve):
                nc.vector.memset(eps, EPS).then_inc(eps_set.sem, 1)
                dve.wait_ge(consts.sem, 64)
                nc.vector.tensor_tensor(lower_x, logit0, logit1, ALU.subtract).then_inc(bounds.sem, 1)
                nc.vector.tensor_tensor(one_x, logit1, logit0, ALU.subtract).then_inc(bounds.sem, 1)
                dve.wait_ge(filled.sem, 2)
                nc.vector.tensor_copy(ident_bf[:], ident[:])
                dve.wait_ge(gain1.sem, 16)
                n1.on_vector(dve)

            @blk.tensor
            def _(pe):
                pe.wait_ge(filled.sem, 2)
                n1.on_tensor(pe)

        class Weights:

            def __init__(self, name, per):
                self.came = signal(name + "_came", 16 * per)
                self.hi = signal(name + "_hi", per)
                self.lo = signal(name + "_lo", per, 1)
    
            def load(self, sp, i, n, src):
                sp.wait_ge(self.lo.sem, self.lo.free(i, n))
                sp.dma_start(w_raw[:].rearrange("p (k n) -> p k n", k=KT), src).then_inc(self.came.sem, 16)

            def high(self, act, i, n, used, value):
                act.wait_ge(self.came.sem, self.came.done(i, 16 * n))
                act.wait_ge(used.sem, value)
                nc.scalar.activation(w_hi[:, (n - 1) % 2], w_raw[:], ACT.Copy).then_inc(self.hi.sem, 1)

            def low(self, dve, i, n):
                dve.wait_ge(self.hi.sem, self.hi.done(i, n))
                nc.vector.tensor_tensor(w_lo[:, (n - 1) % 2], w_raw[:], w_hi[:, (n - 1) % 2].bitcast(F32),
                                        ALU.subtract).then_inc(self.lo.sem, 1)

        def turned_group(slot, tile, cols, psum, ready=None):
            for k in range(KT):
                c = slice(k * CW + tile * P, k * CW + tile * P + P)
                last = three(psum, (w_hi[:, slot, c], w_lo[:, slot, c]),
                             (act_hi[:, k, cols], act_lo[:, k, cols]), k, True)
            return last

        def natural_group(slot, cols, psum):
            for k in range(KT):
                c = slice(k * CW, (k + 1) * CW)
                last = three(psum, (w_hi[:, slot, c], w_lo[:, slot, c]),
                             (act_hi[:, k, cols], act_lo[:, k, cols]), k, False)
            return last

        X_PARTS = [slice(0, HALF), slice(HALF, SEQ)]
        ALL_PARTS = X_PARTS + [slice(SEQ, L)]
        TOKEN_TILES = [slice(t * P, (t + 1) * P) for t in range(TT)] + [slice(SEQ, L)]

        def right(ap, h):
            return ap.rearrange("p (b two j) -> p b two j", two=2, j=h)[:, :, 1, :]

        HG_GROUPS = 2 * len(ALL_PARTS) + 2 * len(X_PARTS) + len(TOKEN_TILES)
        hw = Weights("hw", 4)
        h_proj = signal("h_proj", HG_GROUPS, 1)
        h_evac = signal("h_evac", HG_GROUPS)
        gates = signal("gates", 2)
        tree = signal("tree", 4 * 8)
        scored = signal("scored", 4)
        placed = signal("placed", 4 * 12, 48)
        k_turned = signal("k_turned", 4)
        k_nat = signal("k_nat", 4)
        grown = signal("grown", 4)
        advanced = signal("advanced", 4 * 4)
        meta_k = signal("meta_k", 2 * 2)
        meta_turned, meta_nat, meta_grown = signal("meta_turned", 2), signal("meta_nat", 2), signal("meta_grown", 2)
        started = signal("started", 4)
        o_done, o_evac = signal("o_done", 4), signal("o_evac", 4)
        g_proj, g_evac = signal("g_proj", 4, 1), signal("g_evac", 4)
        g_silu = signal("g_silu", 4, 1)
        h_square, h_sum, h_root = signal("h_square", 4), signal("h_sum", 4), signal("h_root", 4)
        h_inv = signal("h_inv", 4)
        h_scaled = signal("h_scaled", 4)
        h_mixed = signal("h_mixed", 4, 4)
        fills = signal("fills")
        UNITS = [(0, 0), (0, 1), (1, 0), (1, 1)]
        MIX_HG = SB_WIDTH // P

        with nc.Block() as blk:
            @blk.sync
            def _(sp):
                with sp.Fori(0, 2) as i:
                    for n, at0 in enumerate((HGF, HGQ, HGI, HGG)):
                        hw.load(sp, i, n + 1, w_in_v[:, :, bass.ds(at0 + i * CW, CW)])

            @blk.gpsimd
            def _(pool):
                for h in LEVELS[1:]:
                    last = nc.gpsimd.memset(fac[h][:], 1.0)
                last.then_inc(fills.sem, 1)

            @blk.scalar
            def _(act):
                with act.Fori(0, 2) as i:
                    def evac(n, dst, func=ACT.Copy, **kw):
                        act.wait_ge(h_proj.sem, h_proj.done(i, n + 1))
                        return nc.scalar.activation(dst, bank(n % 4, dst.shape[-1], dst.shape[0]), func, **kw)

                    hw.high(act, i, 1, h_proj, h_proj.done(i, 0))
                    hw.high(act, i, 2, g_proj, g_proj.done(i, 0))
                    n = 0
                    for t in range(2):
                        for cols in ALL_PARTS:
                            evac(n, hf[:, t, cols], ACT.Sigmoid)
                            evac(n, hk[:, t, cols], ACT.Sigmoid, scale=-1.0).then_inc(h_evac.sem, 1)
                            n += 1
                    hw.high(act, i, 3, h_proj, h_proj.done(i, 6))
                    act.wait_ge(h_mixed.sem, h_mixed.free(i, 4))
                    for t in range(2):
                        for cols in X_PARTS:
                            evac(n, hq[:, t, cols]).then_inc(h_evac.sem, 1)
                            n += 1
                    hw.high(act, i, 4, h_proj, h_proj.done(i, 10))
                    for t, cols in enumerate(TOKEN_TILES):
                        evac(n, hv[0:cols.stop - cols.start, t, :]).then_inc(h_evac.sem, 1)
                        n += 1
                    for u, (hh, half) in enumerate(UNITS):
                        if half == 0:
                            act.wait_ge(meta_turned.sem, meta_turned.done(i, hh + 1))
                            nc.scalar.activation(kd_nat[0:META, 0:P], bank(7, P, META), ACT.Copy)\
                                .then_inc(meta_nat.sem, 1)
                            act.wait_ge(meta_grown.sem, meta_grown.done(i, hh + 1))
                        act.wait_ge(k_turned.sem, k_turned.done(i, u + 1))
                        nc.scalar.activation(kd_nat[:], bank(7), ACT.Copy).then_inc(k_nat.sem, 1)
                        act.wait_ge(g_proj.sem, g_proj.done(i, u + 1))
                        act.wait_ge(g_silu.sem, g_silu.free(i, u + 1))
                        nc.scalar.activation(gate_sig[:], bank(7), ACT.Sigmoid)
                        nc.scalar.activation(hq[:, hh, X_PARTS[half]], bank(7), ACT.Copy).then_inc(g_evac.sem, 1)
                        act.wait_ge(o_done.sem, o_done.done(i, u + 1))
                        nc.scalar.activation(mixed[:, MIX_HG + 2 * i + hh, X_PARTS[half]], bank(5), ACT.Copy)\
                            .then_inc(o_evac.sem, 1)
                    root_tmp = (kd[8], kd[16])
                    for u in range(4):
                        act.wait_ge(h_sum.sem, h_sum.done(i, u + 1))
                        if u >= 2:
                            act.wait_ge(h_scaled.sem, h_scaled.done(i, u - 1))
                        nc.scalar.activation(root_tmp[u % 2][:], bank(5 + u % 2), ACT.Sqrt, scale=1.0 / HG_DIM,
                                             bias=eps).then_inc(h_root.sem, 1)

            @blk.vector
            def _(dve):
                dve.sem_inc(hw.lo.sem, 1)
                dve.sem_inc(placed.sem, 48)
                dve.sem_inc(g_silu.sem, 1)
                dve.sem_inc(h_mixed.sem, 4)
                dve.wait_ge(fills.sem, 1)
                with dve.Fori(0, 2) as i:
                    def build_tree(u, hh, half):
                        cols = X_PARTS[half]
                        q, f, k = hq[:, hh, cols], hf[:, hh, cols], hk[:, hh, cols]

                        def stage(ins, n):
                            ins.then_inc(tree.sem, 1)
                            dve.wait_ge(tree.sem, tree.done(i, 8 * u + n))

                        def lr(ap, h, side):
                            return ap.rearrange("p (b two j) -> p b two j", two=2, j=h)[:, :, side, :]

                        f4 = f.rearrange("p (b l e) -> p b l e", l=2, e=2)
                        nc.vector.tensor_tensor(fac[2][:, :, 1:3], f4[:, :, :, 0], f4[:, :, :, 1], ALU.mult)
                        nc.vector.tensor_tensor(lr(kd[2], 1, 0), lr(k, 1, 0), lr(f, 1, 1), ALU.mult)
                        nc.vector.tensor_copy(lr(kd[2], 1, 1), lr(k, 1, 1))
                        stage(nc.vector.tensor_tensor(qd[1], q, f, ALU.mult), 1)
                        nc.vector.tensor_tensor(lr(qd[2], 1, 1), lr(qd[1], 1, 1), lr(f, 1, 0), ALU.mult)
                        nc.vector.tensor_copy(lr(qd[2], 1, 0), lr(qd[1], 1, 0))

                        def next_total(h):
                            src = fac[h]
                            if h == P // 2:
                                return nc.vector.tensor_tensor(total[:], src[:, :, 1], src[:, :, 2], ALU.mult)
                            s4 = src[:].rearrange("p (b l) e -> p b l e", l=2)
                            return nc.vector.tensor_tensor(fac[2 * h][:, :, 1:3], s4[:, :, :, 1], s4[:, :, :, 2],
                                                           ALU.mult)

                        stage(next_total(2), 2)
                        for n, h in enumerate(LEVELS[1:]):
                            if h == P // 2:
                                if u:
                                    dve.wait_ge(o_done.sem, o_done.done(i, u))
                            m = U // (2 * h)
                            keep = fac[h][:, :, 2:4].unsqueeze(3).to_broadcast([P, m, 2, h])
                            take = fac[h][:, :, 0:2].unsqueeze(3).to_broadcast([P, m, 2, h])
                            v = "p (b l j) -> p b l j"
                            last = nc.vector.tensor_tensor(kd[2 * h][:].rearrange(v, l=2, j=h),
                                                           kd[h][:].rearrange(v, l=2, j=h), keep, ALU.mult)
                            last = nc.vector.tensor_tensor(qd[2 * h][:].rearrange(v, l=2, j=h),
                                                           qd[h][:].rearrange(v, l=2, j=h), take, ALU.mult)
                            if h < P // 2:
                                last = next_total(2 * h)
                            stage(last, 3 + n)

                    hw.low(dve, i, 1)
                    hw.low(dve, i, 2)
                    for t in range(2):
                        dve.wait_ge(h_evac.sem, h_evac.done(i, 3 * t + 3))
                        col = 2 * i + t
                        nc.vector.tensor_scalar(hf[:, t], hf[:, t], one_minus[:, bass.ds(col, 1)],
                                                lower[:, bass.ds(col, 1)], ALU.mult, ALU.add)
                        nc.vector.tensor_scalar(hk[:, t], hk[:, t], one_minus[:, bass.ds(col, 1)], None,
                                                ALU.mult).then_inc(gates.sem, 1)
                    hw.low(dve, i, 3)
                    dve.wait_ge(gates.sem, gates.done(i, 2))
                    dve.wait_ge(h_evac.sem, h_evac.done(i, 10))
                    build_tree(0, 0, 0)
                    hw.low(dve, i, 4)
                    for u, (hh, half) in enumerate(UNITS):
                        if half == 0:
                            m = hf[:, hh, SEQ:L]
                            nc.vector.memset(meta_decay[:, META - 1:META], 1.0)
                            nc.vector.tensor_tensor_scan(meta_decay[:, 0:META - 1][:, ::-1], m[:, 1:META][:, ::-1],
                                                         ones[:, 0:META - 1], 1.0, ALU.mult, ALU.mult)\
                                .then_inc(meta_k.sem, 1)
                            dve.wait_ge(meta_k.sem, meta_k.done(i, 2 * hh + 1))
                            nc.vector.tensor_tensor(meta_decay[:, META:], hk[:, hh, SEQ:L], meta_decay[:, 0:META],
                                                    ALU.mult).then_inc(meta_k.sem, 1)
                            dve.wait_ge(meta_grown.sem, meta_grown.done(i, hh + 1))
                            nc.vector.tensor_copy(state[:, 0], bank(6, P)).then_inc(started.sem, 1)
                        else:
                            dve.wait_ge(o_done.sem, o_done.done(i, u))
                            nc.vector.tensor_copy(state[:, 0], state[:, UNIT]).then_inc(started.sem, 1)
                        dve.wait_ge(scored.sem, scored.done(i, u + 1))
                        nc.vector.tensor_tensor(scores[:].rearrange("p (c t) -> p c t", c=UNIT),
                                                bank(0).rearrange("p (c t) -> p c t", c=UNIT),
                                                ident[:].unsqueeze(1).to_broadcast([P, UNIT, P]), ALU.mult)\
                            .then_inc(placed.sem, 1)
                        for b in range(4):
                            levels = min(2, len(LEVELS) - 2 * b)
                            v = "p (l c t) -> p l c t"
                            msk = level_mask[:, 2 * b:2 * b + levels, :].unsqueeze(2)\
                                .to_broadcast([P, levels, UNIT, P // 2])
                            nc.vector.tensor_tensor(
                                masked[:, b * HALF:b * HALF + levels * 2 * P].rearrange(v, l=levels, c=UNIT),
                                bank(1 + b, levels * 2 * P).rearrange(v, l=levels, c=UNIT), msk, ALU.mult)\
                                .then_inc(placed.sem, 1)
                        dve.wait_ge(grown.sem, grown.done(i, u + 1))
                        for c in range(UNIT):
                            if c == 0:
                                dve.wait_ge(started.sem, started.done(i, u + 1))
                            else:
                                dve.wait_ge(advanced.sem, advanced.done(i, 4 * u + c))
                            nc.vector.scalar_tensor_tensor(state[:, c + 1], state[:, c], total[:, c:c + 1],
                                                           bank(6)[:, c * P:(c + 1) * P], ALU.mult, ALU.add)\
                                .then_inc(advanced.sem, 1)
                        for n, h in enumerate(LEVELS):
                            dst = scores[:].rearrange("p (a two j) -> p a two j", two=2, j=h)[:, :, 1, :]
                            src = masked[:, n * 2 * P:(n + 1) * 2 * P].rearrange("p (a j) -> p a j", j=h)
                            dve.wait_ge(placed.sem, placed.done(i, 12 * u + 5 + n))
                            nc.vector.tensor_tensor(dst, dst, src, ALU.add).then_inc(placed.sem, 1)
                        if u + 1 < len(UNITS):
                            dve.wait_ge(advanced.sem, advanced.done(i, 4 * u + 4))
                            build_tree(u + 1, *UNITS[u + 1])
                        dve.wait_ge(g_evac.sem, g_evac.done(i, u + 1))
                        nc.vector.tensor_tensor(hq[:, hh, X_PARTS[half]], hq[:, hh, X_PARTS[half]], gate_sig[:],
                                                ALU.mult).then_inc(g_silu.sem, 1)
                    root_tmp = (kd[8], kd[16])
                    for u, (hh, half) in enumerate(UNITS):
                        m = mixed[:, MIX_HG + 2 * i + hh, X_PARTS[half]]
                        dve.wait_ge(o_evac.sem, o_evac.done(i, 4))
                        if u >= 2:
                            dve.wait_ge(h_sum.sem, h_sum.done(i, u - 1))
                        nc.vector.tensor_tensor((scores, kd_nat)[u % 2][:], m, m, ALU.mult).then_inc(h_square.sem, 1)
                    dve.wait_ge(g_silu.sem, g_silu.done(i, 4))
                    for u, (hh, half) in enumerate(UNITS):
                        dve.wait_ge(h_root.sem, h_root.done(i, u + 1))
                        nc.vector.reciprocal(root_tmp[u % 2][:], root_tmp[u % 2][:]).then_inc(h_inv.sem, 1)
                        dve.wait_ge(h_inv.sem, h_inv.done(i, u + 1))
                        m = mixed[:, MIX_HG + 2 * i + hh, X_PARTS[half]]
                        nc.vector.scalar_tensor_tensor(m, m, hgg[:, bass.ds(2 * i + hh, 1)], root_tmp[u % 2][:],
                                                       ALU.mult, ALU.mult).then_inc(h_scaled.sem, 1)
                        dve.wait_ge(h_scaled.sem, h_scaled.done(i, u + 1))
                        nc.vector.tensor_tensor(m, m, hq[:, hh, X_PARTS[half]], ALU.mult).then_inc(h_mixed.sem, 1)

            @blk.tensor
            def _(pe):
                pe.sem_inc(h_proj.sem, 1)
                pe.sem_inc(g_proj.sem, 1)
                with pe.Fori(0, 2) as i:
                    pe.wait_ge(placed.sem, placed.free(i, 48))
                    n = 0

                    def free_bank(n):
                        if n >= 4:
                            pe.wait_ge(h_evac.sem, h_evac.done(i, n - 3))

                    for chunk, parts in ((1, ALL_PARTS), (2, X_PARTS)):
                        pe.wait_ge(hw.lo.sem, hw.lo.done(i, chunk))
                        for t in range(2):
                            for cols in parts:
                                free_bank(n)
                                last = turned_group(chunk - 1, t, cols, bank(n % 4, cols.stop - cols.start))
                                last.then_inc(h_proj.sem, 1)
                                n += 1
                    pe.wait_ge(hw.lo.sem, hw.lo.done(i, 3))
                    for cols in TOKEN_TILES:
                        free_bank(n)
                        last = natural_group(0, cols, bank(n % 4, CW, cols.stop - cols.start))
                        last.then_inc(h_proj.sem, 1)
                        n += 1
                    pe.wait_ge(h_evac.sem, h_evac.done(i, HG_GROUPS))
                    for u, (hh, half) in enumerate(UNITS):
                        cols = X_PARTS[half]
                        if u:
                            pe.wait_ge(g_evac.sem, g_evac.done(i, u))
                            pe.wait_ge(advanced.sem, advanced.done(i, 4 * u))
                            pe.wait_ge(placed.sem, placed.done(i, 12 * u))
                        if half == 0:
                            pe.wait_ge(meta_k.sem, meta_k.done(i, 2 * hh + 2))
                            nc.tensor.transpose(bank(7, P, META), meta_decay[:, META:], ident[:])\
                                .then_inc(meta_turned.sem, 1)
                            pe.wait_ge(meta_nat.sem, meta_nat.done(i, hh + 1))
                            nc.tensor.matmul(bank(6, P), kd_nat[0:META, 0:P], hv[0:META, TT, hh * P:(hh + 1) * P],
                                             start=True, stop=True).then_inc(meta_grown.sem, 1)
                        pe.wait_ge(tree.sem, tree.done(i, 8 * u + 8))
                        for c in range(UNIT):
                            last = nc.tensor.transpose(bank(7)[:, c * P:(c + 1) * P],
                                                       kd[128][:, c * P:(c + 1) * P], ident[:])
                        last.then_inc(k_turned.sem, 1)
                        for c in range(UNIT):
                            cc = slice(half * HALF + c * P, half * HALF + (c + 1) * P)
                            nc.tensor.matmul(bank(0)[:, c * P:(c + 1) * P], hk[:, hh, cc], hq[:, hh, cc],
                                             start=True, stop=True)
                        for n_, h in enumerate(LEVELS):
                            for c in range(UNIT):
                                kk = hk[:, hh, half * HALF + c * P:half * HALF + (c + 1) * P] if h == 1 else \
                                    kd[h][:, c * P:(c + 1) * P]
                                at_ = (n_ % 2) * 256 + c * (P // 2)
                                last = nc.tensor.matmul(bank(1 + n_ // 2)[:, at_:at_ + P // 2], kk,
                                                        right(qd[h][:, c * P:(c + 1) * P], h), start=True, stop=True)
                        last.then_inc(scored.sem, 1)
                        pe.wait_ge(k_nat.sem, k_nat.done(i, u + 1))
                        pe.wait_ge(started.sem, started.done(i, u + 1))
                        for c in range(UNIT):
                            last = nc.tensor.matmul(bank(6)[:, c * P:(c + 1) * P], kd_nat[:, c * P:(c + 1) * P],
                                                    hv[:, UNIT * half + c, hh * P:(hh + 1) * P],
                                                    start=True, stop=True)
                        last.then_inc(grown.sem, 1)
                        if u == 0:
                            pe.wait_ge(hw.lo.sem, hw.lo.done(i, 4))
                        turned_group(1, hh, cols, bank(7)).then_inc(g_proj.sem, 1)
                        pe.wait_ge(placed.sem, placed.done(i, 12 * u + 12))
                        pe.wait_ge(advanced.sem, advanced.done(i, 4 * u + 3))
                        if u:
                            pe.wait_ge(o_evac.sem, o_evac.done(i, u))
                        for c in range(UNIT):
                            cc = slice(c * P, (c + 1) * P)
                            nc.tensor.matmul(bank(5)[:, cc], hv[:, UNIT * half + c, hh * P:(hh + 1) * P],
                                             scores[:, cc], start=True, stop=False)
                            last = nc.tensor.matmul(bank(5)[:, cc], state[:, c], qd[128][:, cc],
                                                    start=False, stop=True)
                        last.then_inc(o_done.sem, 1)
                    pe.wait_ge(o_evac.sem, o_evac.done(i, 4))
                    pe.wait_ge(advanced.sem, advanced.done(i, 16))
                    for u in range(4):
                        pe.wait_ge(h_square.sem, h_square.done(i, u + 1))
                        if u >= 2:
                            pe.wait_ge(h_root.sem, h_root.done(i, u - 1))
                        nc.tensor.matmul(bank(5 + u % 2), ones[:], (scores, kd_nat)[u % 2][:],
                                         start=True, stop=True).then_inc(h_sum.sem, 1)

        SB_GROUPS = HG_GROUPS
        NP_, NG = len(PIECES), len(GROUPS)
        EVEN, ODD = (NG + 1) // 2, NG // 2
        sw = Weights("sw", 3)
        s_proj, s_evac = signal("s_proj", SB_GROUPS, 1), signal("s_evac", SB_GROUPS)
        z_done = signal("z_done", NP_)
        sig_done = signal("sig_done", NP_)
        scanned = signal("scanned", NP_)
        w_done = signal("w_done", NP_)
        t_done = signal("t_done", NG)
        pt_even, pt_odd = signal("pt_even", EVEN), signal("pt_odd", ODD)
        av_done = signal("av_done", 4)
        av_evac = signal("av_evac", 4, 2)
        s_square, s_sum, s_root = signal("s_square", 4), signal("s_sum", 4), signal("s_root", 4)
        s_inv, s_mixed = signal("s_inv", 4), signal("s_mixed", 4, 4)
        later_set = signal("later_set")
        HALF_ENDS = [max(n for n, pc in enumerate(PIECES) if pc[0] == pr and pc[1] == b)
                     for pr in range(2) for b in (3, 7)]

        with nc.Block() as blk:
            @blk.sync
            def _(sp):
                with sp.Fori(0, 2) as i:
                    for n, at0 in enumerate((SBQ, SBK, SBV)):
                        sw.load(sp, i, n + 1, w_in_v[:, :, bass.ds(at0 + i * CW, CW)])

            @blk.scalar
            def _(act):
                with act.Fori(0, 2) as i:
                    def evac(n, dst):
                        act.wait_ge(s_proj.sem, s_proj.done(i, n + 1))
                        nc.scalar.activation(dst, bank(n % 4, dst.shape[-1], dst.shape[0]), ACT.Copy)\
                            .then_inc(s_evac.sem, 1)

                    sw.high(act, i, 1, s_proj, s_proj.done(i, 0))
                    sw.high(act, i, 2, s_proj, s_proj.done(i, 0))
                    n = 0
                    for t in range(2):
                        for cols in X_PARTS:
                            evac(n, sq[:, t, cols])
                            n += 1
                    sw.high(act, i, 3, s_proj, s_proj.done(i, 4))
                    for t in range(2):
                        for cols in ALL_PARTS:
                            evac(n, sk[:, t, 0:META] if cols.start == SEQ else
                                 sk[:, t, META + cols.start:META + cols.stop])
                            n += 1
                    for t, cols in enumerate(TOKEN_TILES):
                        evac(n, sv[0:cols.stop - cols.start, t, :])
                        n += 1

                    def sigmoids(n):
                        pair, b, par, lo, hi, width, buf = PIECES[n]
                        z = bank(2 * (n % 2), hi - lo)
                        act.wait_ge(z_done.sem, z_done.done(i, n + 1))
                        if n >= 4:
                            act.wait_ge(w_done.sem, w_done.done(i, n - 1 - (lo == 0 and width > 2 * HALF)))
                        nc.scalar.activation(beta[:, buf, lo:hi], z, ACT.Sigmoid, scale=-SB_SCALE)
                        nc.scalar.activation(z, z, ACT.Sigmoid, scale=SB_SCALE).then_inc(sig_done.sem, 1)

                    def out_evac(e):
                        pair, half = e // 2, e % 2
                        act.wait_ge(av_done.sem, av_done.done(i, e + 1))
                        nc.scalar.activation(mixed[:, 2 * i + pair, X_PARTS[half]], bank(6 + half), ACT.Copy)\
                            .then_inc(av_evac.sem, 1)

                    act.wait_ge(s_mixed.sem, s_mixed.free(i, 4))
                    sigmoids(0)
                    sigmoids(1)
                    for n in range(NP_):
                        for g in GROUPS_OF[n]:
                            if g % 2 == 0:
                                w = P * len(GROUPS[g][1])
                                act.wait_ge(t_done.sem, t_done.done(i, g + 1))
                                nc.scalar.activation(probs_t[:, 0, 0:w], bank(4, w), ACT.Copy)\
                                    .then_inc(pt_even.sem, 1)
                        if n + 2 < NP_:
                            sigmoids(n + 2)
                        if n - 1 in HALF_ENDS:
                            out_evac(HALF_ENDS.index(n - 1))
                    out_evac(3)
                    for u in range(4):
                        act.wait_ge(s_sum.sem, s_sum.done(i, u + 1))
                        if u >= 2:
                            act.wait_ge(s_mixed.sem, s_mixed.done(i, u - 1))
                        nc.scalar.activation(later[:, u % 2, 0:HALF], bank(4 + u % 2), ACT.Sqrt,
                                             scale=1.0 / SB_DIM, bias=eps).then_inc(s_root.sem, 1)

            @blk.vector
            def _(dve):
                dve.sem_inc(sw.lo.sem, 1)
                dve.sem_inc(s_mixed.sem, 4)
                nc.vector.memset(later[:], 0.0).then_inc(later_set.sem, 1)
                dve.wait_ge(later_set.sem, 1)
                with dve.Fori(0, 2) as i:
                    sw.low(dve, i, 1)
                    sw.low(dve, i, 2)
                    sw.low(dve, i, 3)

                    def weigh(n):
                        pair, b, par, lo, hi, width, buf = PIECES[n]
                        dve.wait_ge(sig_done.sem, sig_done.done(i, n + 1))
                        if hi == width:
                            src, dst, begin = beta[:, buf, lo + 1:hi], later[:, buf, lo:hi - 1], 1.0
                        else:
                            dve.wait_ge(scanned.sem, scanned.done(i, n))
                            src, dst = beta[:, buf, lo + 1:hi + 1], later[:, buf, lo:hi]
                            begin = later[:, buf, hi:hi + 1]
                        w = src.shape[-1]
                        nc.vector.tensor_tensor_scan(dst[:, ::-1], src[:, ::-1], ones[:, 0:1].to_broadcast([P, w]),
                                                     begin, ALU.mult, ALU.mult).then_inc(scanned.sem, 1)
                        dve.wait_ge(scanned.sem, scanned.done(i, n + 1))
                        if n >= 4:
                            gs = [g for m in range(n - (3 if lo == 0 and width > 2 * HALF else 2) + 1) for g in GROUPS_OF[m]]
                            dve.wait_ge(t_done.sem, t_done.done(i, gs[-1] + 1))
                        nc.vector.tensor_tensor(probs[:, buf, lo:hi], bank(2 * (n % 2), hi - lo),
                                                later[:, buf, lo:hi], ALU.mult).then_inc(w_done.sem, 1)

                    weigh(0)
                    weigh(1)
                    for n in range(NP_):
                        for g in GROUPS_OF[n]:
                            if g % 2 == 1:
                                w = P * len(GROUPS[g][1])
                                dve.wait_ge(t_done.sem, t_done.done(i, g + 1))
                                nc.vector.tensor_copy(probs_t[:, 1, 0:w], bank(5, w)).then_inc(pt_odd.sem, 1)
                        if n + 2 < NP_:
                            weigh(n + 2)
                    for u in range(4):
                        m = mixed[:, 2 * i + u // 2, X_PARTS[u % 2]]
                        dve.wait_ge(av_evac.sem, av_evac.done(i, 4))
                        if u >= 2:
                            dve.wait_ge(s_sum.sem, s_sum.done(i, u - 1))
                        nc.vector.tensor_tensor(beta[:, u % 2, 0:HALF], m, m, ALU.mult).then_inc(s_square.sem, 1)
                    for u in range(4):
                        dve.wait_ge(s_root.sem, s_root.done(i, u + 1))
                        nc.vector.reciprocal(later[:, u % 2, 0:HALF], later[:, u % 2, 0:HALF])\
                            .then_inc(s_inv.sem, 1)
                        dve.wait_ge(s_inv.sem, s_inv.done(i, u + 1))
                        m = mixed[:, 2 * i + u // 2, X_PARTS[u % 2]]
                        nc.vector.scalar_tensor_tensor(m, m, sbg[:, bass.ds(2 * i + u // 2, 1)],
                                                       later[:, u % 2, 0:HALF], ALU.mult, ALU.mult)\
                            .then_inc(s_mixed.sem, 1)

            @blk.tensor
            def _(pe):
                pe.sem_inc(av_evac.sem, 2)
                pe.sem_inc(s_proj.sem, 1)
                with pe.Fori(0, 2) as i:
                    n = 0

                    def free_bank(n):
                        if n >= 4:
                            pe.wait_ge(s_evac.sem, s_evac.done(i, n - 3))

                    for chunk, parts in ((1, X_PARTS), (2, ALL_PARTS)):
                        pe.wait_ge(sw.lo.sem, sw.lo.done(i, chunk))
                        for t in range(2):
                            for cols in parts:
                                free_bank(n)
                                turned_group(chunk - 1, t, cols, bank(n % 4, cols.stop - cols.start))\
                                    .then_inc(s_proj.sem, 1)
                                n += 1
                    pe.wait_ge(sw.lo.sem, sw.lo.done(i, 3))
                    for cols in TOKEN_TILES:
                        free_bank(n)
                        natural_group(0, cols, bank(n % 4, CW, cols.stop - cols.start)).then_inc(s_proj.sem, 1)
                        n += 1
                    pe.wait_ge(s_evac.sem, s_evac.done(i, SB_GROUPS))

                    def score(n):
                        pair, b, par, lo, hi, width, buf = PIECES[n]
                        rows = slice(64 * par, 64 * par + 64)
                        for a in range(lo, hi, HALF):
                            z = min(a + HALF, hi)
                            c, e = max(a, width - P), min(z, width)
                            at_ = 2 * (n % 2) * HALF + a - lo
                            last = nc.tensor.matmul(ps[:, at_:at_ + z - a], sq[rows, pair, b * P:(b + 1) * P],
                                                    sk[rows, pair, a:z], start=True, stop=c >= e)
                            if c < e:
                                last = nc.tensor.matmul(ps[:, at_ + c - a:at_ + e - a], ident_bf[:],
                                                        hidden_bf[:, c - (width - P):e - (width - P)],
                                                        start=False, stop=True)
                        last.then_inc(z_done.sem, 1)

                    def turn(g):
                        n, tiles, _, _ = GROUPS[g]
                        buf = PIECES[n][6]
                        for j, (col, rows, _) in enumerate(tiles):
                            last = nc.tensor.transpose(bank(4 + g % 2)[:, j * P:(j + 1) * P],
                                                       probs[:, buf, col:col + P], ident[:])
                        last.then_inc(t_done.sem, 1)

                    def values(g):
                        n, tiles, begin, end = GROUPS[g]
                        pair, b, par = PIECES[n][:3]
                        copied = pt_even if g % 2 == 0 else pt_odd
                        pe.wait_ge(copied.sem, copied.done(i, g // 2 + 1))
                        if begin and par == 0 and b % 4 == 0:
                            pe.wait_ge(av_evac.sem, av_evac.free(i, 2 * pair + b // 4 + 1))
                        dst = ps[64 * par:64 * par + 64, (6 + b // 4) * HALF + (b % 4) * P:][:, 0:P]
                        for j, (col, rows, t) in enumerate(tiles):
                            head = 2 * pair + par
                            last = nc.tensor.matmul(dst, sv[0:rows, t, head * SB_DIM:(head + 1) * SB_DIM],
                                                    probs_t[0:rows, g % 2, j * P:(j + 1) * P],
                                                    start=begin and j == 0, stop=end and j == len(tiles) - 1)
                        if end and par == 1 and b % 4 == 3:
                            last.then_inc(av_done.sem, 1)

                    score(0)
                    score(1)
                    for n in range(NP_):
                        pe.wait_ge(w_done.sem, w_done.done(i, n + 1))
                        if n + 2 < NP_:
                            score(n + 2)
                        for g in GROUPS_OF[n]:
                            turn(g)
                            if g:
                                values(g - 1)
                    values(NG - 1)
                    for u in range(4):
                        pe.wait_ge(s_square.sem, s_square.done(i, u + 1))
                        if u >= 2:
                            pe.wait_ge(s_root.sem, s_root.done(i, u - 1))
                        nc.tensor.matmul(bank(4 + u % 2), ones_pair[:], beta[:, u % 2, 0:HALF],
                                         start=True, stop=True).then_inc(s_sum.sem, 1)

        m_hi, m_lo = signal("m_hi"), signal("m_lo")
        x_back, gain2, gain3 = signal("x_back"), signal("gain2"), signal("gain3")
        ow = Weights("ow", 2)
        o_proj, o_add = signal("o_proj", 2 * TT, 2 * TT), signal("o_add", 2 * TT, TT)
        n2 = Norm("n2", lambda r, s, rows: h_res[:, bass.ds(2 * r + s, 1), :].rearrange("p a n -> p (a n)"),
                  h_norm, h_sq, False)
        came = {c: signal(f"w{c}_came", 16) for c in "gud"}
        hi_ = {c: signal(f"w{c}_hi", 1) for c in "gud"}
        lo_ = {c: signal(f"w{c}_lo", 1) for c in "gud"}
        gu_done = signal("gu_done", 4)
        sig_ = signal("gate_sigmoid", 4)
        gated = signal("gated", 4)
        hidden = signal("hidden", 4)
        f_high, f_low = signal("f_high", 4), signal("f_low", 4)
        dn_done, dn_add = signal("dn_done", 2 * TT), signal("dn_add", 2 * TT)
        e_sum, e_root, e_inv = signal("e_sum", 2), signal("e_root", 2), signal("e_inv", 2)
        e_norm = signal("e_norm", 2, 2)
        stored = [signal("stored0", 16, 16), signal("stored1", 16, 16)]
        w_dst = {"g": (w_hi[:, 0], w_lo[:, 0]), "u": (w_hi[:, 1], w_lo[:, 1]), "d": (d_hi[:], d_lo[:])}

        with nc.Block() as blk:
            @blk.sync
            def _(sp):
                with sp.Fori(0, 2) as r:
                    for s in range(2):
                        ow.load(sp, r, s + 1, w_out_v[:, :, bass.ts(2 * r + s, CW)])

                def load(c, j, before):
                    sp.wait_ge(lo_[before[0]].sem, before[1])
                    if c == "d":
                        sp.dma_start(w_raw[:].rearrange("p (f n) -> p f n", f=2),
                                     w_down_v[:, bass.ds(2 * j, 2), :]).then_inc(came[c].sem, 16)
                    else:
                        src = w_gate_v if c == "g" else w_up_v
                        sp.dma_start(w_raw[:].rearrange("p (k n) -> p k n", k=KT),
                                     src[:, :, bass.ts(j, CW)]).then_inc(came[c].sem, 16)

                sp.wait_ge(ow.lo.sem, ow.lo.free(2, 1))
                sp.dma_start(w_raw[:].rearrange("p (k n) -> p k n", k=KT), w_gate_v[:, :, 0:CW])\
                    .then_inc(came["g"].sem, 16)
                load("u", 0, ("g", 1))
                load("g", 1, ("u", 1))
                load("u", 1, ("g", 2))

                def segment(j, more=True):
                    load("d", j - 1, ("u", j + 1))
                    if more:
                        load("g", j + 1, ("d", j))
                        load("u", j + 1, ("g", j + 2))

                with sp.Fori(0, (FG - 3) // 2) as r:
                    segment(2 * r + 1)
                    segment(2 * r + 2)
                segment(FG - 2)
                load("d", FG - 2, ("u", FG))
                load("d", FG - 1, ("d", FG - 1))
                with sp.Fori(0, TT // 2) as r:
                    for s in range(2):
                        sp.wait_ge(e_norm.sem, e_norm.done(r, s + 1))
                        sp.dma_start(out2[bass.ts(2 * r + s, P), :], h_norm[:, s]).then_inc(stored[s].sem, 16)
                for s in range(2):
                    sp.wait_ge(stored[s].sem, stored[s].done(TT // 2, 0))

            @blk.gpsimd
            def _(pool):
                pool.dma_start(gain[:], norm2_g[0:1, :].to_broadcast([P, D])).then_inc(gain2.sem, 16)
                for t in range(TT):
                    if t == 0:
                        pool.wait_ge(m_lo.sem, KT)
                    pool.dma_start(h_res[:, t, :], x2[t * P:(t + 1) * P, :]).then_inc(x_back.sem, 16)
                pool.wait_ge(n2.normed.sem, n2.normed.done(TT // 2, 0))
                pool.dma_start(gain[:], final_g.rearrange("(a n) -> a n", a=1).to_broadcast([P, D]))\
                    .then_inc(gain3.sem, 16)

            @blk.scalar
            def _(act):
                for k in range(KT):
                    nc.scalar.activation(act_hi[:, k, 0:SEQ], mixed[:, k], ACT.Copy).then_inc(m_hi.sem, 1)
                with act.Fori(0, 2) as r:
                    for s in range(2):
                        ow.high(act, r, s + 1, o_proj, o_proj.free(r, TT * (s + 1)))
                n2.on_scalar(act, lambda r, s, rows: act.wait_ge(o_add.sem, o_add.done(2, 0)))

                def split(c, j, first=False):
                    act.wait_ge(came[c].sem, came[c].done(j, 16))
                    if not first:
                        if c == "d":
                            act.wait_ge(dn_done.sem, dn_done.done(j, 0))
                        else:
                            act.wait_ge(gu_done.sem, gu_done.done(j, 0))
                    nc.scalar.activation(w_dst[c][0], w_raw[:], ACT.Copy).then_inc(hi_[c].sem, 1)

                def segment(j, par, down=True, down_first=False, more=True):
                    if down:
                        split("d", j - 1, first=down_first)
                    for n in range(4):
                        ft, th = n // 2, n % 2
                        act.wait_ge(gu_done.sem, gu_done.done(j, n + 1))
                        nc.scalar.activation(silu[:, n % 2], bank(2 * (n % 2)), ACT.Sigmoid).then_inc(sig_.sem, 1)
                        act.wait_ge(hidden.sem, hidden.done(j, n + 1))
                        nc.scalar.activation(f_hi[:, par, ft, X_PARTS[th]], silu[:, n % 2], ACT.Copy)\
                            .then_inc(f_high.sem, 1)
                    if more:
                        split("g", j + 1)
                        split("u", j + 1)

                act.wait_ge(o_proj.sem, o_proj.done(2, 0))
                split("g", 0, first=True)
                split("u", 0, first=True)
                segment(0, 0, down=False)
                segment(1, 1, down_first=True)
                with act.Fori(0, (FG - 3) // 2) as r:
                    segment(2 * r + 2, 0)
                    segment(2 * r + 3, 1)
                segment(FG - 1, 0, more=False)
                split("d", FG - 1)
                with act.Fori(0, TT // 2) as r:
                    for s in range(2):
                        row = h_res[:, bass.ds(2 * r + s, 1), :].rearrange("p a n -> p (a n)")
                        act.wait_ge(dn_add.sem, dn_add.done(FG, 0))
                        nc.scalar.activation(h_sq[:, s], row, ACT.Square, accum_out=ssq[:, s:s + 1])\
                            .then_inc(e_sum.sem, 1)
                        act.wait_ge(e_sum.sem, e_sum.done(r, s + 1))
                        act.wait_ge(e_norm.sem, e_norm.free(r, s + 1))
                        nc.scalar.activation(std[:, s:s + 1], ssq[:, s:s + 1], ACT.Sqrt, scale=1.0 / D, bias=eps)\
                            .then_inc(e_root.sem, 1)

            @blk.vector
            def _(dve):
                dve.sem_inc(ow.lo.sem, 1)
                dve.sem_inc(o_add.sem, TT)
                for k in range(KT):
                    dve.wait_ge(m_hi.sem, k + 1)
                    nc.vector.tensor_tensor(act_lo[:, k, 0:SEQ], mixed[:, k], act_hi[:, k, 0:SEQ].bitcast(F32),
                                            ALU.subtract).then_inc(m_lo.sem, 1)
                ow.low(dve, 0, 1)
                ow.low(dve, 0, 2)

                def add(r, s):
                    for t in range(TT):
                        dve.wait_ge(o_proj.sem, o_proj.done(r, TT * s + t + 1))
                        h = h_res[:, t, bass.ts(2 * r + s, CW)]
                        nc.vector.tensor_tensor(h, h, bank(t, CW), ALU.add).then_inc(o_add.sem, 1)

                dve.wait_ge(x_back.sem, 16 * TT)
                add(0, 0)
                ow.low(dve, 1, 1)
                add(0, 1)
                ow.low(dve, 1, 2)
                add(1, 0)
                add(1, 1)
                dve.wait_ge(gain2.sem, 16)
                dve.wait_ge(o_add.sem, o_add.done(2, 0))
                n2.on_vector(dve)

                def split(c, j):
                    dve.wait_ge(hi_[c].sem, hi_[c].done(j, 1))
                    nc.vector.tensor_tensor(w_dst[c][1], w_raw[:], w_dst[c][0].bitcast(F32), ALU.subtract)\
                        .then_inc(lo_[c].sem, 1)

                def gate(j, par):
                    for n in range(4):
                        ft, th = n // 2, n % 2
                        s_ = silu[:, n % 2]
                        dve.wait_ge(sig_.sem, sig_.done(j, n + 1))
                        nc.vector.tensor_tensor(s_, s_, bank(2 * (n % 2)), ALU.mult).then_inc(gated.sem, 1)
                        dve.wait_ge(gated.sem, gated.done(j, n + 1))
                        nc.vector.tensor_tensor(s_, s_, bank(2 * (n % 2) + 1), ALU.mult).then_inc(hidden.sem, 1)
                        dve.wait_ge(f_high.sem, f_high.done(j, n + 1))
                        nc.vector.tensor_tensor(f_lo[:, par, ft, X_PARTS[th]], s_,
                                                f_hi[:, par, ft, X_PARTS[th]].bitcast(F32), ALU.subtract)\
                            .then_inc(f_low.sem, 1)

                def down(j, more=True, nxt=None):
                    for g in range(2 * TT):
                        if more and g == 2:
                            split("g", nxt)
                        if more and g == 5:
                            split("u", nxt)
                        t, half = g // 2, g % 2
                        dve.wait_ge(dn_done.sem, dn_done.done(j, g + 1))
                        h = h_res[:, t, X_PARTS[half]]
                        nc.vector.tensor_tensor(h, h, bank(4 + g % 4), ALU.add).then_inc(dn_add.sem, 1)

                def segment(j, par, more=True):
                    split("d", j - 1)
                    gate(j, par)
                    down(j - 1, more, j + 1)

                split("g", 0)
                split("u", 0)
                gate(0, 0)
                split("g", 1)
                split("u", 1)
                segment(1, 1)
                with dve.Fori(0, (FG - 3) // 2) as r:
                    segment(2 * r + 2, 0)
                    segment(2 * r + 3, 1)
                segment(FG - 1, 0, more=False)
                split("d", FG - 1)
                down(FG - 1, more=False)
                dve.sem_inc(e_norm.sem, 2)
                for s in range(2):
                    dve.sem_inc(stored[s].sem, 16)
                dve.wait_ge(gain3.sem, 16)
                with dve.Fori(0, TT // 2) as r:
                    for s in range(2):
                        row = h_res[:, bass.ds(2 * r + s, 1), :].rearrange("p a n -> p (a n)")
                        dve.wait_ge(e_root.sem, e_root.done(r, s + 1))
                        nc.vector.reciprocal(rstd[:, s:s + 1], std[:, s:s + 1]).then_inc(e_inv.sem, 1)
                        dve.wait_ge(e_inv.sem, e_inv.done(r, s + 1))
                        dve.wait_ge(stored[s].sem, stored[s].free(r, 16))
                        nc.vector.scalar_tensor_tensor(h_norm[:, s], row, rstd[:, s:s + 1], gain[:],
                                                       ALU.mult, ALU.mult).then_inc(e_norm.sem, 1)

            @blk.tensor
            def _(pe):
                pe.sem_inc(o_proj.sem, 2 * TT)
                pe.wait_ge(m_lo.sem, KT)
                with pe.Fori(0, 2) as r:
                    for s in range(2):
                        pe.wait_ge(ow.lo.sem, ow.lo.done(r, s + 1))
                        for t in range(TT):
                            pe.wait_ge(o_add.sem, o_add.free(r, TT * s + t + 1))
                            natural_group(s, TOKEN_TILES[t], bank(t, CW)).then_inc(o_proj.sem, 1)
                pe.wait_ge(o_add.sem, o_add.done(2, 0))
                n2.on_tensor(pe)
                pe.wait_ge(n2.lo.sem, n2.lo.done(TT // 2, 0))

                def gate_up(j):
                    for n in range(4):
                        ft, th = n // 2, n % 2
                        if n == 0:
                            pe.wait_ge(lo_["g"].sem, lo_["g"].done(j, 1))
                            pe.wait_ge(lo_["u"].sem, lo_["u"].done(j, 1))
                        if not (isinstance(j, int) and j == 0 and n < 2):
                            pe.wait_ge(hidden.sem, hidden.done(j, n - 1))
                        turned_group(0, ft, X_PARTS[th], bank(2 * (n % 2)))
                        turned_group(1, ft, X_PARTS[th], bank(2 * (n % 2) + 1)).then_inc(gu_done.sem, 1)

                def down(j, par):
                    pe.wait_ge(lo_["d"].sem, lo_["d"].done(j, 1))
                    pe.wait_ge(f_low.sem, f_low.done(j, 4))
                    for g in range(2 * TT):
                        t, half = g // 2, g % 2
                        if not (isinstance(j, int) and j == 0 and g < 4):
                            pe.wait_ge(dn_add.sem, dn_add.done(j, g - 3))
                        for f in range(2):
                            w = slice(f * D + half * HALF, f * D + (half + 1) * HALF)
                            a = TOKEN_TILES[t]
                            order = ((f_hi, d_hi), (f_hi, d_lo), (f_lo, d_hi))
                            for m, (fa, dw) in enumerate(order):
                                last = nc.tensor.matmul(bank(4 + g % 4), fa[:, par, f, a], dw[:, w],
                                                        start=f == 0 and m == 0, stop=f == 1 and m == 2)
                        last.then_inc(dn_done.sem, 1)

                gate_up(0)
                gate_up(1)
                down(0, 0)
                with pe.Fori(0, (FG - 3) // 2) as r:
                    gate_up(2 * r + 2)
                    down(2 * r + 1, 1)
                    gate_up(2 * r + 3)
                    down(2 * r + 2, 0)
                gate_up(FG - 1)
                down(FG - 2, 1)
                down(FG - 1, 0)


_INS = ["x", "meta_tokens", "norm1_g", "w_in", "sb_norm_g", "hg_norm_g", "hg_lb_logits", "w_out",
        "norm2_g", "w_gate", "w_up", "w_down", "final_norm_g"]
_OUTS = [((1, SEQ, D), "float32")]


def kernel(**inputs):
    import numpy as _np
    import concourse.bacc as _bacc
    from concourse import mybir as _mybir
    from concourse.bass_utils import run_bass_kernel_spmd as _run

    nc = _bacc.Bacc("TRN2", target_bir_lowering=False, num_devices=1)
    arrays, args = {}, []
    for name in _INS:
        a = _np.ascontiguousarray(inputs[name])
        arrays[f"in_{name}_dram"] = a
        args.append(nc.dram_tensor(f"in_{name}_dram", a.shape, _mybir.dt.from_np(a.dtype), kind="ExternalInput").ap())
    for i, (shape, dtype) in enumerate(_OUTS):
        dt = _mybir.dt.from_np(_np.dtype(dtype))
        args.append(nc.dram_tensor(f"out_{i}_dram", shape, dt, kind="ExternalOutput").ap())
    hybrid_layer(nc, *args)
    r = _run(nc, [arrays], core_ids=[0])
    return r.results[0]["out_0_dram"]
```

```python
import concourse.bass as bass
from concourse import mybir
from contextlib import ExitStack

F32 = mybir.dt.float32
F32R = mybir.dt.float32r
BF16 = mybir.dt.bfloat16
I32 = mybir.dt.int32
ALU = mybir.AluOpType
ACT = mybir.ActivationFunctionType

P = 128
D = 1024
SEQ = 1024
META = 16
L = SEQ + META
KT = D // P
TT = SEQ // P
SB_HEADS, SB_DIM = 8, 64
HG_HEADS, HG_DIM = 4, 128
SB_WIDTH = SB_HEADS * SB_DIM
HG_WIDTH = HG_HEADS * HG_DIM
SBQ, SBK, SBV, HGQ, HGF, HGI, HGG = (512 * n for n in range(7))
D_FF = -(-8 * D // (3 * 256)) * 256
FG = D_FF // 256
EPS = 1e-6
SB_SCALE = SB_DIM ** -0.5
MASKED = -1e30
CW = 256
CHUNK = KT * CW
HALF = 512
UNIT = 4
LEVELS = [1, 2, 4, 8, 16, 32, 64]


class Signal:

    def __init__(self, sem, credit=0):
        self.sem, self.credit = sem, credit

    def done(self, n):
        return n + self.credit

    def free(self, n):
        return n


def key_tiles(lo, hi):
    tiles = [(META + P * j, P, j) for j in range(TT) if lo <= META + P * j < hi]
    return tiles + ([(0, META, TT)] if lo == 0 else [])


PIECES = []
for _unit in range(4 * TT * 2):
    _pair, _blk, _par = _unit // 16, _unit // 2 % 8, _unit % 2
    _w = META + P * (_blk + 1)
    for _lo, _hi in ([(0, _w)] if _w <= 2 * HALF else [(META + HALF, _w), (0, META + HALF)]):
        PIECES.append((_pair, _blk, _par, _lo, _hi, _w, _unit % 2))
PER_PAIR = len(PIECES) // 4
GROUPS = []
for _n, (_pair, _blk, _par, _lo, _hi, _w, _u) in enumerate(PIECES):
    _t = key_tiles(_lo, _hi)
    for _a in range(0, len(_t), 4):
        GROUPS.append((_n, _t[_a:_a + 4], _hi == _w and _a == 0, _lo == 0 and _a + 4 >= len(_t)))
GROUPS_OF = [[g for g, x in enumerate(GROUPS) if x[0] == n] for n in range(len(PIECES))]
HALF_ENDS = [max(n for n, pc in enumerate(PIECES) if pc[0] == e // 2 and pc[1] == 4 * (e % 2) + 3) for e in range(8)]

HEAD_USES = ["a0", "a1", "b0", "b1", "m", "bt0", "bt1", "at", "q0", "q1", "g0", "g1"]
PAIR_USES = HEAD_USES[:10]
USES = [(j, u) for j in range(8) for u in (HEAD_USES if j < 4 else PAIR_USES)]
USE = {ju: n for n, ju in enumerate(USES)}

CHUNKS = []
for _j in range(8):
    CHUNKS.append((("A", _j), 0, USE[_j - 1, "m"] if _j else None))
    if _j < 5:
        CHUNKS.append((("B", _j), 1, USE[_j - 1, "g1"] if _j else None))
    elif _j == 6:
        CHUNKS.append((("B", _j), 1, USE[5, "q1"]))
CHUNKS += [(("O", 0), 0, USE[7, "m"]), (("O", 1), 1, USE[7, "q1"])]
CHUNK_NO = {c[0]: n for n, c in enumerate(CHUNKS)}
CHUNK_NO["O", 2], CHUNK_NO["O", 3] = len(CHUNKS), len(CHUNKS) + 1
FILL = {0: "a0", 1: "a1", 3: "b0", 5: "b1", 6: "m", 7: "bt0", 8: "bt1", 9: "at", 10: "q0", 12: "q1"}
NORM_AT = {}
for _e, _n in enumerate(HALF_ENDS[:7]):
    NORM_AT[_n + (4 if _e % 2 == 0 else 3)] = (_e, "sums")
    NORM_AT[_n + (6 if _e % 2 == 0 else 5)] = (_e, "spread")


def hybrid_layer(nc, x, meta, norm1_g, w_in, sb_g, hg_g, lb_logits, w_out, norm2_g,
                 w_gate, w_up, w_down, final_g, out):
    x2, out2 = x[0], out[0]
    w_in_v = w_in[0].rearrange("(k p) n -> p k n", p=P)
    w_out_v = w_out[0].rearrange("(k p) n -> p k n", p=P)
    w_gate_v = w_gate[0].rearrange("(k p) n -> p k n", p=P)
    w_up_v = w_up[0].rearrange("(k p) n -> p k n", p=P)
    w_down_v = w_down[0].rearrange("(f p) n -> p f n", p=P)

    ctx = ExitStack()
    with ctx:
        def sb(name, shape, dt=F32, stack=ctx):
            return stack.enter_context(nc.sbuf_tensor(name, shape, dt))

        def signal(name, credit=0):
            return Signal(ctx.enter_context(nc.semaphore(name)), credit)

        ident = sb("ident", [P, P])
        ident_bf = sb("ident_bf", [P, P], BF16)
        hidden_bf = sb("hidden_bf", [P, P], BF16)
        ones = sb("ones", [P, P])
        ones_pair = sb("ones_pair", [P, 2])
        level_mask = sb("level_mask", [P, len(LEVELS), P // 2])
        gain = sb("gain", [P, D])
        small = sb("small", [P, 96])
        sbg, hgg = small[:, 0:4], small[:, 4:8]
        logit0, logit1 = small[:, 8:12], small[:, 12:16]
        lower, one_minus = small[:, 16:20], small[:, 20:24]
        lower_x, one_x = small[:, 24:28], small[:, 28:32]
        ssq, std, rstd = small[:, 32:34], small[:, 34:36], small[:, 36:38]
        eps = small[:, 38:39]
        root, inv = small[:, 40:56], small[:, 56:72]
        meta_decay = sb("meta_decay", [P, 2 * META])
        meta_rows = sb("meta_rows", [META, P])
        act_hi = sb("a_hi", [P, KT, L], F32R)
        act_lo = sb("a_lo", [P, KT, L], F32R)
        w_raw = sb("w_raw", [P, CHUNK])
        w_hi = sb("w_hi", [P, 2, CHUNK], F32R)
        w_lo = sb("w_lo", [P, 2, CHUNK], F32R)

        U = UNIT * P
        with ExitStack() as heads:
            mixed = sb("mixed", [P, KT, SEQ], stack=heads)
            bq = sb("bq", [P, 2, SEQ], stack=heads)
            bf = sb("bf", [P, 2, L], stack=heads)
            bv = sb("bv", [P, 2, (TT + 1) * P], stack=heads)
            with ExitStack() as hg:
                bk = sb("bk", [P, 2, L], stack=hg)
                g_even = sb("g_even", [P, SEQ], stack=hg)
                kd = {h: sb(f"kd{h}", [P, U], stack=hg) for h in (8, 16, 32, 64, 128)}
                qd = {h: sb(f"qd{h}", [P, U], stack=hg) for h in (64, 128)}
                spare = mixed[:, 0:4, :].rearrange("p a b -> p (a b)")
                for n, h in enumerate((2, 4)):
                    kd[h] = spare[:, n * U:(n + 1) * U]
                for n, h in enumerate((1, 2, 4, 8, 16, 32)):
                    qd[h] = spare[:, (2 + n) * U:(3 + n) * U]
                masked = spare[:, 0:4 * U]
                fac = {h: sb(f"fac{h}", [P, U // (2 * h), 4], stack=hg) for h in LEVELS[1:]}
                total = sb("total", [P, UNIT], stack=hg)
                scores = sb("scores", [P, U], stack=hg)
                kd_nat = sb("kd_nat", [P, U], stack=hg)
                state = sb("state", [P, UNIT + 1, P], stack=hg)
            with ExitStack() as at:
                beta = sb("beta", [P, 2, L], stack=at)
                later = sb("later", [P, 2, L], stack=at)
                probs = sb("probs", [P, 2, L], stack=at)
                probs_t = sb("probs_t", [P, 2, HALF], stack=at)
                squares = sb("squares", [P, HALF], stack=at)
                spread = sb("spread", [P, HALF], stack=at)
            with ExitStack() as first:
                x_in = sb("x_in", [P, 2, D], stack=first)
                x_norm = sb("x_norm", [P, 2, D], stack=first)
                x_sq = sb("x_sq", [P, 2, D], stack=first)
        gate_buf = (g_even[:], gain[:])
        with ExitStack() as ff:
            with ExitStack() as n2s:
                h_norm = sb("h_norm", [P, 2, D], stack=n2s)
                h_sq = sb("h_sq", [P, 2, D], stack=n2s)
            f_hi = sb("f_hi", [P, 2, 2, SEQ], F32R, stack=ff)
            f_lo = sb("f_lo", [P, 2, 2, SEQ], F32R, stack=ff)
            h_res = sb("h_res", [P, TT, D], stack=ff)
            d_hi = sb("d_hi", [P, CHUNK], F32R, stack=ff)
            d_lo = sb("d_lo", [P, CHUNK], F32R, stack=ff)
            silu = sb("silu", [P, 2, HALF], stack=ff)

        ps = ctx.enter_context(nc.psum_tensor("ps", [P, 8 * HALF], F32))

        def bank(n, w=HALF, rows=P):
            return ps[0:rows, n * HALF:n * HALF + w]

        X_PARTS = [slice(0, HALF), slice(HALF, SEQ)]
        TOKEN_TILES = [slice(t * P, (t + 1) * P) for t in range(TT)]
        META_COLS = slice(SEQ, L)
        MIX_HG = SB_WIDTH // P
        UNITS = [(h, half) for h in range(HG_HEADS) for half in range(2)]

        def turned_group(slot, tile, cols, psum):
            for k in range(KT):
                c = slice(k * CW + tile * P, k * CW + tile * P + P)
                wh, wl, ah, al = w_hi[:, slot, c], w_lo[:, slot, c], act_hi[:, k, cols], act_lo[:, k, cols]
                nc.tensor.matmul(psum, wh, ah, start=k == 0, stop=False)
                nc.tensor.matmul(psum, wh, al, start=False, stop=False)
                last = nc.tensor.matmul(psum, wl, ah, start=False, stop=k == KT - 1)
            return last

        def natural_group(slot, cols, psum, order=range(KT), before_last=None):
            for n, k in enumerate(order):
                if n == KT - 1 and before_last:
                    before_last()
                c = slice(k * CW, (k + 1) * CW)
                wh, wl, ah, al = w_hi[:, slot, c], w_lo[:, slot, c], act_hi[:, k, cols], act_lo[:, k, cols]
                nc.tensor.matmul(psum, ah, wh, start=n == 0, stop=False)
                nc.tensor.matmul(psum, ah, wl, start=False, stop=False)
                last = nc.tensor.matmul(psum, al, wh, start=False, stop=n == KT - 1)
            return last

        consts, gain1, filled = signal("consts"), signal("gain1"), signal("filled")
        eps_set, bounds, fills = signal("eps_set"), signal("bounds"), signal("fills")
        x_came = [signal("x_came0"), signal("x_came1")]
        w_came, w_high, w_low = signal("w_came"), signal("w_high"), signal("w_low")
        p_done, p_evac = signal("p_done"), signal("p_evac")
        g_silu = signal("g_silu")
        gates = signal("gates")
        tree = signal("tree")
        scored = signal("scored")
        placed = signal("placed")
        k_turned, k_nat = signal("k_turned"), signal("k_nat")
        grown = signal("grown")
        advanced = signal("advanced")
        meta_k = signal("meta_k")
        meta_turned, meta_nat, meta_grown = signal("meta_turned"), signal("meta_nat"), signal("meta_grown")
        started = signal("started")
        o_done, o_evac = signal("o_done"), signal("o_evac")
        h_square, h_sum, h_root = signal("h_square"), signal("h_sum"), signal("h_root")
        h_inv, h_wide, h_spread = signal("h_inv"), signal("h_wide"), signal("h_spread")
        h_scaled, h_mixed = signal("h_scaled"), signal("h_mixed")
        z_done, sig_done = signal("z_done"), signal("sig_done")
        scanned, w_done = signal("scanned"), signal("w_done")
        t_done = signal("t_done")
        pt_even, pt_odd = signal("pt_even"), signal("pt_odd")
        av_done, av_evac = signal("av_done"), signal("av_evac")
        s_square, s_sum, s_root = signal("s_square"), signal("s_sum"), signal("s_root")
        s_inv, s_wide, s_spread = signal("s_inv"), signal("s_wide"), signal("s_spread")
        s_mixed = signal("s_mixed")
        m_hi, m_lo = signal("m_hi"), signal("m_lo")
        x_back, gain2, gain3 = signal("x_back"), signal("gain2"), signal("gain3")
        o_proj, o_add = signal("o_proj"), signal("o_add")
        came = {c: signal(f"w{c}_came") for c in "gud"}
        high = {c: signal(f"w{c}_high") for c in "gud"}
        low = {c: signal(f"w{c}_low") for c in "gud"}
        gu_done = signal("gu_done")
        gate_sig = signal("gate_sig")
        gated = signal("gated")
        hidden = signal("hidden")
        f_high, f_low = signal("f_high"), signal("f_low")
        dn_done, dn_add = signal("dn_done"), signal("dn_add")
        e_sum, e_root, e_inv, e_norm = signal("e_sum"), signal("e_root"), signal("e_inv"), signal("e_norm")
        stored = [signal("stored0"), signal("stored1")]

        class Norm:
            def __init__(self, name, src, dst, square):
                self.src, self.dst, self.square = src, dst, square
                self.summed, self.rooted = signal(name + "_summed"), signal(name + "_rooted")
                self.inverted, self.normed = signal(name + "_inverted"), signal(name + "_normed", 2)
                self.turned = signal(name + "_turned", 2)
                self.hi, self.lo = signal(name + "_hi"), signal(name + "_lo", 4)

            def cols(self, t, rows):
                return META_COLS if rows == META else bass.ts(t, P)

            def stats(self, act, t, s, rows=P):
                act.wait_ge(self.normed.sem, self.normed.free(t + 1))
                nc.scalar.activation(self.square[0:rows, s], self.src(t, s, rows), ACT.Square,
                                     accum_out=ssq[0:rows, s:s + 1]).then_inc(self.summed.sem, 1)
                act.wait_ge(self.summed.sem, self.summed.done(t + 1))
                nc.scalar.activation(std[0:rows, s:s + 1], ssq[0:rows, s:s + 1], ACT.Sqrt,
                                     scale=1.0 / D, bias=eps[0:rows]).then_inc(self.rooted.sem, 1)

            def high(self, act, t, s, rows=P):
                act.wait_ge(self.turned.sem, self.turned.done(t + 1))
                for b in range(2):
                    src = bank(2 * s + b).rearrange("p (k t) -> p k t", k=4)[:, :, 0:rows]
                    nc.scalar.activation(act_hi[:, 4 * b:4 * b + 4, self.cols(t, rows)], src, ACT.Copy)\
                        .then_inc(self.hi.sem, 1)

            def scale(self, dve, t, s, rows=P):
                dve.wait_ge(self.rooted.sem, self.rooted.done(t + 1))
                nc.vector.reciprocal(rstd[0:rows, s:s + 1], std[0:rows, s:s + 1]).then_inc(self.inverted.sem, 1)
                dve.wait_ge(self.inverted.sem, self.inverted.done(t + 1))
                dve.wait_ge(self.turned.sem, self.turned.free(t + 1))
                nc.vector.scalar_tensor_tensor(self.dst[0:rows, s], self.src(t, s, rows), rstd[0:rows, s:s + 1],
                                               gain[0:rows], ALU.mult, ALU.mult).then_inc(self.normed.sem, 1)

            def low(self, dve, t, s, rows=P):
                for b in range(2):
                    dve.wait_ge(self.hi.sem, self.hi.done(2 * t + b + 1))
                    src = bank(2 * s + b).rearrange("p (k t) -> p k t", k=4)[:, :, 0:rows]
                    c = self.cols(t, rows)
                    nc.vector.tensor_tensor(act_lo[:, 4 * b:4 * b + 4, c], src,
                                            act_hi[:, 4 * b:4 * b + 4, c].bitcast(F32),
                                            ALU.subtract).then_inc(self.lo.sem, 1)

            def transposes(self, pe, t, s, rows=P):
                pe.wait_ge(self.normed.sem, self.normed.done(t + 1))
                pe.wait_ge(self.lo.sem, self.lo.free(2 * t + 2))
                for k in range(KT):
                    last = nc.tensor.transpose(bank(2 * s + k // 4)[:, (k % 4) * P:(k % 4) * P + rows],
                                               self.dst[0:rows, s, k * P:(k + 1) * P], ident[0:rows, 0:rows])
                last.then_inc(self.turned.sem, 1)

        n1 = Norm("n1", lambda t, s, rows: x_in[0:rows, s], x_norm, x_sq)
        n2 = Norm("n2", lambda t, s, rows: h_res[:, t, :], h_norm, h_sq)

        def load_chunk(sp, name):
            kind, j = name
            n = CHUNK_NO[name]
            if n:
                sp.wait_ge(w_low.sem, w_low.done(n))
            dst = w_raw[:].rearrange("p (k n) -> p k n", k=KT)
            if kind == "O":
                parts = [(dst, w_out_v[:, :, j * CW:(j + 1) * CW])]
            elif kind == "B" and j >= 4:
                parts = [(dst, w_in_v[:, :, SBQ + (j - 4) * P:SBQ + (j - 2) * P])]
            else:
                two = {"A": (HGF, HGI), "B": (HGQ, HGG)}[kind] if j < 4 else (SBK, SBV)
                parts = [(dst[:, :, b * P:(b + 1) * P], w_in_v[:, :, c + j % 4 * P:c + (j % 4 + 1) * P])
                         for b, c in enumerate(two)]
            for d, src in parts:
                sp.dma_start(d, src).then_inc(w_came.sem, 16 if len(parts) == 2 else 32)

        def high_chunk(act, name, free=None):
            n = CHUNK_NO[name]
            act.wait_ge(w_came.sem, w_came.done(32 * (n + 1)))
            if free is None and n < len(CHUNKS) and CHUNKS[n][2] is not None:
                free = (p_done, CHUNKS[n][2] + 1)
            if free:
                act.wait_ge(free[0].sem, free[0].done(free[1]))
            nc.scalar.activation(w_hi[:, slot_of(name)], w_raw[:], ACT.Copy).then_inc(w_high.sem, 1)

        def low_chunk(dve, name):
            n, s = CHUNK_NO[name], slot_of(name)
            dve.wait_ge(w_high.sem, w_high.done(n + 1))
            nc.vector.tensor_tensor(w_lo[:, s], w_raw[:], w_hi[:, s].bitcast(F32), ALU.subtract)\
                .then_inc(w_low.sem, 1)

        def slot_of(name):
            return name[1] % 2 if name[0] == "O" else "AB".index(name[0])

        def bank_of(n):
            return (5, 7)[n % 2] if USES[n][0] < 5 else 7

        def project(pe, j, u):
            n = USE[j, u]
            b, par, kind, half = bank_of(n), j % 2, u.rstrip("01"), u[-1] == "1"
            cols = X_PARTS[half]
            back = 2 if USES[n][0] < 5 else 1
            if n >= back:
                pe.wait_ge(p_evac.sem, p_evac.done(n - back + 1))
                if j == 5 and u == "a0":
                    pe.wait_ge(p_evac.sem, p_evac.done(n))
            if kind == "a" and 0 < j < 5:
                pe.wait_ge(g_silu.sem, g_silu.done(2 * j - 1 + half))
            if kind in "abm":
                pe.wait_ge(w_low.sem, w_low.done(CHUNK_NO["A", j] + 1))
            if kind in "qg":
                pe.wait_ge(w_low.sem, w_low.done(CHUNK_NO["B", j if j < 4 else j - j % 2] + 1))
            if kind == "a":
                last = turned_group(0, 0, cols, bank(b))
            elif kind == "b":
                last = turned_group(0, 1, cols, bank(b))
            elif kind == "q":
                last = turned_group(1, 0 if j < 4 else j % 2, cols, bank(b))
            elif kind == "g":
                last = turned_group(1, 1, cols, bank(b))
            elif kind == "m":
                last = natural_group(0, META_COLS, bank(b, CW, META))
            elif kind == "bt":
                pe.wait_ge(p_evac.sem, p_evac.done(USE[j, "b1"] + 1))
                for c in range(UNIT):
                    a = half * HALF + c * P
                    last = nc.tensor.transpose(bank(b)[:, c * P:(c + 1) * P], bv[:, par, a:a + P], ident[:])
            else:
                pe.wait_ge(p_evac.sem, p_evac.done(USE[j, "m"] + 1))
                last = nc.tensor.transpose(bank(b, META), meta_rows[:], ident[0:META, 0:META])
            last.then_inc(p_done.sem, 1)

        def evacuate(act, j, u):
            n = USE[j, u]
            b, par, kind, half = bank_of(n), j % 2, u.rstrip("01"), u[-1] == "1"
            cols = X_PARTS[half]
            act.wait_ge(p_done.sem, p_done.done(n + 1))
            if kind in ("a", "at"):
                w = META if kind == "at" else HALF
                if j < 4:
                    c = META_COLS if kind == "at" else cols
                    nc.scalar.activation(bf[:, par, c], bank(b, w), ACT.Sigmoid)
                    last = nc.scalar.activation(bk[:, par, c], bank(b, w), ACT.Sigmoid, scale=-1.0)
                else:
                    c = slice(0, META) if kind == "at" else slice(META + cols.start, META + cols.stop)
                    last = nc.scalar.activation(bf[:, par, c], bank(b, w), ACT.Copy)
            elif kind in ("b", "bt"):
                last = nc.scalar.activation(bv[:, par, cols], bank(b), ACT.Copy)
            elif kind == "m":
                nc.scalar.activation(meta_rows[:], bank(b, P, META), ACT.Copy)
                last = nc.scalar.activation(bv[0:META, par, SEQ:], bank(b, CW, META)[:, P:], ACT.Copy)
            elif kind == "q":
                last = nc.scalar.activation(bq[:, par, cols], bank(b), ACT.Copy)
            else:
                if j >= 2 and not half:
                    act.wait_ge(h_mixed.sem, h_mixed.done(2 * (j - 1)))
                if j == 1 and not half:
                    act.wait_ge(n1.normed.sem, n1.normed.done(TT + 1))
                last = nc.scalar.activation(gate_buf[par][:, cols], bank(b), ACT.Sigmoid)
            last.then_inc(p_evac.sem, 1)

        def right(ap, h):
            return ap.rearrange("p (b two j) -> p b two j", two=2, j=h)[:, :, 1, :]

        def unit_scores(pe, n):
            head, half = UNITS[n]
            par = head % 2
            pe.wait_ge(tree.sem, tree.done(8 * n + 8))
            pe.wait_ge(started.sem, started.done(n + 1 if half == 0 else n))
            if n:
                pe.wait_ge(advanced.sem, advanced.done(4 * n))
                pe.wait_ge(o_evac.sem, o_evac.done(n))
                pe.wait_ge(h_root.sem, h_root.done(n))
            if half == 0 and head:
                pe.wait_ge(h_scaled.sem, h_scaled.done(2 * head))
            for c in range(UNIT):
                last = nc.tensor.transpose(bank(6)[:, c * P:(c + 1) * P], kd[128][:, c * P:(c + 1) * P], ident[:])
            last.then_inc(k_turned.sem, 1)
            for c in range(UNIT):
                cc = slice(half * HALF + c * P, half * HALF + (c + 1) * P)
                nc.tensor.matmul(bank(0)[:, c * P:(c + 1) * P], bk[:, par, cc], bq[:, par, cc],
                                 start=True, stop=True)
            for l, h in enumerate(LEVELS):
                for c in range(UNIT):
                    keys = bk[:, par, half * HALF + c * P:half * HALF + (c + 1) * P] if h == 1 else \
                        kd[h][:, c * P:(c + 1) * P]
                    a = (l % 2) * 2 * P + c * (P // 2)
                    last = nc.tensor.matmul(bank(1 + l // 2)[:, a:a + P // 2], keys,
                                            right(qd[h][:, c * P:(c + 1) * P], h), start=True, stop=True)
            last.then_inc(scored.sem, 1)

        def unit_growth(pe, n):
            head, half = UNITS[n]
            pe.wait_ge(k_nat.sem, k_nat.done(n + 1))
            for c in range(UNIT):
                a = (UNIT * half + c) * P
                last = nc.tensor.matmul(bank(6)[:, c * P:(c + 1) * P], kd_nat[:, c * P:(c + 1) * P],
                                        bv[:, head % 2, a:a + P], start=True, stop=True)
            last.then_inc(grown.sem, 1)

        def unit_outputs(pe, n):
            head, half = UNITS[n]
            pe.wait_ge(placed.sem, placed.done(12 * n + 12))
            pe.wait_ge(advanced.sem, advanced.done(4 * n + 3))
            for c in range(UNIT):
                cc, a = slice(c * P, (c + 1) * P), (UNIT * half + c) * P
                nc.tensor.matmul(bank(0)[:, cc], bv[:, head % 2, a:a + P], scores[:, cc], start=True, stop=False)
                last = nc.tensor.matmul(bank(0)[:, cc], state[:, c], qd[128][:, cc], start=False, stop=True)
            last.then_inc(o_done.sem, 1)

        def unit_sums(pe, n):
            pe.wait_ge(h_square.sem, h_square.done(n + 1))
            for c in range(UNIT):
                last = nc.tensor.matmul(bank(4)[:, 2 * P + c:2 * P + c + 1],
                                        (kd_nat, scores)[n % 2][:, c * P:(c + 1) * P], ones[:, 0:1],
                                        start=True, stop=True)
            last.then_inc(h_sum.sem, 1)

        def unit_spread(pe, n):
            pe.wait_ge(h_wide.sem, h_wide.done(n + 1))
            for c in range(UNIT):
                last = nc.tensor.matmul(bank(1 + n % 2)[:, c * P:(c + 1) * P],
                                        (kd_nat, scores)[n % 2][:, c * P:(c + 1) * P], ident[:],
                                        start=True, stop=True)
            last.then_inc(h_spread.sem, 1)

        def meta_transpose(pe, head):
            pe.wait_ge(meta_k.sem, meta_k.done(2 * head + 2))
            if head:
                pe.wait_ge(advanced.sem, advanced.done(8 * head))
            nc.tensor.transpose(bank(6, P, META), meta_decay[:, META:], ident[:]).then_inc(meta_turned.sem, 1)

        def meta_growth(pe, head):
            pe.wait_ge(meta_nat.sem, meta_nat.done(head + 1))
            nc.tensor.matmul(bank(6, P), meta_rows[:], bv[0:META, head % 2, SEQ:],
                             start=True, stop=True).then_inc(meta_grown.sem, 1)

        def recurrence_tensor(pe):
            for h in range(-1, HG_HEADS):
                j = h + 1
                if h >= 0:
                    unit_scores(pe, 2 * h)
                project(pe, j, "a0")
                if h >= 0:
                    unit_growth(pe, 2 * h)
                project(pe, j, "a1")
                if h >= 0:
                    unit_outputs(pe, 2 * h)
                project(pe, j, "b0")
                project(pe, j, "b1")
                if h >= 0:
                    unit_sums(pe, 2 * h)
                for u in ("m", "bt0", "bt1", "at"):
                    project(pe, j, u)
                if h >= 0:
                    unit_scores(pe, 2 * h + 1)
                project(pe, j, "q0")
                if h >= 0:
                    unit_growth(pe, 2 * h + 1)
                project(pe, j, "q1")
                if h >= 0:
                    unit_outputs(pe, 2 * h + 1)
                if j < HG_HEADS:
                    meta_transpose(pe, j)
                    project(pe, j, "g0")
                    meta_growth(pe, j)
                if h >= 0:
                    if j == HG_HEADS:
                        project(pe, j + 1, "a0")
                    unit_sums(pe, 2 * h + 1)
                    unit_spread(pe, 2 * h)
                if j < HG_HEADS:
                    project(pe, j, "g1")
                else:
                    project(pe, j + 1, "a1")
                if h >= 0:
                    unit_spread(pe, 2 * h + 1)

        def recurrence_scalar(act):
            def keys(n):
                act.wait_ge(k_turned.sem, k_turned.done(n + 1))
                if n:
                    act.wait_ge(h_sum.sem, h_sum.done(n))
                    if n % 2 == 0:
                        act.wait_ge(h_spread.sem, h_spread.done(n - 1))
                nc.scalar.activation(kd_nat[:], bank(6), ACT.Copy).then_inc(k_nat.sem, 1)

            def outputs(n):
                head, half = UNITS[n]
                act.wait_ge(o_done.sem, o_done.done(n + 1))
                act.wait_ge(grown.sem, grown.done(n + 1))
                nc.scalar.activation((kd_nat, scores)[n % 2][:], bank(0), ACT.Square).then_inc(h_square.sem, 1)
                nc.scalar.activation(mixed[:, MIX_HG + head, X_PARTS[half]], bank(0), ACT.Copy)\
                    .then_inc(o_evac.sem, 1)

            def roots(n):
                act.wait_ge(h_sum.sem, h_sum.done(n + 1))
                if n >= 2:
                    act.wait_ge(h_inv.sem, h_inv.done(n - 1))
                nc.scalar.activation(root[:, 4 * (n % 2):4 * (n % 2) + 4], bank(4)[:, 2 * P:2 * P + 4], ACT.Sqrt,
                                     scale=1.0 / HG_DIM, bias=eps).then_inc(h_root.sem, 1)

            for h in range(-1, HG_HEADS):
                j = h + 1
                if h >= 0:
                    keys(2 * h)
                    high_chunk(act, ("B", j))
                evacuate(act, j, "a0")
                evacuate(act, j, "a1")
                if h >= 0:
                    outputs(2 * h)
                evacuate(act, j, "b0")
                evacuate(act, j, "b1")
                if h >= 0:
                    roots(2 * h)
                for u in ("m", "bt0", "bt1", "at"):
                    evacuate(act, j, u)
                if h >= 0:
                    keys(2 * h + 1)
                high_chunk(act, ("A", j + 1))
                evacuate(act, j, "q0")
                evacuate(act, j, "q1")
                if h >= 0:
                    outputs(2 * h + 1)
                if j < HG_HEADS:
                    act.wait_ge(meta_turned.sem, meta_turned.done(j + 1))
                    nc.scalar.activation(meta_rows[:], bank(6, P, META), ACT.Copy).then_inc(meta_nat.sem, 1)
                    evacuate(act, j, "g0")
                else:
                    evacuate(act, j + 1, "a0")
                if h >= 0:
                    roots(2 * h + 1)
                if j < HG_HEADS:
                    evacuate(act, j, "g1")
                else:
                    evacuate(act, j + 1, "a1")

        def tree_steps(dve, n):
            head, half = UNITS[n]
            cols = X_PARTS[half]
            q, f, k = bq[:, head % 2, cols], bf[:, head % 2, cols], bk[:, head % 2, cols]

            def stage(ins, m):
                ins.then_inc(tree.sem, 1)
                dve.wait_ge(tree.sem, tree.done(8 * n + m))

            def side(ap, h, right_):
                return ap.rearrange("p (b two j) -> p b two j", two=2, j=h)[:, :, right_, :]

            def next_total(h):
                if h == P // 2:
                    return nc.vector.tensor_tensor(total[:], fac[h][:, :, 1], fac[h][:, :, 2], ALU.mult)
                s4 = fac[h][:].rearrange("p (b l) e -> p b l e", l=2)
                return nc.vector.tensor_tensor(fac[2 * h][:, :, 1:3], s4[:, :, :, 1], s4[:, :, :, 2], ALU.mult)

            if n:
                dve.wait_ge(placed.sem, placed.done(12 * n))
            f4 = f.rearrange("p (b l e) -> p b l e", l=2, e=2)
            nc.vector.tensor_tensor(fac[2][:, :, 1:3], f4[:, :, :, 0], f4[:, :, :, 1], ALU.mult)
            nc.vector.tensor_tensor(side(kd[2], 1, 0), side(k, 1, 0), side(f, 1, 1), ALU.mult)
            nc.vector.tensor_copy(side(kd[2], 1, 1), side(k, 1, 1))
            stage(nc.vector.tensor_tensor(qd[1], q, f, ALU.mult), 1)
            nc.vector.tensor_tensor(side(qd[2], 1, 1), side(qd[1], 1, 1), side(f, 1, 0), ALU.mult)
            nc.vector.tensor_copy(side(qd[2], 1, 0), side(qd[1], 1, 0))
            stage(next_total(2), 2)
            for m, h in enumerate(LEVELS[1:]):
                if h == P // 2 and n:
                    dve.wait_ge(o_done.sem, o_done.done(n))
                b = U // (2 * h)
                keep = fac[h][:, :, 2:4].unsqueeze(3).to_broadcast([P, b, 2, h])
                take = fac[h][:, :, 0:2].unsqueeze(3).to_broadcast([P, b, 2, h])
                v = "p (b l j) -> p b l j"
                nc.vector.tensor_tensor(kd[2 * h][:].rearrange(v, l=2, j=h), kd[h][:].rearrange(v, l=2, j=h),
                                        keep, ALU.mult)
                last = nc.vector.tensor_tensor(qd[2 * h][:].rearrange(v, l=2, j=h),
                                               qd[h][:].rearrange(v, l=2, j=h), take, ALU.mult)
                if h < P // 2:
                    last = next_total(2 * h)
                stage(last, 3 + m)

        def recurrence_vector(dve):
            def place(n):
                head, half = UNITS[n]
                dve.wait_ge(scored.sem, scored.done(n + 1))
                if n:
                    dve.wait_ge(h_sum.sem, h_sum.done(n))
                if half == 0 and n:
                    dve.wait_ge(h_spread.sem, h_spread.done(n))
                nc.vector.tensor_tensor(scores[:].rearrange("p (c t) -> p c t", c=UNIT),
                                        bank(0).rearrange("p (c t) -> p c t", c=UNIT),
                                        ident[:].unsqueeze(1).to_broadcast([P, UNIT, P]), ALU.mult)\
                    .then_inc(placed.sem, 1)
                for b in range(4):
                    levels = min(2, len(LEVELS) - 2 * b)
                    v = "p (l c t) -> p l c t"
                    msk = level_mask[:, 2 * b:2 * b + levels, :].unsqueeze(2)\
                        .to_broadcast([P, levels, UNIT, P // 2])
                    nc.vector.tensor_tensor(
                        masked[:, b * HALF:b * HALF + levels * 2 * P].rearrange(v, l=levels, c=UNIT),
                        bank(1 + b, levels * 2 * P).rearrange(v, l=levels, c=UNIT), msk, ALU.mult)\
                        .then_inc(placed.sem, 1)
                for m, h in enumerate(LEVELS):
                    dst = right(scores[:], h)
                    src = masked[:, m * 2 * P:(m + 1) * 2 * P].rearrange("p (a j) -> p a j", j=h)
                    dve.wait_ge(placed.sem, placed.done(12 * n + 5 + m))
                    nc.vector.tensor_tensor(dst, dst, src, ALU.add).then_inc(placed.sem, 1)
                if half:
                    dve.wait_ge(o_done.sem, o_done.done(n))
                    nc.vector.tensor_copy(state[:, 0], state[:, UNIT]).then_inc(started.sem, 1)
                dve.wait_ge(grown.sem, grown.done(n + 1))
                for c in range(UNIT):
                    if c == 0:
                        dve.wait_ge(started.sem, started.done(n + 1))
                    else:
                        dve.wait_ge(advanced.sem, advanced.done(4 * n + c))
                    nc.vector.scalar_tensor_tensor(state[:, c + 1], state[:, c], total[:, c:c + 1],
                                                   bank(6)[:, c * P:(c + 1) * P], ALU.mult, ALU.add)\
                        .then_inc(advanced.sem, 1)
                dve.wait_ge(advanced.sem, advanced.done(4 * n + 4))

            def invert(n):
                dve.wait_ge(h_root.sem, h_root.done(n + 1))
                c = slice(4 * (n % 2), 4 * (n % 2) + 4)
                nc.vector.reciprocal(inv[:, c], root[:, c]).then_inc(h_inv.sem, 1)

            def widen(n):
                dve.wait_ge(h_inv.sem, h_inv.done(n + 1))
                dve.wait_ge(h_sum.sem, h_sum.done(n + 1))
                dve.wait_ge(grown.sem, grown.done(n + 1 + (1 - n % 2)))
                c = slice(4 * (n % 2), 4 * (n % 2) + 4)
                nc.vector.tensor_copy((kd_nat, scores)[n % 2][:].rearrange("p (c t) -> p c t", c=UNIT),
                                      inv[:, c].unsqueeze(2).to_broadcast([P, UNIT, P])).then_inc(h_wide.sem, 1)

            def finish(n):
                head, half = UNITS[n]
                m = mixed[:, MIX_HG + head, X_PARTS[half]]
                dve.wait_ge(h_spread.sem, h_spread.done(n + 1))
                nc.vector.scalar_tensor_tensor(m, m, hgg[:, head:head + 1], bank(1 + n % 2), ALU.mult, ALU.mult)\
                    .then_inc(h_scaled.sem, 1)
                dve.wait_ge(h_scaled.sem, h_scaled.done(n + 1))
                nc.vector.tensor_tensor(m, m, gate_buf[head % 2][:, X_PARTS[half]], ALU.mult)\
                    .then_inc(h_mixed.sem, 1)

            def prepare(j):
                par = j % 2
                dve.wait_ge(p_evac.sem, p_evac.done(USE[j, "at"] + 1))
                nc.vector.tensor_scalar(bf[:, par], bf[:, par], one_minus[:, j:j + 1], lower[:, j:j + 1],
                                        ALU.mult, ALU.add)
                nc.vector.tensor_scalar(bk[:, par], bk[:, par], one_minus[:, j:j + 1], None, ALU.mult)\
                    .then_inc(gates.sem, 1)
                dve.wait_ge(gates.sem, gates.done(j + 1))
                if j:
                    dve.wait_ge(meta_turned.sem, meta_turned.done(j))
                nc.vector.memset(meta_decay[:, META - 1:META], 1.0)
                nc.vector.tensor_tensor_scan(meta_decay[:, 0:META - 1][:, ::-1], bf[:, par, SEQ + 1:L][:, ::-1],
                                             ones[:, 0:META - 1], 1.0, ALU.mult, ALU.mult).then_inc(meta_k.sem, 1)
                dve.wait_ge(meta_k.sem, meta_k.done(2 * j + 1))
                nc.vector.tensor_tensor(meta_decay[:, META:], bk[:, par, SEQ:L], meta_decay[:, 0:META],
                                        ALU.mult).then_inc(meta_k.sem, 1)
                dve.wait_ge(p_evac.sem, p_evac.done(USE[j, "q1"] + 1))
                tree_steps(dve, 2 * j)

            dve.wait_ge(fills.sem, 1)
            for h in range(-1, HG_HEADS):
                j = h + 1
                if h >= 0:
                    low_chunk(dve, ("B", j))
                    place(2 * h)
                    tree_steps(dve, 2 * h + 1)
                    invert(2 * h)
                low_chunk(dve, ("A", j + 1))
                if h >= 0:
                    place(2 * h + 1)
                    widen(2 * h)
                if j < HG_HEADS:
                    prepare(j)
                    dve.wait_ge(meta_grown.sem, meta_grown.done(j + 1))
                    if j:
                        dve.wait_ge(o_done.sem, o_done.done(2 * j))
                    nc.vector.tensor_copy(state[:, 0], bank(6, P)).then_inc(started.sem, 1)
                if h >= 0:
                    invert(2 * h + 1)
                    widen(2 * h + 1)
                    finish(2 * h)
                for half in range(2):
                    if j < HG_HEADS:
                        n = USE[j, f"g{half}"]
                        g = gate_buf[j % 2][:, X_PARTS[half]]
                        dve.wait_ge(p_evac.sem, p_evac.done(n + 1))
                        nc.vector.tensor_tensor(g, g, bank(bank_of(n)), ALU.mult).then_inc(g_silu.sem, 1)
                if h >= 0:
                    if h == HG_HEADS - 1:
                        dve.wait_ge(g_silu.sem, g_silu.done(2 * HG_HEADS))
                    finish(2 * h + 1)

        NP, NG = len(PIECES), len(GROUPS)

        def fill_of(n):
            pair, m = n // PER_PAIR, n % PER_PAIR
            if pair == 3 or m not in FILL or (pair == 0 and FILL[m] in ("a0", "a1")):
                return None
            return 5 + pair, FILL[m]

        NORM_ORDER = [NORM_AT[n] for n in sorted(NORM_AT)]

        def attention_tensor(pe):
            def score(n):
                pair, b, par, lo, hi, width, buf = PIECES[n]
                rows, kv = slice(64 * par, 64 * par + 64), pair % 2
                if n % PER_PAIR == 0:
                    pe.wait_ge(p_evac.sem, p_evac.done(USE[4 + pair, "q1"] + 1))
                for a in range(lo, hi, HALF):
                    z = min(a + HALF, hi)
                    c, e = max(a, width - P), min(z, width)
                    at_ = 2 * (n % 2) * HALF + a - lo
                    last = nc.tensor.matmul(ps[:, at_:at_ + z - a], bq[rows, kv, b * P:(b + 1) * P],
                                            bf[rows, kv, a:z], start=True, stop=c >= e)
                    if c < e:
                        last = nc.tensor.matmul(ps[:, at_ + c - a:at_ + e - a], ident_bf[:],
                                                hidden_bf[:, c - (width - P):e - (width - P)],
                                                start=False, stop=True)
                last.then_inc(z_done.sem, 1)

            def turn(g):
                n, tiles, _, _ = GROUPS[g]
                for j, (col, _, _) in enumerate(tiles):
                    last = nc.tensor.transpose(bank((4, 6)[g % 2])[:, j * P:(j + 1) * P],
                                               probs[:, PIECES[n][6], col:col + P], ident[:])
                last.then_inc(t_done.sem, 1)

            def values(g):
                n, tiles, begin, end = GROUPS[g]
                pair, b, par = PIECES[n][:3]
                copied = (pt_even, pt_odd)[g % 2]
                pe.wait_ge(copied.sem, copied.done(g // 2 + 1))
                e = 2 * pair + b // 4
                if begin and par == 0 and b % 4 == 0 and e:
                    pe.wait_ge(av_evac.sem, av_evac.done(e))
                dst = ps[64 * par:64 * par + 64, 5 * HALF + (b % 4) * P:5 * HALF + (b % 4 + 1) * P]
                for j, (_, rows, t) in enumerate(tiles):
                    a = t * P + par * SB_DIM
                    last = nc.tensor.matmul(dst, bv[0:rows, pair % 2, a:a + SB_DIM],
                                            probs_t[0:rows, g % 2, j * P:(j + 1) * P],
                                            start=begin and j == 0, stop=end and j == len(tiles) - 1)
                if end and par == 1 and b % 4 == 3:
                    last.then_inc(av_done.sem, 1)

            pe.wait_ge(h_mixed.sem, h_mixed.done(2 * HG_HEADS))
            score(0)
            score(1)
            for n in range(NP):
                pe.wait_ge(w_done.sem, w_done.done(n + 1))
                if n + 2 < NP:
                    score(n + 2)
                for i, g in enumerate(GROUPS_OF[n]):
                    turn(g)
                    if g:
                        values(g - 1)
                    if i == 0 and fill_of(n):
                        bank7_free(pe, n)
                        project(pe, *fill_of(n))
                    if i == 0 and n in NORM_AT:
                        bank7_free(pe, n, True)
                        head_norm_tensor(pe, *NORM_AT[n])
            values(NG - 1)

        def steps_before(n, step):
            return sum(1 for m, (e, st) in NORM_AT.items() if m < n and st == step)

        def bank7_free(pe, n, norm=False):
            if norm:
                done = [USE[f] for m in range(n + 1) if (f := fill_of(m))]
                if done:
                    pe.wait_ge(p_evac.sem, p_evac.done(max(done) + 1))
            a, b = steps_before(n, "sums"), steps_before(n, "spread")
            if a:
                pe.wait_ge(s_root.sem, s_root.done(a))
            if b:
                pe.wait_ge(s_mixed.sem, s_mixed.done(b))

        def head_norm_tensor(pe, e, step):
            if step == "sums":
                pe.wait_ge(s_square.sem, s_square.done(e + 1))
                for c in range(UNIT):
                    last = nc.tensor.matmul(bank(7)[:, 2 * c:2 * c + 2], squares[:, c * P:(c + 1) * P],
                                            ones_pair[:], start=True, stop=True)
                last.then_inc(s_sum.sem, 1)
            else:
                pe.wait_ge(s_wide.sem, s_wide.done(e + 1))
                for c in range(UNIT):
                    last = nc.tensor.matmul(bank(7)[:, c * P:(c + 1) * P], spread[:, c * P:(c + 1) * P], ident[:],
                                            start=True, stop=True)
                last.then_inc(s_spread.sem, 1)

        def head_norm_scalar(act, e, step):
            if step == "sums":
                act.wait_ge(s_sum.sem, s_sum.done(e + 1))
                if e:
                    act.wait_ge(s_inv.sem, s_inv.done(e))
                nc.scalar.activation(root[:, 8:16], bank(7, 8), ACT.Sqrt, scale=1.0 / SB_DIM, bias=eps)\
                    .then_inc(s_root.sem, 1)

        def head_norm_vector(dve, e, step):
            if step == "sums":
                dve.wait_ge(s_root.sem, s_root.done(e + 1))
                if e:
                    dve.wait_ge(s_spread.sem, s_spread.done(e))
                nc.vector.reciprocal(inv[:, 8:16], root[:, 8:16]).then_inc(s_inv.sem, 1)
                dve.wait_ge(s_inv.sem, s_inv.done(e + 1))
                nc.vector.tensor_copy(spread[:].rearrange("p (c t) -> p c t", c=2 * UNIT),
                                      inv[:, 8:16].unsqueeze(2).to_broadcast([P, 2 * UNIT, SB_DIM]))\
                    .then_inc(s_wide.sem, 1)
            else:
                m = mixed[:, e // 2, X_PARTS[e % 2]]
                dve.wait_ge(s_spread.sem, s_spread.done(e + 1))
                dve.wait_ge(av_evac.sem, av_evac.done(e + 1))
                nc.vector.scalar_tensor_tensor(m, m, sbg[:, e // 2:e // 2 + 1], bank(7), ALU.mult, ALU.mult)\
                    .then_inc(s_mixed.sem, 1)

        SPLITS = [(4 + t, half) for t in range(4) for half in range(2)] + \
            [(t, half) for t in range(4) for half in range(2)]
        SPLIT_AT = {3 * PER_PAIR + 2 + n: SPLITS[n] for n in range(15)}

        def split_scalar(act, t, half):
            if t < 4:
                act.wait_ge(s_mixed.sem, s_mixed.done(2 * t + half + 1))
            act.wait_ge(p_done.sem, p_done.done(len(USES)))
            nc.scalar.activation(act_hi[:, t, X_PARTS[half]], mixed[:, t, X_PARTS[half]], ACT.Copy)\
                .then_inc(m_hi.sem, 1)

        def split_vector(dve, t, half):
            dve.wait_ge(m_hi.sem, m_hi.done(SPLITS.index((t, half)) + 1))
            nc.vector.tensor_tensor(act_lo[:, t, X_PARTS[half]], mixed[:, t, X_PARTS[half]],
                                    act_hi[:, t, X_PARTS[half]].bitcast(F32), ALU.subtract).then_inc(m_lo.sem, 1)

        CHUNK_AT = {7: ("A", 6), 13: ("B", 6), PER_PAIR + 7: ("A", 7), 2 * PER_PAIR + 7: ("O", 0),
                    2 * PER_PAIR + 13: ("O", 1)}

        def attention_scalar(act):
            def sigmoids(n):
                pair, b, par, lo, hi, width, buf = PIECES[n]
                z = bank(2 * (n % 2), hi - lo)
                act.wait_ge(z_done.sem, z_done.done(n + 1))
                if n >= 2:
                    act.wait_ge(w_done.sem, w_done.done(n - 1))
                nc.scalar.activation(beta[:, buf, lo:hi], z, ACT.Sigmoid, scale=-SB_SCALE)
                nc.scalar.activation(z, z, ACT.Sigmoid, scale=SB_SCALE).then_inc(sig_done.sem, 1)

            def out_evac(e):
                act.wait_ge(av_done.sem, av_done.done(e + 1))
                if e:
                    act.wait_ge(s_sum.sem, s_sum.done(e))
                nc.scalar.activation(squares[:], bank(5), ACT.Square).then_inc(s_square.sem, 1)
                nc.scalar.activation(mixed[:, e // 2, X_PARTS[e % 2]], bank(5), ACT.Copy).then_inc(av_evac.sem, 1)

            def group(g):
                if g % 2 == 0:
                    w = P * len(GROUPS[g][1])
                    act.wait_ge(t_done.sem, t_done.done(g + 1))
                    nc.scalar.activation(probs_t[:, 0, 0:w], bank(4, w), ACT.Copy).then_inc(pt_even.sem, 1)

            act.wait_ge(h_mixed.sem, h_mixed.done(2 * HG_HEADS))
            sigmoids(0)
            sigmoids(1)
            for n in range(NP):
                busy = fill_of(n) is not None
                group(GROUPS_OF[n][0])
                if n - 1 in HALF_ENDS:
                    out_evac(HALF_ENDS.index(n - 1))
                if busy:
                    if n + 2 < NP:
                        sigmoids(n + 2)
                    evacuate(act, *fill_of(n))
                if n in NORM_AT:
                    head_norm_scalar(act, *NORM_AT[n])
                for g in GROUPS_OF[n][1:]:
                    group(g)
                if not busy and n + 2 < NP:
                    sigmoids(n + 2)
                if n in CHUNK_AT:
                    high_chunk(act, CHUNK_AT[n])
                if n in SPLIT_AT:
                    split_scalar(act, *SPLIT_AT[n])
            out_evac(7)

        def attention_vector(dve):
            def weigh(n):
                pair, b, par, lo, hi, width, buf = PIECES[n]
                dve.wait_ge(sig_done.sem, sig_done.done(n + 1))
                if hi == width:
                    src, dst, begin = beta[:, buf, lo + 1:hi], later[:, buf, lo:hi - 1], 1.0
                else:
                    dve.wait_ge(scanned.sem, scanned.done(n))
                    src, dst = beta[:, buf, lo + 1:hi + 1], later[:, buf, lo:hi]
                    begin = later[:, buf, hi:hi + 1]
                nc.vector.tensor_tensor_scan(dst[:, ::-1], src[:, ::-1],
                                             ones[:, 0:1].to_broadcast([P, src.shape[-1]]),
                                             begin, ALU.mult, ALU.mult).then_inc(scanned.sem, 1)
                dve.wait_ge(scanned.sem, scanned.done(n + 1))
                older = [m for m in range(n) if PIECES[m][6] == buf and PIECES[m][:3] != PIECES[n][:3]]
                if older:
                    dve.wait_ge(t_done.sem, t_done.done(GROUPS_OF[older[-1]][-1] + 1))
                nc.vector.tensor_tensor(probs[:, buf, lo:hi], bank(2 * (n % 2), hi - lo),
                                        later[:, buf, lo:hi], ALU.mult).then_inc(w_done.sem, 1)

            def group(g):
                if g % 2 == 1:
                    w = P * len(GROUPS[g][1])
                    dve.wait_ge(t_done.sem, t_done.done(g + 1))
                    nc.vector.tensor_copy(probs_t[:, 1, 0:w], bank(6, w)).then_inc(pt_odd.sem, 1)

            dve.wait_ge(h_mixed.sem, h_mixed.done(2 * HG_HEADS))
            nc.vector.memset(later[:], 0.0).then_inc(fills.sem, 1)
            dve.wait_ge(fills.sem, 2)
            weigh(0)
            weigh(1)
            for n in range(NP):
                busy = fill_of(n) is not None
                group(GROUPS_OF[n][0])
                if busy and n + 2 < NP:
                    weigh(n + 2)
                for g in GROUPS_OF[n][1:]:
                    group(g)
                if not busy and n + 2 < NP:
                    weigh(n + 2)
                if n in NORM_AT:
                    head_norm_vector(dve, *NORM_AT[n])
                if n in CHUNK_AT:
                    low_chunk(dve, CHUNK_AT[n])
                if n in SPLIT_AT:
                    split_vector(dve, *SPLIT_AT[n])

        w_dst = {"g": (w_hi[:, 0], w_lo[:, 0]), "u": (w_hi[:, 1], w_lo[:, 1]), "d": (d_hi[:], d_lo[:])}

        with nc.Block() as blk:
            @blk.sync
            def _(sp):
                sp.dma_start(x_in[:, 0], x2[0:P, :]).then_inc(x_came[0].sem, 16)
                sp.dma_start(x_in[:, 1], x2[P:2 * P, :]).then_inc(x_came[1].sem, 16)
                load_chunk(sp, ("A", 0))
                with sp.Fori(1, TT // 2) as r:
                    for s in range(2):
                        sp.wait_ge(n1.normed.sem, n1.normed.free(r * 2 + (s + 1)))
                        sp.dma_start(x_in[:, s], x2[bass.ts(2 * r + s, P), :]).then_inc(x_came[s].sem, 16)
                sp.wait_ge(n1.normed.sem, n1.normed.free(TT + 1))
                sp.dma_start(x_in[0:META, 0], meta).then_inc(x_came[0].sem, 16)
                for name, _, _ in CHUNKS[1:]:
                    load_chunk(sp, name)
                load_chunk(sp, ("O", 2))
                load_chunk(sp, ("O", 3))

                def load(c, j, before):
                    sp.wait_ge(before[0].sem, before[0].done(before[1]))
                    if c == "d":
                        sp.dma_start(w_raw[:].rearrange("p (f n) -> p f n", f=2),
                                     w_down_v[:, bass.ds(2 * j, 2), :]).then_inc(came[c].sem, 16)
                    else:
                        src = w_gate_v if c == "g" else w_up_v
                        sp.dma_start(w_raw[:].rearrange("p (k n) -> p k n", k=KT),
                                     src[:, :, bass.ts(j, CW)]).then_inc(came[c].sem, 16)

                load("g", 0, (w_low, CHUNK_NO["O", 3] + 1))
                load("u", 0, (low["g"], 1))
                load("g", 1, (low["u"], 1))
                load("u", 1, (low["g"], 2))

                def segment(j):
                    load("d", j - 1, (low["u"], j + 1))
                    load("g", j + 1, (low["d"], j))
                    load("u", j + 1, (low["g"], j + 2))

                with sp.Fori(0, (FG - 3) // 2) as r:
                    segment(2 * r + 1)
                    segment(2 * r + 2)
                segment(FG - 2)
                load("d", FG - 2, (low["u"], FG))
                load("d", FG - 1, (low["d"], FG - 1))
                for t in range(TT):
                    sp.wait_ge(e_norm.sem, e_norm.done(t + 1))
                    sp.dma_start(out2[t * P:(t + 1) * P, :], h_sq[:, t % 2]).then_inc(stored[t % 2].sem, 16)
                for s in range(2):
                    sp.wait_ge(stored[s].sem, 16 * TT // 2)

            @blk.gpsimd
            def _(pool):
                pool.dma_start(gain[:], norm1_g[0:1, :].to_broadcast([P, D])).then_inc(gain1.sem, 16)
                with nc.allow_non_contiguous_dma(reason="a gain for each partition"):
                    for dst, src in ((sbg, sb_g[0]), (hgg, hg_g[0]), (logit0, lb_logits[0]), (logit1, lb_logits[1])):
                        pool.dma_start(dst, src.rearrange("(t p) -> p t", p=P)).then_inc(consts.sem, 16)
                nc.gpsimd.memset(ident[:], 0.0)
                nc.gpsimd.memset(ones[:], 1.0)
                nc.gpsimd.memset(ones_pair[:], 1.0)
                nc.gpsimd.memset(level_mask[:], 1.0)
                nc.gpsimd.memset(hidden_bf[:], 0.0).then_inc(filled.sem, 1)
                pool.wait_ge(filled.sem, 1)
                nc.gpsimd.affine_select(out=ident[:], in_=ident[:], compare_op=ALU.not_equal, fill=1.0,
                                        base=0, pattern=[[-1, P]], channel_multiplier=1).then_inc(filled.sem, 1)
                nc.gpsimd.affine_select(out=ones_pair[:, 0:1], in_=ones_pair[:, 0:1], compare_op=ALU.is_ge,
                                        fill=0.0, base=63, pattern=[[0, 1]], channel_multiplier=-1)
                nc.gpsimd.affine_select(out=ones_pair[:, 1:2], in_=ones_pair[:, 1:2], compare_op=ALU.is_ge,
                                        fill=0.0, base=-64, pattern=[[0, 1]], channel_multiplier=1)
                nc.gpsimd.affine_select(out=hidden_bf[:], in_=hidden_bf[:], compare_op=ALU.is_gt, fill=MASKED,
                                        base=0, pattern=[[-1, P]], channel_multiplier=1)
                for n, h in enumerate(LEVELS):
                    m = level_mask[:, n, :].rearrange("p (b j) -> p b j", j=h)
                    nc.gpsimd.affine_select(out=m, in_=m, compare_op=ALU.is_ge, fill=0.0, base=0,
                                            pattern=[[-2 * h, P // (2 * h)], [0, h]], channel_multiplier=1)\
                        .then_inc(filled.sem, 1)
                    pool.wait_ge(filled.sem, 3 + 2 * n)
                    nc.gpsimd.affine_select(out=m, in_=m, compare_op=ALU.is_ge, fill=0.0, base=h - 1,
                                            pattern=[[2 * h, P // (2 * h)], [0, h]], channel_multiplier=-1)\
                        .then_inc(filled.sem, 1)
                pool.wait_ge(n1.normed.sem, n1.normed.done(TT + 1))
                pool.wait_ge(n1.turned.sem, n1.turned.done(TT + 1))
                for h in LEVELS[1:]:
                    last = nc.gpsimd.memset(fac[h][:], 1.0)
                last.then_inc(fills.sem, 1)
                pool.wait_ge(h_mixed.sem, h_mixed.done(2 * HG_HEADS))
                pool.dma_start(gain[:], norm2_g[0:1, :].to_broadcast([P, D])).then_inc(gain2.sem, 16)
                pool.wait_ge(av_evac.sem, av_evac.done(8))
                for t in range(TT):
                    pool.dma_start(h_res[:, t, :], x2[t * P:(t + 1) * P, :]).then_inc(x_back.sem, 16)
                pool.wait_ge(n2.normed.sem, n2.normed.done(TT))
                pool.dma_start(gain[:], final_g.rearrange("(a n) -> a n", a=1).to_broadcast([P, D]))\
                    .then_inc(gain3.sem, 16)

            @blk.scalar
            def _(act):
                act.wait_ge(eps_set.sem, 1)

                def arrived(t, s):
                    act.wait_ge(x_came[s].sem, t * 8 + (16 - 8 * s))

                for s in range(2):
                    arrived(s, s)
                    n1.stats(act, s, s)
                high_chunk(act, ("A", 0))
                with act.Fori(0, TT // 2 - 1) as r:
                    for s in range(2):
                        arrived(2 * r + (2 + s), s)
                        n1.stats(act, 2 * r + (2 + s), s)
                    for s in range(2):
                        n1.high(act, 2 * r + s, s)
                arrived(TT, 0)
                n1.stats(act, TT, 0, META)
                for s in range(2):
                    n1.high(act, TT - 2 + s, s)
                n1.high(act, TT, 0, META)
                act.wait_ge(bounds.sem, 2)
                nc.scalar.activation(lower, lower_x, ACT.Sigmoid)
                nc.scalar.activation(one_minus, one_x, ACT.Sigmoid).then_inc(bounds.sem, 1)
                high_chunk(act, ("B", 0))
                recurrence_scalar(act)
                attention_scalar(act)
                head_norm_scalar(act, 7, "sums")
                for t, half in SPLITS[15:]:
                    split_scalar(act, t, half)
                high_chunk(act, ("O", 2), (o_proj, TT))
                high_chunk(act, ("O", 3), (o_proj, 2 * TT))

                def split(c, j, free=None, dst=None):
                    act.wait_ge(came[c].sem, came[c].done(16 * j + 16))
                    if free:
                        act.wait_ge(free[0].sem, free[0].done(free[1]))
                    nc.scalar.activation(dst if dst is not None else w_dst[c][0], w_raw[:], ACT.Copy)\
                        .then_inc(high[c].sem, 1)

                split("g", 0, (o_proj, 3 * TT))
                for t in range(TT + 1):
                    if t < TT:
                        act.wait_ge(o_add.sem, o_add.done(3 * TT + t + 1))
                        if t == 0:
                            act.wait_ge(m_lo.sem, 16)
                        n2.stats(act, t, t % 2)
                    if t:
                        n2.high(act, t - 1, (t - 1) % 2)
                split("u", 0, (o_proj, 4 * TT))

                def groups(j, par):
                    for n in range(4):
                        ft, th = n // 2, n % 2
                        act.wait_ge(gu_done.sem, gu_done.done(4 * j + (n + 1)))
                        nc.scalar.activation(silu[:, n % 2], bank(2 * (n % 2)), ACT.Sigmoid).then_inc(gate_sig.sem, 1)
                        act.wait_ge(hidden.sem, hidden.done(4 * j + (n + 1)))
                        nc.scalar.activation(f_hi[:, par, ft, X_PARTS[th]], silu[:, n % 2], ACT.Copy)\
                            .then_inc(f_high.sem, 1)

                def next_chunks(j):
                    split("g", j, (gu_done, 4 * j))
                    split("u", j, (gu_done, 4 * j))

                def segment(j, par):
                    split("d", j - 1, (dn_done, 16 * j - 16))
                    groups(j, par)
                    next_chunks(j + 1)

                groups(0, 0)
                next_chunks(1)
                split("d", 0)
                groups(1, 1)
                next_chunks(2)
                with act.Fori(0, (FG - 3) // 2) as r:
                    segment(2 * r + 2, 0)
                    segment(2 * r + 3, 1)
                split("d", FG - 2, (dn_done, 16 * (FG - 2)))
                groups(FG - 1, 0)
                split("d", FG - 1, (gu_done, 4 * FG), w_hi[:, 0])
                for t in range(TT):
                    act.wait_ge(dn_add.sem, dn_add.done(16 * (FG - 1) + 2 * t + 2))
                    if t >= 2:
                        act.wait_ge(e_norm.sem, e_norm.done(t - 1))
                    nc.scalar.activation(silu[:].rearrange("p a b -> p (a b)"), h_res[:, t, :], ACT.Square,
                                         accum_out=ssq[:, t % 2:t % 2 + 1]).then_inc(e_sum.sem, 1)
                    act.wait_ge(e_sum.sem, e_sum.done(t + 1))
                    nc.scalar.activation(std[:, t % 2:t % 2 + 1], ssq[:, t % 2:t % 2 + 1], ACT.Sqrt,
                                         scale=1.0 / D, bias=eps).then_inc(e_root.sem, 1)

            @blk.vector
            def _(dve):
                nc.vector.memset(eps, EPS).then_inc(eps_set.sem, 1)
                dve.sem_inc(n1.normed.sem, 2)
                dve.sem_inc(n1.lo.sem, 4)
                dve.sem_inc(n2.normed.sem, 2)
                dve.sem_inc(n2.lo.sem, 4)
                dve.wait_ge(consts.sem, 64)
                nc.vector.tensor_tensor(lower_x, logit0, logit1, ALU.subtract).then_inc(bounds.sem, 1)
                nc.vector.tensor_tensor(one_x, logit1, logit0, ALU.subtract).then_inc(bounds.sem, 1)
                dve.wait_ge(filled.sem, 2)
                nc.vector.tensor_copy(ident_bf[:], ident[:]).then_inc(eps_set.sem, 1)
                dve.wait_ge(gain1.sem, 16)
                for s in range(2):
                    n1.scale(dve, s, s)
                low_chunk(dve, ("A", 0))
                with dve.Fori(0, TT // 2 - 1) as r:
                    for s in range(2):
                        n1.scale(dve, 2 * r + (2 + s), s)
                    for s in range(2):
                        n1.low(dve, 2 * r + s, s)
                n1.scale(dve, TT, 0, META)
                for s in range(2):
                    n1.low(dve, TT - 2 + s, s)
                n1.low(dve, TT, 0, META)
                dve.wait_ge(bounds.sem, 3)
                low_chunk(dve, ("B", 0))
                recurrence_vector(dve)
                attention_vector(dve)
                head_norm_vector(dve, 7, "sums")
                head_norm_vector(dve, 7, "spread")
                for t, half in SPLITS[15:]:
                    split_vector(dve, t, half)

                def add(c, t):
                    dve.wait_ge(o_proj.sem, o_proj.done(TT * c + t + 1))
                    h = h_res[:, t, c * CW:(c + 1) * CW]
                    nc.vector.tensor_tensor(h, h, bank(4 + t % 4, CW), ALU.add).then_inc(o_add.sem, 1)

                def split(c, j, dst=None, src=None):
                    dve.wait_ge(high[c].sem, high[c].done(j + 1))
                    hi_, lo_ = dst or w_dst[c]
                    nc.vector.tensor_tensor(lo_, w_raw[:], hi_.bitcast(F32), ALU.subtract).then_inc(low[c].sem, 1)

                dve.wait_ge(x_back.sem, 16 * TT)
                for c in range(4):
                    for t in range(TT):
                        add(c, t)
                        if c == 1 and t == 2:
                            low_chunk(dve, ("O", 2))
                        if c == 2 and t == 2:
                            low_chunk(dve, ("O", 3))
                        if c == 3:
                            if t == 0:
                                dve.wait_ge(gain2.sem, 16)
                                split("g", 0)
                            n2.scale(dve, t, t % 2)
                            if t:
                                n2.low(dve, t - 1, (t - 1) % 2)
                n2.low(dve, TT - 1, (TT - 1) % 2)

                def gate(j, par):
                    for n in range(4):
                        ft, th = n // 2, n % 2
                        s_ = silu[:, n % 2]
                        dve.wait_ge(gate_sig.sem, gate_sig.done(4 * j + (n + 1)))
                        nc.vector.tensor_tensor(s_, s_, bank(2 * (n % 2)), ALU.mult).then_inc(gated.sem, 1)
                        dve.wait_ge(gated.sem, gated.done(4 * j + (n + 1)))
                        nc.vector.tensor_tensor(s_, s_, bank(2 * (n % 2) + 1), ALU.mult).then_inc(hidden.sem, 1)
                        dve.wait_ge(f_high.sem, f_high.done(4 * j + (n + 1)))
                        nc.vector.tensor_tensor(f_lo[:, par, ft, X_PARTS[th]], s_,
                                                f_hi[:, par, ft, X_PARTS[th]].bitcast(F32), ALU.subtract)\
                            .then_inc(f_low.sem, 1)

                def down_add(j, g):
                    t, half = g // 2, g % 2
                    dve.wait_ge(dn_done.sem, dn_done.done(16 * j + (g + 1)))
                    h = h_res[:, t, X_PARTS[half]]
                    nc.vector.tensor_tensor(h, h, bank(4 + g % 4), ALU.add).then_inc(dn_add.sem, 1)

                def down(j):
                    for g in range(2 * TT):
                        if g == 2:
                            split("g", j + 2)
                        if g == 10:
                            split("u", j + 2)
                        down_add(j, g)

                def segment(j, par):
                    split("d", j - 1)
                    gate(j, par)
                    down(j - 1)

                split("u", 0)
                gate(0, 0)
                split("g", 1)
                split("u", 1)
                segment(1, 1)
                with dve.Fori(0, (FG - 3) // 2) as r:
                    segment(2 * r + 2, 0)
                    segment(2 * r + 3, 1)
                split("d", FG - 2)
                gate(FG - 1, 0)
                for g in range(2 * TT):
                    if g == 4:
                        split("d", FG - 1, (w_hi[:, 0], w_lo[:, 0]))
                    down_add(FG - 2, g)
                dve.wait_ge(gain3.sem, 16)

                def final(t):
                    s = t % 2
                    dve.wait_ge(e_root.sem, e_root.done(t + 1))
                    nc.vector.reciprocal(rstd[:, s:s + 1], std[:, s:s + 1]).then_inc(e_inv.sem, 1)
                    dve.wait_ge(e_inv.sem, e_inv.done(t + 1))
                    if t >= 2:
                        dve.wait_ge(stored[s].sem, 16 * (t // 2))
                    nc.vector.scalar_tensor_tensor(h_sq[:, s], h_res[:, t, :], rstd[:, s:s + 1], gain[:],
                                                   ALU.mult, ALU.mult).then_inc(e_norm.sem, 1)

                for t in range(TT):
                    down_add(FG - 1, 2 * t)
                    down_add(FG - 1, 2 * t + 1)
                    if t:
                        final(t - 1)
                final(TT - 1)

            @blk.tensor
            def _(pe):
                pe.sem_inc(n1.turned.sem, 2)
                pe.sem_inc(n2.turned.sem, 2)
                pe.wait_ge(filled.sem, 2)
                with pe.Fori(0, TT // 2) as r:
                    for s in range(2):
                        n1.transposes(pe, 2 * r + s, s)
                n1.transposes(pe, TT, 0, META)
                pe.wait_ge(n1.lo.sem, n1.lo.done(2 * TT + 2))
                recurrence_tensor(pe)
                attention_tensor(pe)

                order = [4, 5, 6, 7, 0, 1, 2, 3]

                def out_group(c, t):
                    n = TT * c + t
                    if c == 0 and t == 4:
                        pe.wait_ge(m_lo.sem, 16)
                    if t == 0:
                        pe.wait_ge(w_low.sem, w_low.done(CHUNK_NO["O", c] + 1))
                    if n >= 4:
                        pe.wait_ge(o_add.sem, o_add.done(n - 3))
                    natural_group(c % 2, TOKEN_TILES[t], bank(4 + t % 4, CW), order).then_inc(o_proj.sem, 1)

                pe.wait_ge(pt_even.sem, (NG + 1) // 2)
                pe.wait_ge(m_lo.sem, 15)
                pe.wait_ge(av_evac.sem, 8)
                for c in range(4):
                    for t in range(TT):
                        if c == 0 and t == 1:
                            head_norm_tensor(pe, 7, "sums")
                        if c == 0 and t == 3:
                            pe.wait_ge(s_mixed.sem, 8)
                        out_group(c, t)
                        if c == 0 and t == 1:
                            head_norm_tensor(pe, 7, "spread")
                        if c == 3 and t:
                            n2.transposes(pe, t - 1, (t - 1) % 2)
                n2.transposes(pe, TT - 1, (TT - 1) % 2)
                pe.wait_ge(n2.lo.sem, n2.lo.done(2 * TT))

                def gate_up(j):
                    for n in range(4):
                        ft, th = n // 2, n % 2
                        if n == 0:
                            pe.wait_ge(low["g"].sem, low["g"].done(j + 1))
                            pe.wait_ge(low["u"].sem, low["u"].done(j + 1))
                        if not (isinstance(j, int) and j == 0 and n < 2):
                            pe.wait_ge(hidden.sem, hidden.done(4 * j + (n - 1)))
                        turned_group(0, ft, X_PARTS[th], bank(2 * (n % 2)))
                        turned_group(1, ft, X_PARTS[th], bank(2 * (n % 2) + 1)).then_inc(gu_done.sem, 1)

                def down(j, par, weights=(d_hi, d_lo)):
                    dh, dl = weights
                    pe.wait_ge(low["d"].sem, low["d"].done(j + 1))
                    pe.wait_ge(f_low.sem, f_low.done(4 * j + 4))
                    for g in range(2 * TT):
                        t, half = g // 2, g % 2
                        if not (isinstance(j, int) and j == 0 and g < 4):
                            pe.wait_ge(dn_add.sem, dn_add.done(16 * j + (g - 3)))
                        for f in range(2):
                            w = slice(f * D + half * HALF, f * D + (half + 1) * HALF)
                            a = TOKEN_TILES[t]
                            for m, (fa, dw) in enumerate(((f_hi, dh), (f_hi, dl), (f_lo, dh))):
                                last = nc.tensor.matmul(bank(4 + g % 4), fa[:, par, f, a], dw[:, w],
                                                        start=f == 0 and m == 0, stop=f == 1 and m == 2)
                        last.then_inc(dn_done.sem, 1)

                gate_up(0)
                gate_up(1)
                down(0, 0)
                with pe.Fori(0, (FG - 3) // 2) as r:
                    gate_up(2 * r + 2)
                    down(2 * r + 1, 1)
                    gate_up(2 * r + 3)
                    down(2 * r + 2, 0)
                gate_up(FG - 1)
                down(FG - 2, 1)
                down(FG - 1, 0, (w_hi[:, 0], w_lo[:, 0]))


_INS = ["x", "meta_tokens", "norm1_g", "w_in", "sb_norm_g", "hg_norm_g", "hg_lb_logits", "w_out",
        "norm2_g", "w_gate", "w_up", "w_down", "final_norm_g"]
_OUTS = [((1, SEQ, D), "float32")]


def kernel(**inputs):
    import numpy as _np
    import concourse.bacc as _bacc
    from concourse import mybir as _mybir
    from concourse.bass_utils import run_bass_kernel_spmd as _run

    nc = _bacc.Bacc("TRN2", target_bir_lowering=False, num_devices=1)
    arrays, args = {}, []
    for name in _INS:
        a = _np.ascontiguousarray(inputs[name])
        arrays[f"in_{name}_dram"] = a
        args.append(nc.dram_tensor(f"in_{name}_dram", a.shape, _mybir.dt.from_np(a.dtype), kind="ExternalInput").ap())
    for i, (shape, dtype) in enumerate(_OUTS):
        dt = _mybir.dt.from_np(_np.dtype(dtype))
        args.append(nc.dram_tensor(f"out_{i}_dram", shape, dt, kind="ExternalOutput").ap())
    hybrid_layer(nc, *args)
    r = _run(nc, [arrays], core_ids=[0])
    return r.results[0]["out_0_dram"]
```

```python
import concourse.bass as bass
from concourse import mybir
from contextlib import ExitStack

F32 = mybir.dt.float32
F32R = mybir.dt.float32r
BF16 = mybir.dt.bfloat16
I32 = mybir.dt.int32
ALU = mybir.AluOpType
ACT = mybir.ActivationFunctionType

P = 128
D = 1024
SEQ = 1024
META = 16
L = SEQ + META
KT = D // P
TT = SEQ // P
SB_HEADS, SB_DIM = 8, 64
HG_HEADS, HG_DIM = 4, 128
SB_WIDTH = SB_HEADS * SB_DIM
HG_WIDTH = HG_HEADS * HG_DIM
SBQ, SBK, SBV, HGQ, HGF, HGI, HGG = (512 * n for n in range(7))
D_FF = -(-8 * D // (3 * 256)) * 256
FG = D_FF // 256
EPS = 1e-6
SB_SCALE = SB_DIM ** -0.5
MASKED = -1e30
CW = 256
CHUNK = KT * CW
HALF = 512
UNIT = 4
LEVELS = [1, 2, 4, 8, 16, 32, 64]


class Signal:

    def __init__(self, sem, credit=0):
        self.sem, self.credit = sem, credit

    def done(self, n):
        return n + self.credit

    def free(self, n):
        return n


def key_tiles(lo, hi):
    tiles = [(META + P * j, P, j) for j in range(TT) if lo <= META + P * j < hi]
    return tiles + ([(0, META, TT)] if lo == 0 else [])


PIECES = []
for _unit in range(4 * TT * 2):
    _pair, _blk, _par = _unit // 16, _unit // 2 % 8, _unit % 2
    _w = META + P * (_blk + 1)
    for _lo, _hi in ([(0, _w)] if _w <= 2 * HALF else [(META + HALF, _w), (0, META + HALF)]):
        PIECES.append((_pair, _blk, _par, _lo, _hi, _w, _unit % 2))
PER_PAIR = len(PIECES) // 4
GROUPS = []
for _n, (_pair, _blk, _par, _lo, _hi, _w, _u) in enumerate(PIECES):
    _t = key_tiles(_lo, _hi)
    for _a in range(0, len(_t), 4):
        GROUPS.append((_n, _t[_a:_a + 4], _hi == _w and _a == 0, _lo == 0 and _a + 4 >= len(_t)))
GROUPS_OF = [[g for g, x in enumerate(GROUPS) if x[0] == n] for n in range(len(PIECES))]
HALF_ENDS = [max(n for n, pc in enumerate(PIECES) if pc[0] == e // 2 and pc[1] == 4 * (e % 2) + 3) for e in range(8)]

HEAD_USES = ["a0", "a1", "a2", "b0", "b1", "b2", "bt0", "bt1", "bm", "q0", "q1", "g0", "g1"]
PAIR_USES = HEAD_USES[:11]
THIRDS = [slice(0, 352), slice(352, 704), slice(704, L)]
FIRST_USES = ["a0", "b0", "a1", "b1", "a2", "b2"] + HEAD_USES[6:]
USES = [(j, u) for j in range(8) for u in (FIRST_USES if j == 0 else HEAD_USES if j < 4 else PAIR_USES)]
USE = {ju: n for n, ju in enumerate(USES)}

CHUNKS = []
for _j in range(8):
    CHUNKS.append((("A", _j), 0, USE[_j - 1, "b2"] if _j else None))
    if _j < 5:
        CHUNKS.append((("B", _j), 1, USE[_j - 1, "g1"] if _j else None))
    elif _j == 6:
        CHUNKS.append((("B", _j), 1, USE[5, "q1"]))
CHUNKS += [(("O", 0), 0, USE[7, "b2"]), (("O", 1), 1, USE[7, "q1"])]
CHUNK_NO = {c[0]: n for n, c in enumerate(CHUNKS)}
CHUNK_NO["O", 2], CHUNK_NO["O", 3] = len(CHUNKS), len(CHUNKS) + 1
FILL = {0: "a0", 1: "a1", 3: "a2", 5: "b0", 6: "b1", 7: "b2", 8: "bt0", 9: "bt1", 10: "bm", 12: "q0", 14: "q1"}
NORM_AT = {}
for _e, _n in enumerate(HALF_ENDS[:7]):
    NORM_AT[_n + (4 if _e % 2 == 0 else 3)] = (_e, "sums")
    NORM_AT[_n + (6 if _e % 2 == 0 else 5)] = (_e, "spread")


def hybrid_layer(nc, x, meta, norm1_g, w_in, sb_g, hg_g, lb_logits, w_out, norm2_g,
                 w_gate, w_up, w_down, final_g, out):
    x2, out2 = x[0], out[0]
    w_in_v = w_in[0].rearrange("(k p) n -> p k n", p=P)
    w_out_v = w_out[0].rearrange("(k p) n -> p k n", p=P)
    w_gate_v = w_gate[0].rearrange("(k p) n -> p k n", p=P)
    w_up_v = w_up[0].rearrange("(k p) n -> p k n", p=P)
    w_down_v = w_down[0].rearrange("(f p) n -> p f n", p=P)

    ctx = ExitStack()
    with ctx:
        def sb(name, shape, dt=F32, stack=ctx):
            return stack.enter_context(nc.sbuf_tensor(name, shape, dt))

        def signal(name, credit=0):
            return Signal(ctx.enter_context(nc.semaphore(name)), credit)

        ident = sb("ident", [P, P])
        ident_bf = sb("ident_bf", [P, P], BF16)
        hidden_bf = sb("hidden_bf", [P, P], BF16)
        ones = sb("ones", [P, P])
        ones_pair = sb("ones_pair", [P, 2])
        level_mask = sb("level_mask", [P, len(LEVELS), P // 2])
        gain = sb("gain", [P, D])
        small = sb("small", [P, 96])
        sbg, hgg = small[:, 0:4], small[:, 4:8]
        logit0, logit1 = small[:, 8:12], small[:, 12:16]
        lower, one_minus = small[:, 16:20], small[:, 20:24]
        lower_x, one_x = small[:, 24:28], small[:, 28:32]
        ssq, std, rstd = small[:, 32:34], small[:, 34:36], small[:, 36:38]
        eps = small[:, 38:39]
        root, inv = small[:, 40:56], small[:, 56:72]
        table_load = small[:, 72:73]
        meta_decay = sb("meta_decay", [P, 2 * META])
        meta_rows = sb("meta_rows", [META, P])
        act_hi = sb("a_hi", [P, KT, L], F32R)
        act_lo = sb("a_lo", [P, KT, L], F32R)
        w_raw = sb("w_raw", [P, CHUNK])
        w_hi = sb("w_hi", [P, 2, CHUNK], F32R)
        w_lo = sb("w_lo", [P, 2, CHUNK], F32R)

        U = UNIT * P
        with ExitStack() as heads:
            mixed = sb("mixed", [P, KT, SEQ], stack=heads)
            bq = sb("bq", [P, 2, SEQ], stack=heads)
            bf = sb("bf", [P, 2, L], stack=heads)
            bv = sb("bv", [P, 2, (TT + 1) * P], stack=heads)
            with ExitStack() as hg:
                bk = sb("bk", [P, 2, L], stack=hg)
                with ExitStack() as first:
                    x_in = mixed
                    x_meta = sb("x_meta", [META, D], stack=first)
                    x_norm = sb("x_norm", [P, 2, D], stack=first)
                    x_sq = sb("x_sq", [P, 2, D], stack=first)
                g_even = sb("g_even", [P, SEQ], stack=hg)
                kd = {h: sb(f"kd{h}", [P, U], stack=hg) for h in (8, 16, 32, 64, 128)}
                qd = {h: sb(f"qd{h}", [P, U], stack=hg) for h in (64, 128)}
                spare = mixed[:, 0:4, :].rearrange("p a b -> p (a b)")
                for n, h in enumerate((2, 4)):
                    kd[h] = spare[:, n * U:(n + 1) * U]
                for n, h in enumerate((1, 2, 4, 8, 16, 32)):
                    qd[h] = spare[:, (2 + n) * U:(3 + n) * U]
                masked = spare[:, 0:4 * U]
                fac = {h: sb(f"fac{h}", [P, U // (2 * h), 4], stack=hg) for h in LEVELS[1:]}
                total = sb("total", [P, UNIT], stack=hg)
                scores = sb("scores", [P, U], stack=hg)
                kd_nat = sb("kd_nat", [P, U], stack=hg)
                state = sb("state", [P, UNIT + 1, P], stack=hg)
            with ExitStack() as at:
                beta = sb("beta", [P, 2, L], stack=at)
                later = sb("later", [P, 2, L], stack=at)
                probs = sb("probs", [P, 2, L], stack=at)
                probs_t = sb("probs_t", [P, 3, HALF], stack=at)
                squares = sb("squares", [P, HALF], stack=at)
                spread = sb("spread", [P, HALF], stack=at)
        gate_buf = (g_even[:], gain[:])
        with ExitStack() as ff:
            with ExitStack() as n2s:
                h_norm = sb("h_norm", [P, 2, D], stack=n2s)
                h_sq = sb("h_sq", [P, 2, D], stack=n2s)
            f_hi = sb("f_hi", [P, 2, 2, SEQ], F32R, stack=ff)
            f_lo = sb("f_lo", [P, 2, 2, SEQ], F32R, stack=ff)
            h_res = sb("h_res", [P, TT, D], stack=ff)
            d_hi = sb("d_hi", [P, CHUNK], F32R, stack=ff)
            d_lo = sb("d_lo", [P, CHUNK], F32R, stack=ff)
            silu = sb("silu", [P, 2, HALF], stack=ff)

        ps = ctx.enter_context(nc.psum_tensor("ps", [P, 8 * HALF], F32))

        def bank(n, w=HALF, rows=P):
            return ps[0:rows, n * HALF:n * HALF + w]

        X_PARTS = [slice(0, HALF), slice(HALF, SEQ)]
        TOKEN_TILES = [slice(t * P, (t + 1) * P) for t in range(TT)]
        META_COLS = slice(SEQ, L)
        MIX_HG = SB_WIDTH // P
        UNITS = [(h, half) for h in range(HG_HEADS) for half in range(2)]

        slots = [(w_hi[:, 0], w_lo[:, 0]), (w_hi[:, 1], w_lo[:, 1]), (d_hi[:], d_lo[:])]

        def out_bank(c, t):
            return 4 + t % (2 if c == 3 else 4)

        def ffn_tile(n, first=False):
            if first:
                return (n % 2, n // 2) + ((6, 4), (7, 5), (0, 1), (2, 3))[n]
            return n // 2, n % 2, 2 * (n % 2), 2 * (n % 2) + 1

        def ffn_slot(c, first=False):
            return slots[{"g": 2, "u": 0, "d": 1}[c] if not first else {"g": 0, "u": 1}[c]]

        def turned_group(weights, tile, cols, psum):
            for k in range(KT):
                c = slice(k * CW + tile * P, k * CW + tile * P + P)
                wh, wl, ah, al = weights[0][:, c], weights[1][:, c], act_hi[:, k, cols], act_lo[:, k, cols]
                nc.tensor.matmul(psum, wh, ah, start=k == 0, stop=False)
                nc.tensor.matmul(psum, wh, al, start=False, stop=False)
                last = nc.tensor.matmul(psum, wl, ah, start=False, stop=k == KT - 1)
            return last

        def natural_group(slot, cols, psum, order=range(KT), before_last=None):
            for n, k in enumerate(order):
                if n == KT - 1 and before_last:
                    before_last()
                c = slice(k * CW, (k + 1) * CW)
                wh, wl, ah, al = w_hi[:, slot, c], w_lo[:, slot, c], act_hi[:, k, cols], act_lo[:, k, cols]
                nc.tensor.matmul(psum, ah, wh, start=n == 0, stop=False)
                nc.tensor.matmul(psum, ah, wl, start=False, stop=False)
                last = nc.tensor.matmul(psum, al, wh, start=False, stop=n == KT - 1)
            return last

        consts, gain1, filled = signal("consts"), signal("gain1"), signal("filled")
        eps_set, bounds, fills = signal("eps_set"), signal("bounds"), signal("fills")
        x_came = [signal(f"x_came{t}") for t in range(TT + 1)]
        w_came, w_high, w_low = signal("w_came"), signal("w_high"), signal("w_low")
        p_done, p_evac = signal("p_done"), signal("p_evac")
        g_silu = signal("g_silu")
        gates = signal("gates")
        tree = signal("tree")
        scored = signal("scored")
        placed = signal("placed")
        k_turned, k_nat = signal("k_turned"), signal("k_nat")
        grown = signal("grown")
        advanced = signal("advanced")
        meta_k = signal("meta_k")
        meta_turned, meta_nat, meta_grown = signal("meta_turned"), signal("meta_nat"), signal("meta_grown")
        started = signal("started")
        o_done, o_evac = signal("o_done"), signal("o_evac")
        h_square, h_sum, h_root = signal("h_square"), signal("h_sum"), signal("h_root")
        h_inv, h_wide, h_spread = signal("h_inv"), signal("h_wide"), signal("h_spread")
        h_scaled, h_mixed = signal("h_scaled"), signal("h_mixed")
        z_done = signal("z_done")
        beta_done, sig_done = signal("beta_done"), signal("sig_done")
        scanned, w_done = signal("scanned"), signal("w_done")
        t_done = signal("t_done")
        pt_even, pt_odd = signal("pt_even"), signal("pt_odd")
        av_done, av_evac = signal("av_done"), signal("av_evac")
        s_square, s_sum, s_root = signal("s_square"), signal("s_sum"), signal("s_root")
        s_inv, s_wide, s_spread = signal("s_inv"), signal("s_wide"), signal("s_spread")
        s_mixed = signal("s_mixed")
        m_hi, m_lo = signal("m_hi"), signal("m_lo")
        x_back, gain2, gain3 = signal("x_back"), signal("gain2"), signal("gain3")
        o_proj, o_add = signal("o_proj"), signal("o_add")
        came = {c: signal(f"w{c}_came") for c in "gud"}
        high = {c: signal(f"w{c}_high") for c in "gud"}
        low = {c: signal(f"w{c}_low") for c in "gud"}
        gu_done = signal("gu_done")
        gates_used = signal("gates_used")
        gate_sig = signal("gate_sig")
        gated = signal("gated")
        hidden = signal("hidden")
        f_high, f_low = signal("f_high"), signal("f_low")
        dn_done, dn_add = signal("dn_done"), signal("dn_add")
        e_sum, e_root, e_inv, e_norm = signal("e_sum"), signal("e_root"), signal("e_inv"), signal("e_norm")
        stored = [signal("stored0"), signal("stored1")]

        class Norm:
            def __init__(self, name, src, dst, square):
                self.src, self.dst, self.square = src, dst, square
                self.summed, self.rooted = signal(name + "_summed"), signal(name + "_rooted")
                self.inverted, self.normed = signal(name + "_inverted"), signal(name + "_normed", 2)
                self.turned = signal(name + "_turned", 2)
                self.hi, self.lo = signal(name + "_hi"), signal(name + "_lo", 4)

            def cols(self, t, rows):
                return META_COLS if rows == META else bass.ts(t, P)

            def stats(self, act, t, s, rows=P):
                act.wait_ge(self.normed.sem, self.normed.free(t + 1))
                nc.scalar.activation(self.square[0:rows, s], self.src(t, s, rows), ACT.Square,
                                     accum_out=ssq[0:rows, s:s + 1]).then_inc(self.summed.sem, 1)
                act.wait_ge(self.summed.sem, self.summed.done(t + 1))
                nc.scalar.activation(std[0:rows, s:s + 1], ssq[0:rows, s:s + 1], ACT.Sqrt,
                                     scale=1.0 / D, bias=eps[0:rows]).then_inc(self.rooted.sem, 1)

            def high(self, act, t, s, rows=P):
                act.wait_ge(self.turned.sem, self.turned.done(t + 1))
                for b in range(2):
                    src = bank(2 * s + b).rearrange("p (k t) -> p k t", k=4)[:, :, 0:rows]
                    nc.scalar.activation(act_hi[:, 4 * b:4 * b + 4, self.cols(t, rows)], src, ACT.Copy)\
                        .then_inc(self.hi.sem, 1)

            def scale(self, dve, t, s, rows=P):
                dve.wait_ge(self.rooted.sem, self.rooted.done(t + 1))
                nc.vector.reciprocal(rstd[0:rows, s:s + 1], std[0:rows, s:s + 1]).then_inc(self.inverted.sem, 1)
                dve.wait_ge(self.inverted.sem, self.inverted.done(t + 1))
                dve.wait_ge(self.turned.sem, self.turned.free(t + 1))
                nc.vector.scalar_tensor_tensor(self.dst[0:rows, s], self.src(t, s, rows), rstd[0:rows, s:s + 1],
                                               gain[0:rows], ALU.mult, ALU.mult).then_inc(self.normed.sem, 1)

            def low(self, dve, t, s, rows=P):
                for b in range(2):
                    dve.wait_ge(self.hi.sem, self.hi.done(2 * t + b + 1))
                    src = bank(2 * s + b).rearrange("p (k t) -> p k t", k=4)[:, :, 0:rows]
                    c = self.cols(t, rows)
                    nc.vector.tensor_tensor(act_lo[:, 4 * b:4 * b + 4, c], src,
                                            act_hi[:, 4 * b:4 * b + 4, c].bitcast(F32),
                                            ALU.subtract).then_inc(self.lo.sem, 1)

            def transposes(self, pe, t, s, rows=P):
                pe.wait_ge(self.normed.sem, self.normed.done(t + 1))
                pe.wait_ge(self.lo.sem, self.lo.free(2 * t + 2))
                for k in range(KT):
                    last = nc.tensor.transpose(bank(2 * s + k // 4)[:, (k % 4) * P:(k % 4) * P + rows],
                                               self.dst[0:rows, s, k * P:(k + 1) * P], ident[0:rows, 0:rows])
                last.then_inc(self.turned.sem, 1)

        def rows_of(t):
            return P if t < TT else META

        n1 = Norm("n1", lambda t, s, rows: x_in[:, t, :] if t < TT else x_meta[:], x_norm, x_sq)
        n2 = Norm("n2", lambda t, s, rows: h_res[:, t, :], h_norm, h_sq)

        def load_chunk(sp, name):
            kind, j = name
            n = CHUNK_NO[name]
            if n:
                sp.wait_ge(w_low.sem, w_low.done(n))
            dst = w_raw[:].rearrange("p (k n) -> p k n", k=KT)
            if kind == "O":
                parts = [(dst, w_out_v[:, :, j * CW:(j + 1) * CW])]
            elif kind == "B" and j >= 4:
                parts = [(dst, w_in_v[:, :, SBQ + (j - 4) * P:SBQ + (j - 2) * P])]
            else:
                two = {"A": (HGF, HGI), "B": (HGQ, HGG)}[kind] if j < 4 else (SBK, SBV)
                parts = [(dst[:, :, b * P:(b + 1) * P], w_in_v[:, :, c + j % 4 * P:c + (j % 4 + 1) * P])
                         for b, c in enumerate(two)]
            for d, src in parts:
                sp.dma_start(d, src).then_inc(w_came.sem, 16 if len(parts) == 2 else 32)

        CHUNK_HALVES = [slice(0, CHUNK // 2), slice(CHUNK // 2, CHUNK)]

        def copy_part(name, c):
            return nc.scalar.activation(w_hi[:, slot_of(name), c], w_raw[:, c], ACT.Copy)

        def high_chunk(act, name, free=None, part=None):
            n = CHUNK_NO[name]
            act.wait_ge(w_came.sem, w_came.done(32 * (n + 1)))
            if free is None and n < len(CHUNKS) and CHUNKS[n][2] is not None:
                free = (p_done, CHUNKS[n][2] + 1)
            if free:
                act.wait_ge(free[0].sem, free[0].done(free[1]))
            last = copy_part(name, slice(0, CHUNK) if part is None else CHUNK_HALVES[part])
            if part != 0:
                last.then_inc(w_high.sem, 1)

        def low_chunk(dve, name, part=None):
            n, s = CHUNK_NO[name], slot_of(name)
            c = slice(0, CHUNK) if part is None else CHUNK_HALVES[part]
            dve.wait_ge(w_high.sem, w_high.done(n + 1))
            last = nc.vector.tensor_tensor(w_lo[:, s, c], w_raw[:, c], w_hi[:, s, c].bitcast(F32), ALU.subtract)
            if part != 0:
                last.then_inc(w_low.sem, 1)

        def slot_of(name):
            return name[1] % 2 if name[0] == "O" else "AB".index(name[0])

        def bank_of(n):
            return (5, 7)[n % 2] if USES[n][0] < 5 else 7

        def project(pe, j, u):
            n = USE[j, u]
            b, par, kind = bank_of(n), j % 2, u.rstrip("012")
            part = 0 if kind == "bm" else int(u[-1])
            cols = THIRDS[part] if kind in "ab" else X_PARTS[part]
            w = cols.stop - cols.start
            back = 2 if USES[n][0] < 5 else 1
            if n >= back:
                pe.wait_ge(p_evac.sem, p_evac.done(n - back + 1))
                if j == 5 and u == "a0":
                    pe.wait_ge(p_evac.sem, p_evac.done(n))
            if u in ("a0", "a1") and 0 < j < 5:
                pe.wait_ge(g_silu.sem, g_silu.done(2 * j - 1 + part))
            if kind in "ab":
                pe.wait_ge(w_low.sem, w_low.done(CHUNK_NO["A", j] + 1))
            if kind in "qg":
                pe.wait_ge(w_low.sem, w_low.done(CHUNK_NO["B", j if j < 4 else j - j % 2] + 1))
            if kind == "a":
                last = turned_group(slots[0], 0, cols, bank(b, w))
            elif kind == "b":
                last = turned_group(slots[0], 1, cols, bank(b, w))
            elif kind == "q":
                last = turned_group(slots[1], 0 if j < 4 else j % 2, cols, bank(b))
            elif kind == "g":
                last = turned_group(slots[1], 1, cols, bank(b))
            elif kind == "bt":
                pe.wait_ge(p_evac.sem, p_evac.done(USE[j, "b2"] + 1))
                for c in range(UNIT):
                    a = part * HALF + c * P
                    last = nc.tensor.transpose(bank(b)[:, c * P:(c + 1) * P], bv[:, par, a:a + P], ident[:])
            else:
                last = nc.tensor.transpose(bank(b, P, META), bv[:, par, META_COLS], ident[:])
            last.then_inc(p_done.sem, 1)

        def evacuate(act, j, u):
            n = USE[j, u]
            b, par, kind = bank_of(n), j % 2, u.rstrip("012")
            part = 0 if kind == "bm" else int(u[-1])
            cols = THIRDS[part] if kind in "ab" else X_PARTS[part]
            w = cols.stop - cols.start
            act.wait_ge(p_done.sem, p_done.done(n + 1))
            if kind == "a" and j < 4:
                nc.scalar.activation(bf[:, par, cols], bank(b, w), ACT.Sigmoid)
                last = nc.scalar.activation(bk[:, par, cols], bank(b, w), ACT.Sigmoid, scale=-1.0)
            elif kind == "a":
                own = min(cols.stop, SEQ) - cols.start
                last = nc.scalar.activation(bf[:, par, META + cols.start:META + cols.start + own],
                                            bank(b, own), ACT.Copy)
                if own < w:
                    last = nc.scalar.activation(bf[:, par, 0:META], bank(b, w)[:, own:], ACT.Copy)
            elif kind in ("b", "bt"):
                last = nc.scalar.activation(bv[:, par, cols], bank(b, w), ACT.Copy)
            elif kind == "bm":
                last = nc.scalar.activation(bv[0:META, par, SEQ:], bank(b, P, META), ACT.Copy)
            elif kind == "q":
                last = nc.scalar.activation(bq[:, par, cols], bank(b), ACT.Copy)
            else:
                if j >= 2 and not part:
                    act.wait_ge(h_mixed.sem, h_mixed.done(2 * (j - 1)))
                if j == 1 and not part:
                    act.wait_ge(n1.normed.sem, n1.normed.done(TT + 1))
                last = nc.scalar.activation(gate_buf[par][:, cols], bank(b), ACT.Sigmoid)
            last.then_inc(p_evac.sem, 1)

        def right(ap, h):
            return ap.rearrange("p (b two j) -> p b two j", two=2, j=h)[:, :, 1, :]

        def unit_scores(pe, n):
            head, half = UNITS[n]
            par = head % 2
            pe.wait_ge(tree.sem, tree.done(8 * n + 8))
            pe.wait_ge(started.sem, started.done(n + 1 if half == 0 else n))
            if n:
                pe.wait_ge(advanced.sem, advanced.done(4 * n))
                pe.wait_ge(o_evac.sem, o_evac.done(n))
                pe.wait_ge(h_root.sem, h_root.done(n))
            if half == 0 and head:
                pe.wait_ge(h_scaled.sem, h_scaled.done(2 * head))
            for c in range(UNIT):
                last = nc.tensor.transpose(bank(6)[:, c * P:(c + 1) * P], kd[128][:, c * P:(c + 1) * P], ident[:])
            last.then_inc(k_turned.sem, 1)
            for c in range(UNIT):
                cc = slice(half * HALF + c * P, half * HALF + (c + 1) * P)
                nc.tensor.matmul(bank(0)[:, c * P:(c + 1) * P], bk[:, par, cc], bq[:, par, cc],
                                 start=True, stop=True)
            for l, h in enumerate(LEVELS):
                for c in range(UNIT):
                    keys = bk[:, par, half * HALF + c * P:half * HALF + (c + 1) * P] if h == 1 else \
                        kd[h][:, c * P:(c + 1) * P]
                    a = (l % 2) * 2 * P + c * (P // 2)
                    last = nc.tensor.matmul(bank(1 + l // 2)[:, a:a + P // 2], keys,
                                            right(qd[h][:, c * P:(c + 1) * P], h), start=True, stop=True)
            last.then_inc(scored.sem, 1)

        def unit_growth(pe, n):
            head, half = UNITS[n]
            pe.wait_ge(k_nat.sem, k_nat.done(n + 1))
            for c in range(UNIT):
                a = (UNIT * half + c) * P
                last = nc.tensor.matmul(bank(6)[:, c * P:(c + 1) * P], kd_nat[:, c * P:(c + 1) * P],
                                        bv[:, head % 2, a:a + P], start=True, stop=True)
            last.then_inc(grown.sem, 1)

        def unit_outputs(pe, n):
            head, half = UNITS[n]
            pe.wait_ge(placed.sem, placed.done(12 * n + 12))
            pe.wait_ge(advanced.sem, advanced.done(4 * n + 3))
            for c in range(UNIT):
                cc, a = slice(c * P, (c + 1) * P), (UNIT * half + c) * P
                nc.tensor.matmul(bank(0)[:, cc], bv[:, head % 2, a:a + P], scores[:, cc], start=True, stop=False)
                last = nc.tensor.matmul(bank(0)[:, cc], state[:, c], qd[128][:, cc], start=False, stop=True)
            last.then_inc(o_done.sem, 1)

        def unit_sums(pe, n):
            pe.wait_ge(h_square.sem, h_square.done(n + 1))
            for c in range(UNIT):
                last = nc.tensor.matmul(bank(4)[:, 2 * P + c:2 * P + c + 1],
                                        (kd_nat, scores)[n % 2][:, c * P:(c + 1) * P], ones[:, 0:1],
                                        start=True, stop=True)
            last.then_inc(h_sum.sem, 1)

        def unit_spread(pe, n):
            pe.wait_ge(h_wide.sem, h_wide.done(n + 1))
            for c in range(UNIT):
                last = nc.tensor.matmul(bank(1 + n % 2)[:, c * P:(c + 1) * P],
                                        (kd_nat, scores)[n % 2][:, c * P:(c + 1) * P], ident[:],
                                        start=True, stop=True)
            last.then_inc(h_spread.sem, 1)

        def meta_transpose(pe, head):
            pe.wait_ge(meta_k.sem, meta_k.done(2 * head + 2))
            if head:
                pe.wait_ge(advanced.sem, advanced.done(8 * head))
            nc.tensor.transpose(bank(6, P, META), meta_decay[:, META:], ident[:]).then_inc(meta_turned.sem, 1)

        def meta_growth(pe, head):
            pe.wait_ge(meta_nat.sem, meta_nat.done(head + 1))
            nc.tensor.matmul(bank(6, P), meta_rows[:], bv[0:META, head % 2, SEQ:],
                             start=True, stop=True).then_inc(meta_grown.sem, 1)

        def recurrence_tensor(pe):
            for h in range(-1, HG_HEADS):
                j = h + 1
                if h >= 0:
                    project(pe, j, "a0")
                    unit_scores(pe, 2 * h)
                    project(pe, j, "a1")
                    unit_growth(pe, 2 * h)
                    project(pe, j, "a2")
                    unit_outputs(pe, 2 * h)
                    project(pe, j, "b0")
                    project(pe, j, "b1")
                    unit_sums(pe, 2 * h)
                    project(pe, j, "b2")
                for u in ("bt0", "bt1", "bm"):
                    project(pe, j, u)
                if h >= 0:
                    unit_scores(pe, 2 * h + 1)
                project(pe, j, "q0")
                if h >= 0:
                    unit_growth(pe, 2 * h + 1)
                project(pe, j, "q1")
                if h >= 0:
                    unit_outputs(pe, 2 * h + 1)
                if j < HG_HEADS:
                    meta_transpose(pe, j)
                    project(pe, j, "g0")
                    meta_growth(pe, j)
                if h >= 0:
                    if j == HG_HEADS:
                        project(pe, j + 1, "a0")
                    unit_sums(pe, 2 * h + 1)
                    unit_spread(pe, 2 * h)
                if j < HG_HEADS:
                    project(pe, j, "g1")
                else:
                    project(pe, j + 1, "a1")
                if h >= 0:
                    unit_spread(pe, 2 * h + 1)
            project(pe, HG_HEADS + 1, "a2")

        def recurrence_scalar(act):
            def keys(n):
                act.wait_ge(k_turned.sem, k_turned.done(n + 1))
                if n:
                    act.wait_ge(h_sum.sem, h_sum.done(n))
                    if n % 2 == 0:
                        act.wait_ge(h_spread.sem, h_spread.done(n - 1))
                nc.scalar.activation(kd_nat[:], bank(6), ACT.Copy).then_inc(k_nat.sem, 1)

            def outputs(n):
                head, half = UNITS[n]
                act.wait_ge(o_done.sem, o_done.done(n + 1))
                act.wait_ge(grown.sem, grown.done(n + 1))
                nc.scalar.activation((kd_nat, scores)[n % 2][:], bank(0), ACT.Square).then_inc(h_square.sem, 1)
                nc.scalar.activation(mixed[:, MIX_HG + head, X_PARTS[half]], bank(0), ACT.Copy)\
                    .then_inc(o_evac.sem, 1)

            def roots(n):
                act.wait_ge(h_sum.sem, h_sum.done(n + 1))
                if n >= 2:
                    act.wait_ge(h_inv.sem, h_inv.done(n - 1))
                nc.scalar.activation(root[:, 4 * (n % 2):4 * (n % 2) + 4], bank(4)[:, 2 * P:2 * P + 4], ACT.Sqrt,
                                     scale=1.0 / HG_DIM, bias=eps).then_inc(h_root.sem, 1)

            for h in range(-1, HG_HEADS):
                j = h + 1
                if h >= 0:
                    keys(2 * h)
                    high_chunk(act, ("B", j))
                    evacuate(act, j, "a0")
                    evacuate(act, j, "a1")
                    evacuate(act, j, "a2")
                    outputs(2 * h)
                    evacuate(act, j, "b0")
                    evacuate(act, j, "b1")
                    roots(2 * h)
                    evacuate(act, j, "b2")
                for u in ("bt0", "bt1", "bm"):
                    evacuate(act, j, u)
                if h >= 0:
                    keys(2 * h + 1)
                high_chunk(act, ("A", j + 1))
                evacuate(act, j, "q0")
                evacuate(act, j, "q1")
                if h >= 0:
                    outputs(2 * h + 1)
                if j < HG_HEADS:
                    act.wait_ge(meta_turned.sem, meta_turned.done(j + 1))
                    nc.scalar.activation(meta_rows[:], bank(6, P, META), ACT.Copy).then_inc(meta_nat.sem, 1)
                    evacuate(act, j, "g0")
                else:
                    evacuate(act, j + 1, "a0")
                if h >= 0:
                    roots(2 * h + 1)
                if j < HG_HEADS:
                    evacuate(act, j, "g1")
                else:
                    evacuate(act, j + 1, "a1")
                    evacuate(act, j + 1, "a2")

        def tree_steps(dve, n):
            head, half = UNITS[n]
            cols = X_PARTS[half]
            q, f, k = bq[:, head % 2, cols], bf[:, head % 2, cols], bk[:, head % 2, cols]

            def stage(ins, m):
                ins.then_inc(tree.sem, 1)
                dve.wait_ge(tree.sem, tree.done(8 * n + m))

            def side(ap, h, right_):
                return ap.rearrange("p (b two j) -> p b two j", two=2, j=h)[:, :, right_, :]

            def next_total(h):
                if h == P // 2:
                    return nc.vector.tensor_tensor(total[:], fac[h][:, :, 1], fac[h][:, :, 2], ALU.mult)
                s4 = fac[h][:].rearrange("p (b l) e -> p b l e", l=2)
                return nc.vector.tensor_tensor(fac[2 * h][:, :, 1:3], s4[:, :, :, 1], s4[:, :, :, 2], ALU.mult)

            if n:
                dve.wait_ge(placed.sem, placed.done(12 * n))
            f4 = f.rearrange("p (b l e) -> p b l e", l=2, e=2)
            nc.vector.tensor_tensor(fac[2][:, :, 1:3], f4[:, :, :, 0], f4[:, :, :, 1], ALU.mult)
            nc.vector.tensor_tensor(side(kd[2], 1, 0), side(k, 1, 0), side(f, 1, 1), ALU.mult)
            nc.vector.tensor_copy(side(kd[2], 1, 1), side(k, 1, 1))
            stage(nc.vector.tensor_tensor(qd[1], q, f, ALU.mult), 1)
            nc.vector.tensor_tensor(side(qd[2], 1, 1), side(qd[1], 1, 1), side(f, 1, 0), ALU.mult)
            nc.vector.tensor_copy(side(qd[2], 1, 0), side(qd[1], 1, 0))
            stage(next_total(2), 2)
            for m, h in enumerate(LEVELS[1:]):
                if h == P // 2 and n:
                    dve.wait_ge(o_done.sem, o_done.done(n))
                b = U // (2 * h)
                keep = fac[h][:, :, 2:4].unsqueeze(3).to_broadcast([P, b, 2, h])
                take = fac[h][:, :, 0:2].unsqueeze(3).to_broadcast([P, b, 2, h])
                v = "p (b l j) -> p b l j"
                nc.vector.tensor_tensor(kd[2 * h][:].rearrange(v, l=2, j=h), kd[h][:].rearrange(v, l=2, j=h),
                                        keep, ALU.mult)
                last = nc.vector.tensor_tensor(qd[2 * h][:].rearrange(v, l=2, j=h),
                                               qd[h][:].rearrange(v, l=2, j=h), take, ALU.mult)
                if h < P // 2:
                    last = next_total(2 * h)
                stage(last, 3 + m)

        def recurrence_vector(dve):
            def place(n):
                head, half = UNITS[n]
                dve.wait_ge(scored.sem, scored.done(n + 1))
                if n:
                    dve.wait_ge(h_sum.sem, h_sum.done(n))
                if half == 0 and n:
                    dve.wait_ge(h_spread.sem, h_spread.done(n))
                nc.vector.tensor_tensor(scores[:].rearrange("p (c t) -> p c t", c=UNIT),
                                        bank(0).rearrange("p (c t) -> p c t", c=UNIT),
                                        ident[:].unsqueeze(1).to_broadcast([P, UNIT, P]), ALU.mult)\
                    .then_inc(placed.sem, 1)
                for b in range(4):
                    levels = min(2, len(LEVELS) - 2 * b)
                    v = "p (l c t) -> p l c t"
                    msk = level_mask[:, 2 * b:2 * b + levels, :].unsqueeze(2)\
                        .to_broadcast([P, levels, UNIT, P // 2])
                    nc.vector.tensor_tensor(
                        masked[:, b * HALF:b * HALF + levels * 2 * P].rearrange(v, l=levels, c=UNIT),
                        bank(1 + b, levels * 2 * P).rearrange(v, l=levels, c=UNIT), msk, ALU.mult)\
                        .then_inc(placed.sem, 1)
                for m, h in enumerate(LEVELS):
                    dst = right(scores[:], h)
                    src = masked[:, m * 2 * P:(m + 1) * 2 * P].rearrange("p (a j) -> p a j", j=h)
                    dve.wait_ge(placed.sem, placed.done(12 * n + 5 + m))
                    nc.vector.tensor_tensor(dst, dst, src, ALU.add).then_inc(placed.sem, 1)
                if half:
                    dve.wait_ge(o_done.sem, o_done.done(n))
                    nc.vector.tensor_copy(state[:, 0], state[:, UNIT]).then_inc(started.sem, 1)
                dve.wait_ge(grown.sem, grown.done(n + 1))
                for c in range(UNIT):
                    if c == 0:
                        dve.wait_ge(started.sem, started.done(n + 1))
                    else:
                        dve.wait_ge(advanced.sem, advanced.done(4 * n + c))
                    nc.vector.scalar_tensor_tensor(state[:, c + 1], state[:, c], total[:, c:c + 1],
                                                   bank(6)[:, c * P:(c + 1) * P], ALU.mult, ALU.add)\
                        .then_inc(advanced.sem, 1)
                dve.wait_ge(advanced.sem, advanced.done(4 * n + 4))

            def invert(n):
                dve.wait_ge(h_root.sem, h_root.done(n + 1))
                c = slice(4 * (n % 2), 4 * (n % 2) + 4)
                nc.vector.reciprocal(inv[:, c], root[:, c]).then_inc(h_inv.sem, 1)

            def widen(n):
                dve.wait_ge(h_inv.sem, h_inv.done(n + 1))
                dve.wait_ge(h_sum.sem, h_sum.done(n + 1))
                dve.wait_ge(grown.sem, grown.done(n + 1 + (1 - n % 2)))
                c = slice(4 * (n % 2), 4 * (n % 2) + 4)
                nc.vector.tensor_copy((kd_nat, scores)[n % 2][:].rearrange("p (c t) -> p c t", c=UNIT),
                                      inv[:, c].unsqueeze(2).to_broadcast([P, UNIT, P])).then_inc(h_wide.sem, 1)

            def finish(n):
                head, half = UNITS[n]
                m = mixed[:, MIX_HG + head, X_PARTS[half]]
                dve.wait_ge(h_spread.sem, h_spread.done(n + 1))
                nc.vector.scalar_tensor_tensor(m, m, hgg[:, head:head + 1], bank(1 + n % 2), ALU.mult, ALU.mult)\
                    .then_inc(h_scaled.sem, 1)
                dve.wait_ge(h_scaled.sem, h_scaled.done(n + 1))
                nc.vector.tensor_tensor(m, m, gate_buf[head % 2][:, X_PARTS[half]], ALU.mult)\
                    .then_inc(h_mixed.sem, 1)

            def prepare(j):
                par = j % 2
                dve.wait_ge(p_evac.sem, p_evac.done(USE[j, "a2"] + 1))
                nc.vector.tensor_scalar(bf[:, par], bf[:, par], one_minus[:, j:j + 1], lower[:, j:j + 1],
                                        ALU.mult, ALU.add)
                nc.vector.tensor_scalar(bk[:, par], bk[:, par], one_minus[:, j:j + 1], None, ALU.mult)\
                    .then_inc(gates.sem, 1)
                dve.wait_ge(gates.sem, gates.done(j + 1))
                if j:
                    dve.wait_ge(meta_turned.sem, meta_turned.done(j))
                nc.vector.memset(meta_decay[:, META - 1:META], 1.0)
                nc.vector.tensor_tensor_scan(meta_decay[:, 0:META - 1][:, ::-1], bf[:, par, SEQ + 1:L][:, ::-1],
                                             ones[:, 0:META - 1], 1.0, ALU.mult, ALU.mult).then_inc(meta_k.sem, 1)
                dve.wait_ge(meta_k.sem, meta_k.done(2 * j + 1))
                nc.vector.tensor_tensor(meta_decay[:, META:], bk[:, par, SEQ:L], meta_decay[:, 0:META],
                                        ALU.mult).then_inc(meta_k.sem, 1)
                dve.wait_ge(p_evac.sem, p_evac.done(USE[j, "q1"] + 1))
                tree_steps(dve, 2 * j)

            dve.wait_ge(fills.sem, 1)
            for h in range(-1, HG_HEADS):
                j = h + 1
                if h >= 0:
                    low_chunk(dve, ("B", j))
                    place(2 * h)
                    tree_steps(dve, 2 * h + 1)
                    invert(2 * h)
                low_chunk(dve, ("A", j + 1))
                if h >= 0:
                    place(2 * h + 1)
                    widen(2 * h)
                if j < HG_HEADS:
                    prepare(j)
                    dve.wait_ge(meta_grown.sem, meta_grown.done(j + 1))
                    if j:
                        dve.wait_ge(o_done.sem, o_done.done(2 * j))
                    nc.vector.tensor_copy(state[:, 0], bank(6, P)).then_inc(started.sem, 1)
                if h >= 0:
                    invert(2 * h + 1)
                    widen(2 * h + 1)
                    finish(2 * h)
                for half in range(2):
                    if j < HG_HEADS:
                        n = USE[j, f"g{half}"]
                        g = gate_buf[j % 2][:, X_PARTS[half]]
                        dve.wait_ge(p_evac.sem, p_evac.done(n + 1))
                        nc.vector.tensor_tensor(g, g, bank(bank_of(n)), ALU.mult).then_inc(g_silu.sem, 1)
                if h >= 0:
                    if h == HG_HEADS - 1:
                        dve.wait_ge(g_silu.sem, g_silu.done(2 * HG_HEADS))
                    finish(2 * h + 1)

        NP, NG = len(PIECES), len(GROUPS)

        def fill_of(n):
            pair, m = n // PER_PAIR, n % PER_PAIR
            if pair == 3 or m not in FILL or (pair == 0 and FILL[m] in ("a0", "a1", "a2", "b0")):
                return None
            return 5 + pair, FILL[m]

        NORM_ORDER = [NORM_AT[n] for n in sorted(NORM_AT)]

        def attention_tensor(pe):
            def score(n):
                pair, b, par, lo, hi, width, buf = PIECES[n]
                rows, kv = slice(64 * par, 64 * par + 64), pair % 2
                if n % PER_PAIR == 0:
                    pe.wait_ge(p_evac.sem, p_evac.done(USE[4 + pair, "q1"] + 1))
                for a in range(lo, hi, HALF):
                    z = min(a + HALF, hi)
                    c, e = max(a, width - P), min(z, width)
                    at_ = 2 * (n % 2) * HALF + a - lo
                    last = nc.tensor.matmul(ps[:, at_:at_ + z - a], bq[rows, kv, b * P:(b + 1) * P],
                                            bf[rows, kv, a:z], start=True, stop=c >= e)
                    if c < e:
                        last = nc.tensor.matmul(ps[:, at_ + c - a:at_ + e - a], ident_bf[:],
                                                hidden_bf[:, c - (width - P):e - (width - P)],
                                                start=False, stop=True)
                last.then_inc(z_done.sem, 1)

            def turn(g):
                n, tiles, _, _ = GROUPS[g]
                if g >= 2:
                    copied = (pt_even, pt_odd)[g % 2]
                    pe.wait_ge(copied.sem, copied.done(g // 2))
                for j, (col, _, _) in enumerate(tiles):
                    last = nc.tensor.transpose(bank((4, 6)[g % 2])[:, j * P:(j + 1) * P],
                                               probs[:, PIECES[n][6], col:col + P], ident[:])
                last.then_inc(t_done.sem, 1)

            def values(g):
                n, tiles, begin, end = GROUPS[g]
                pair, b, par = PIECES[n][:3]
                copied = (pt_even, pt_odd)[g % 2]
                pe.wait_ge(copied.sem, copied.done(g // 2 + 1))
                e = 2 * pair + b // 4
                if begin and par == 0 and b % 4 == 0 and e:
                    pe.wait_ge(av_evac.sem, av_evac.done(e))
                dst = ps[64 * par:64 * par + 64, 5 * HALF + (b % 4) * P:5 * HALF + (b % 4 + 1) * P]
                for j, (_, rows, t) in enumerate(tiles):
                    a = t * P + par * SB_DIM
                    last = nc.tensor.matmul(dst, bv[0:rows, pair % 2, a:a + SB_DIM],
                                            probs_t[0:rows, g % 3, j * P:(j + 1) * P],
                                            start=begin and j == 0, stop=end and j == len(tiles) - 1)
                if end and par == 1 and b % 4 == 3:
                    last.then_inc(av_done.sem, 1)

            pe.wait_ge(h_mixed.sem, h_mixed.done(2 * HG_HEADS))
            score(0)
            score(1)
            project(pe, HG_HEADS + 1, "b0")
            for n in range(NP):
                pe.wait_ge(w_done.sem, w_done.done(n + 1))
                for i, g in enumerate(GROUPS_OF[n]):
                    turn(g)
                    if i == 0 and n + 2 < NP:
                        score(n + 2)
                    if g >= 2:
                        values(g - 2)
                    if i == 0 and fill_of(n):
                        bank7_free(pe, n)
                        project(pe, *fill_of(n))
                    if i == 0 and n in NORM_AT:
                        bank7_free(pe, n, True)
                        head_norm_tensor(pe, *NORM_AT[n])
            values(NG - 2)
            values(NG - 1)

        def steps_before(n, step):
            return sum(1 for m, (e, st) in NORM_AT.items() if m < n and st == step)

        def bank7_free(pe, n, norm=False):
            if norm:
                done = [USE[f] for m in range(n + 1) if (f := fill_of(m))]
                if done:
                    pe.wait_ge(p_evac.sem, p_evac.done(max(done) + 1))
            a, b = steps_before(n, "sums"), steps_before(n, "spread")
            if a:
                pe.wait_ge(s_root.sem, s_root.done(a))
            if b:
                pe.wait_ge(s_mixed.sem, s_mixed.done(b))

        def head_norm_tensor(pe, e, step):
            if step == "sums":
                pe.wait_ge(s_square.sem, s_square.done(e + 1))
                for c in range(UNIT):
                    last = nc.tensor.matmul(bank(7)[:, 2 * c:2 * c + 2], squares[:, c * P:(c + 1) * P],
                                            ones_pair[:], start=True, stop=True)
                last.then_inc(s_sum.sem, 1)
            else:
                pe.wait_ge(s_wide.sem, s_wide.done(e + 1))
                for c in range(UNIT):
                    last = nc.tensor.matmul(bank(7)[:, c * P:(c + 1) * P], spread[:, c * P:(c + 1) * P], ident[:],
                                            start=True, stop=True)
                last.then_inc(s_spread.sem, 1)

        def head_norm_scalar(act, e, step):
            if step == "sums":
                act.wait_ge(s_sum.sem, s_sum.done(e + 1))
                if e:
                    act.wait_ge(s_inv.sem, s_inv.done(e))
                nc.scalar.activation(root[:, 8:16], bank(7, 8), ACT.Sqrt, scale=1.0 / SB_DIM, bias=eps)\
                    .then_inc(s_root.sem, 1)

        def head_norm_vector(dve, e, step):
            if step == "sums":
                dve.wait_ge(s_root.sem, s_root.done(e + 1))
                if e:
                    dve.wait_ge(s_spread.sem, s_spread.done(e))
                nc.vector.reciprocal(inv[:, 8:16], root[:, 8:16]).then_inc(s_inv.sem, 1)
                dve.wait_ge(s_inv.sem, s_inv.done(e + 1))
                nc.vector.tensor_copy(spread[:].rearrange("p (c t) -> p c t", c=2 * UNIT),
                                      inv[:, 8:16].unsqueeze(2).to_broadcast([P, 2 * UNIT, SB_DIM]))\
                    .then_inc(s_wide.sem, 1)
            else:
                m = mixed[:, e // 2, X_PARTS[e % 2]]
                dve.wait_ge(s_spread.sem, s_spread.done(e + 1))
                dve.wait_ge(av_evac.sem, av_evac.done(e + 1))
                nc.vector.scalar_tensor_tensor(m, m, sbg[:, e // 2:e // 2 + 1], bank(7), ALU.mult, ALU.mult)\
                    .then_inc(s_mixed.sem, 1)

        SPLITS = [(4 + t, half) for t in range(4) for half in range(2)] + \
            [(t, half) for t in range(4) for half in range(2)]
        SPLIT_AT = {3 * PER_PAIR - 3 + n + (4 if n == 14 else 0): SPLITS[n] for n in range(15)}

        def split_scalar(act, t, half):
            if t < 4:
                act.wait_ge(s_mixed.sem, s_mixed.done(2 * t + half + 1))
            act.wait_ge(p_done.sem, p_done.done(len(USES)))
            nc.scalar.activation(act_hi[:, t, X_PARTS[half]], mixed[:, t, X_PARTS[half]], ACT.Copy)\
                .then_inc(m_hi.sem, 1)

        def split_vector(dve, t, half):
            dve.wait_ge(m_hi.sem, m_hi.done(SPLITS.index((t, half)) + 1))
            nc.vector.tensor_tensor(act_lo[:, t, X_PARTS[half]], mixed[:, t, X_PARTS[half]],
                                    act_hi[:, t, X_PARTS[half]].bitcast(F32), ALU.subtract).then_inc(m_lo.sem, 1)

        CHUNK_AT = {8: ("A", 6), 15: ("B", 6), PER_PAIR + 8: ("A", 7), 2 * PER_PAIR + 8: ("O", 0)}

        def attention_scalar(act):
            def sigmoids(n):
                pair, b, par, lo, hi, width, buf = PIECES[n]
                z = bank(2 * (n % 2), hi - lo)
                act.wait_ge(z_done.sem, z_done.done(n + 1))
                if n >= 2:
                    act.wait_ge(w_done.sem, w_done.done(n - 1))
                nc.scalar.activation(beta[:, buf, lo:hi], z, ACT.Sigmoid, scale=-SB_SCALE)\
                    .then_inc(beta_done.sem, 1)
                nc.scalar.activation(z, z, ACT.Sigmoid, scale=SB_SCALE).then_inc(sig_done.sem, 1)

            def out_evac(e):
                act.wait_ge(av_done.sem, av_done.done(e + 1))
                if e:
                    act.wait_ge(s_sum.sem, s_sum.done(e))
                nc.scalar.activation(squares[:], bank(5), ACT.Square).then_inc(s_square.sem, 1)
                nc.scalar.activation(mixed[:, e // 2, X_PARTS[e % 2]], bank(5), ACT.Copy).then_inc(av_evac.sem, 1)

            def group(g):
                if g % 2 == 0:
                    w = P * len(GROUPS[g][1])
                    act.wait_ge(t_done.sem, t_done.done(g + 1))
                    nc.scalar.activation(probs_t[:, g % 3, 0:w], bank(4, w), ACT.Copy).then_inc(pt_even.sem, 1)

            act.wait_ge(h_mixed.sem, h_mixed.done(2 * HG_HEADS))
            sigmoids(0)
            sigmoids(1)
            evacuate(act, HG_HEADS + 1, "b0")
            for n in range(NP):
                busy = fill_of(n) is not None
                group(GROUPS_OF[n][0])
                if n + 2 < NP:
                    sigmoids(n + 2)
                if busy:
                    evacuate(act, *fill_of(n))
                if n in NORM_AT:
                    head_norm_scalar(act, *NORM_AT[n])
                for g in GROUPS_OF[n][1:]:
                    group(g)
                if n - 1 in HALF_ENDS:
                    out_evac(HALF_ENDS.index(n - 1))
                for part in range(2):
                    if n - part in CHUNK_AT:
                        high_chunk(act, CHUNK_AT[n - part], None, part)
                if n in SPLIT_AT:
                    split_scalar(act, *SPLIT_AT[n])
            out_evac(7)

        def attention_vector(dve):
            def weigh(n):
                pair, b, par, lo, hi, width, buf = PIECES[n]
                dve.wait_ge(beta_done.sem, beta_done.done(n + 1))
                if hi == width:
                    src, dst, begin = beta[:, buf, lo + 1:hi], later[:, buf, lo:hi - 1], 1.0
                else:
                    dve.wait_ge(scanned.sem, scanned.done(n))
                    src, dst = beta[:, buf, lo + 1:hi + 1], later[:, buf, lo:hi]
                    begin = later[:, buf, hi:hi + 1]
                nc.vector.tensor_tensor_scan(dst[:, ::-1], src[:, ::-1],
                                             ones[:, 0:1].to_broadcast([P, src.shape[-1]]),
                                             begin, ALU.mult, ALU.mult).then_inc(scanned.sem, 1)
                dve.wait_ge(scanned.sem, scanned.done(n + 1))
                older = [m for m in range(n) if PIECES[m][6] == buf and PIECES[m][:3] != PIECES[n][:3]]
                if older:
                    dve.wait_ge(t_done.sem, t_done.done(GROUPS_OF[older[-1]][-1] + 1))
                dve.wait_ge(sig_done.sem, sig_done.done(n + 1))
                nc.vector.tensor_tensor(probs[:, buf, lo:hi], bank(2 * (n % 2), hi - lo),
                                        later[:, buf, lo:hi], ALU.mult).then_inc(w_done.sem, 1)

            def group(g):
                if g % 2 == 1:
                    w = P * len(GROUPS[g][1])
                    dve.wait_ge(t_done.sem, t_done.done(g + 1))
                    nc.vector.tensor_copy(probs_t[:, g % 3, 0:w], bank(6, w)).then_inc(pt_odd.sem, 1)

            dve.wait_ge(h_mixed.sem, h_mixed.done(2 * HG_HEADS))
            nc.vector.memset(later[:], 0.0).then_inc(fills.sem, 1)
            dve.wait_ge(fills.sem, 2)
            weigh(0)
            weigh(1)
            for n in range(NP):
                busy = fill_of(n) is not None
                group(GROUPS_OF[n][0])
                if busy and n + 2 < NP:
                    weigh(n + 2)
                for g in GROUPS_OF[n][1:]:
                    group(g)
                if not busy and n + 2 < NP:
                    weigh(n + 2)
                if n in NORM_AT:
                    head_norm_vector(dve, *NORM_AT[n])
                for part in range(2):
                    if n - 2 - part in CHUNK_AT:
                        low_chunk(dve, CHUNK_AT[n - 2 - part], part)
                if n in SPLIT_AT:
                    split_vector(dve, *SPLIT_AT[n])

        with nc.Block() as blk:
            @blk.sync
            def _(sp):
                for t in range(TT):
                    sp.dma_start(x_in[:, t], x2[t * P:(t + 1) * P, :]).then_inc(x_came[t].sem, 16)
                    if t == 3:
                        load_chunk(sp, ("A", 0))
                sp.dma_start(x_meta[:], meta).then_inc(x_came[TT].sem, 16)
                for name, _, _ in CHUNKS[1:]:
                    load_chunk(sp, name)
                load_chunk(sp, ("O", 2))
                load_chunk(sp, ("O", 3))

                def load(c, j, before):
                    sp.wait_ge(before[0].sem, before[0].done(before[1]))
                    if c == "d":
                        sp.dma_start(w_raw[:].rearrange("p (f n) -> p f n", f=2),
                                     w_down_v[:, bass.ds(2 * j, 2), :]).then_inc(came[c].sem, 16)
                    else:
                        src = w_gate_v if c == "g" else w_up_v
                        sp.dma_start(w_raw[:].rearrange("p (k n) -> p k n", k=KT),
                                     src[:, :, bass.ts(j, CW)]).then_inc(came[c].sem, 16)

                load("g", 0, (w_low, CHUNK_NO["O", 3] + 1))
                load("u", 0, (low["g"], 1))
                load("g", 1, (low["u"], 1))
                load("u", 1, (low["g"], 2))

                def segment(j):
                    load("d", j - 1, (low["u"], j + 1))
                    load("g", j + 1, (low["d"], j))
                    load("u", j + 1, (low["g"], j + 2))

                with sp.Fori(0, (FG - 3) // 2) as r:
                    segment(2 * r + 1)
                    segment(2 * r + 2)
                segment(FG - 2)
                load("d", FG - 2, (low["u"], FG))
                load("d", FG - 1, (low["d"], FG - 1))
                for t in range(TT):
                    sp.wait_ge(e_norm.sem, e_norm.done(t + 1))
                    sp.dma_start(out2[t * P:(t + 1) * P, :], h_sq[:, t % 2]).then_inc(stored[t % 2].sem, 16)
                for s in range(2):
                    sp.wait_ge(stored[s].sem, 16 * TT // 2)

            @blk.gpsimd
            def _(pool):
                pool.dma_start(gain[:], norm1_g[0:1, :].to_broadcast([P, D])).then_inc(gain1.sem, 16)
                nc.gpsimd.memset(ident[:], 0.0).then_inc(filled.sem, 1)
                pool.wait_ge(filled.sem, 1)
                nc.gpsimd.affine_select(out=ident[:], in_=ident[:], compare_op=ALU.not_equal, fill=1.0,
                                        base=0, pattern=[[-1, P]], channel_multiplier=1).then_inc(filled.sem, 1)
                with nc.allow_non_contiguous_dma(reason="a gain for each partition"):
                    for dst, src in ((sbg, sb_g[0]), (hgg, hg_g[0]), (logit0, lb_logits[0]), (logit1, lb_logits[1])):
                        pool.dma_start(dst, src.rearrange("(t p) -> p t", p=P)).then_inc(consts.sem, 16)
                nc.gpsimd.memset(ones[:], 1.0)
                nc.gpsimd.memset(ones_pair[:], 1.0)
                nc.gpsimd.memset(level_mask[:], 1.0)
                nc.gpsimd.memset(hidden_bf[:], 0.0).then_inc(filled.sem, 1)
                pool.wait_ge(filled.sem, 3)
                nc.gpsimd.affine_select(out=ones_pair[:, 0:1], in_=ones_pair[:, 0:1], compare_op=ALU.is_ge,
                                        fill=0.0, base=63, pattern=[[0, 1]], channel_multiplier=-1)
                nc.gpsimd.affine_select(out=ones_pair[:, 1:2], in_=ones_pair[:, 1:2], compare_op=ALU.is_ge,
                                        fill=0.0, base=-64, pattern=[[0, 1]], channel_multiplier=1)
                nc.gpsimd.affine_select(out=hidden_bf[:], in_=hidden_bf[:], compare_op=ALU.is_gt, fill=MASKED,
                                        base=0, pattern=[[-1, P]], channel_multiplier=1)
                for n, h in enumerate(LEVELS):
                    m = level_mask[:, n, :].rearrange("p (b j) -> p b j", j=h)
                    nc.gpsimd.affine_select(out=m, in_=m, compare_op=ALU.is_ge, fill=0.0, base=0,
                                            pattern=[[-2 * h, P // (2 * h)], [0, h]], channel_multiplier=1)\
                        .then_inc(filled.sem, 1)
                    pool.wait_ge(filled.sem, 4 + 2 * n)
                    nc.gpsimd.affine_select(out=m, in_=m, compare_op=ALU.is_ge, fill=0.0, base=h - 1,
                                            pattern=[[2 * h, P // (2 * h)], [0, h]], channel_multiplier=-1)\
                        .then_inc(filled.sem, 1)
                pool.wait_ge(n1.normed.sem, n1.normed.done(TT + 1))
                pool.wait_ge(n1.turned.sem, n1.turned.done(TT + 1))
                for h in LEVELS[1:]:
                    last = nc.gpsimd.memset(fac[h][:], 1.0)
                last.then_inc(fills.sem, 1)
                pool.wait_ge(h_mixed.sem, h_mixed.done(2 * HG_HEADS))
                pool.dma_start(gain[:], norm2_g[0:1, :].to_broadcast([P, D])).then_inc(gain2.sem, 16)
                pool.wait_ge(av_evac.sem, av_evac.done(8))
                for t in range(TT):
                    pool.dma_start(h_res[:, t, :], x2[t * P:(t + 1) * P, :]).then_inc(x_back.sem, 16)
                pool.wait_ge(n2.normed.sem, n2.normed.done(TT))
                pool.dma_start(gain[:], final_g.rearrange("(a n) -> a n", a=1).to_broadcast([P, D]))\
                    .then_inc(gain3.sem, 16)

            @blk.scalar
            def _(act):
                act.wait_ge(eps_set.sem, 1)
                nc.scalar.activation(table_load, eps, ACT.Sqrt)

                def stats(t):
                    act.wait_ge(x_came[t].sem, 16)
                    n1.stats(act, t, t % 2, rows_of(t))

                def high_part(t):
                    n1.high(act, t, t % 2, rows_of(t))

                for t in range(TT + 1):
                    stats(t)
                    if 2 <= t < TT:
                        high_part(t - 2)
                    if t == 3:
                        high_chunk(act, ("A", 0))
                evacuate(act, 0, "a0")
                evacuate(act, 0, "b0")
                high_part(TT - 2)
                high_part(TT - 1)
                evacuate(act, 0, "a1")
                high_part(TT)
                act.wait_ge(bounds.sem, 2)
                nc.scalar.activation(lower, lower_x, ACT.Sigmoid)
                nc.scalar.activation(one_minus, one_x, ACT.Sigmoid).then_inc(bounds.sem, 1)
                evacuate(act, 0, "b1")
                high_chunk(act, ("B", 0))
                evacuate(act, 0, "a2")
                evacuate(act, 0, "b2")
                recurrence_scalar(act)
                attention_scalar(act)
                head_norm_scalar(act, 7, "sums")
                for t, half in SPLITS[15:]:
                    split_scalar(act, t, half)
                high_chunk(act, ("O", 1))
                high_chunk(act, ("O", 2), (o_proj, TT))
                high_chunk(act, ("O", 3), (o_proj, 2 * TT))

                def split(c, j, free=None, slot=None):
                    act.wait_ge(came[c].sem, came[c].done(16 * j + 16))
                    if free:
                        act.wait_ge(free[0].sem, free[0].done(free[1]))
                    nc.scalar.activation((slot or ffn_slot(c))[0], w_raw[:], ACT.Copy)\
                        .then_inc(high[c].sem, 1)

                split("g", 0, (o_proj, 3 * TT), ffn_slot("g", True))
                for t in range(TT + 2):
                    if t < TT:
                        act.wait_ge(o_add.sem, o_add.done(3 * TT + t + 1))
                        if t == 0:
                            act.wait_ge(m_lo.sem, 16)
                        n2.stats(act, t, t % 2)
                    if t == TT:
                        split("u", 0, (o_proj, 4 * TT), ffn_slot("u", True))
                    if t >= 2:
                        n2.high(act, t - 2, t % 2)

                def groups(j, par, first=False):
                    for n in range(4):
                        ft, th, g_bank, _ = ffn_tile(n, first)
                        act.wait_ge(gu_done.sem, gu_done.done(4 * j + (n + 1)))
                        nc.scalar.activation(silu[:, n % 2], bank(g_bank), ACT.Sigmoid).then_inc(gate_sig.sem, 1)
                        act.wait_ge(hidden.sem, hidden.done(4 * j + (n + 1)))
                        nc.scalar.activation(f_hi[:, par, ft, X_PARTS[th]], silu[:, n % 2], ACT.Copy)\
                            .then_inc(f_high.sem, 1)

                def next_chunks(j):
                    split("g", j, (gu_done, 4 * j))
                    split("u", j, (gu_done, 4 * j))

                def segment(j, par):
                    split("d", j - 1, (dn_done, 16 * j - 16))
                    groups(j, par)
                    next_chunks(j + 1)

                split("g", 1)
                groups(0, 0, True)
                split("u", 1, (gates_used, 1))
                split("d", 0, (gu_done, 4))
                groups(1, 1)
                next_chunks(2)
                with act.Fori(0, (FG - 3) // 2) as r:
                    segment(2 * r + 2, 0)
                    segment(2 * r + 3, 1)
                split("d", FG - 2, (dn_done, 16 * (FG - 2)))
                groups(FG - 1, 0)
                split("d", FG - 1, (gu_done, 4 * FG), ffn_slot("g"))
                for t in range(TT):
                    act.wait_ge(dn_add.sem, dn_add.done(16 * (FG - 1) + 2 * t + 2))
                    if t >= 2:
                        act.wait_ge(e_norm.sem, e_norm.done(t - 1))
                    nc.scalar.activation(silu[:].rearrange("p a b -> p (a b)"), h_res[:, t, :], ACT.Square,
                                         accum_out=ssq[:, t % 2:t % 2 + 1]).then_inc(e_sum.sem, 1)
                    act.wait_ge(e_sum.sem, e_sum.done(t + 1))
                    nc.scalar.activation(std[:, t % 2:t % 2 + 1], ssq[:, t % 2:t % 2 + 1], ACT.Sqrt,
                                         scale=1.0 / D, bias=eps).then_inc(e_root.sem, 1)

            @blk.vector
            def _(dve):
                nc.vector.memset(eps, EPS).then_inc(eps_set.sem, 1)
                dve.sem_inc(n1.normed.sem, 2)
                dve.sem_inc(n1.lo.sem, 4)
                dve.sem_inc(n2.normed.sem, 2)
                dve.sem_inc(n2.lo.sem, 4)
                dve.wait_ge(gain1.sem, 16)

                def scale(t):
                    n1.scale(dve, t, t % 2, rows_of(t))

                def low_part(t):
                    n1.low(dve, t, t % 2, rows_of(t))

                for t in range(TT + 1):
                    scale(t)
                    if 2 <= t < TT:
                        low_part(t - 2)
                    if t == 3:
                        low_chunk(dve, ("A", 0))
                low_part(TT - 2)
                low_part(TT - 1)
                dve.wait_ge(filled.sem, 2)
                nc.vector.tensor_copy(ident_bf[:], ident[:])
                dve.wait_ge(consts.sem, 64)
                nc.vector.tensor_tensor(lower_x, logit0, logit1, ALU.subtract).then_inc(bounds.sem, 1)
                nc.vector.tensor_tensor(one_x, logit1, logit0, ALU.subtract).then_inc(bounds.sem, 1)
                low_part(TT)
                dve.wait_ge(bounds.sem, 3)
                low_chunk(dve, ("B", 0))
                recurrence_vector(dve)
                attention_vector(dve)
                head_norm_vector(dve, 7, "sums")
                head_norm_vector(dve, 7, "spread")
                for t, half in SPLITS[15:]:
                    split_vector(dve, t, half)

                def add(c, t):
                    dve.wait_ge(o_proj.sem, o_proj.done(TT * c + t + 1))
                    h = h_res[:, t, c * CW:(c + 1) * CW]
                    nc.vector.tensor_tensor(h, h, bank(out_bank(c, t), CW), ALU.add).then_inc(o_add.sem, 1)

                def split(c, j, slot=None):
                    dve.wait_ge(high[c].sem, high[c].done(j + 1))
                    hi_, lo_ = slot or ffn_slot(c)
                    nc.vector.tensor_tensor(lo_, w_raw[:], hi_.bitcast(F32), ALU.subtract).then_inc(low[c].sem, 1)

                dve.wait_ge(x_back.sem, 16 * TT)
                for c in range(4):
                    for t in range(TT):
                        add(c, t)
                        if c == 0 and t == 0:
                            low_chunk(dve, ("O", 1))
                        if c == 1 and t == 2:
                            low_chunk(dve, ("O", 2))
                        if c == 2 and t == 2:
                            low_chunk(dve, ("O", 3))
                        if c == 3:
                            if t == 0:
                                dve.wait_ge(gain2.sem, 16)
                                split("g", 0, ffn_slot("g", True))
                            if t:
                                n2.scale(dve, t - 1, (t - 1) % 2)
                            if t >= 2:
                                n2.low(dve, t - 2, t % 2)
                n2.scale(dve, TT - 1, (TT - 1) % 2)
                split("u", 0, ffn_slot("u", True))
                n2.low(dve, TT - 2, TT % 2)
                n2.low(dve, TT - 1, (TT - 1) % 2)

                def gate(j, par, first=False):
                    for n in range(4):
                        ft, th, g_bank, u_bank = ffn_tile(n, first)
                        s_ = silu[:, n % 2]
                        dve.wait_ge(gate_sig.sem, gate_sig.done(4 * j + (n + 1)))
                        nc.vector.tensor_tensor(s_, s_, bank(g_bank), ALU.mult).then_inc(gated.sem, 1)
                        dve.wait_ge(gated.sem, gated.done(4 * j + (n + 1)))
                        nc.vector.tensor_tensor(s_, s_, bank(u_bank), ALU.mult).then_inc(hidden.sem, 1)
                        dve.wait_ge(f_high.sem, f_high.done(4 * j + (n + 1)))
                        nc.vector.tensor_tensor(f_lo[:, par, ft, X_PARTS[th]], s_,
                                                f_hi[:, par, ft, X_PARTS[th]].bitcast(F32), ALU.subtract)\
                            .then_inc(f_low.sem, 1)

                def down_add(j, g):
                    t, half = g // 2, g % 2
                    dve.wait_ge(dn_done.sem, dn_done.done(16 * j + (g + 1)))
                    h = h_res[:, t, X_PARTS[half]]
                    nc.vector.tensor_tensor(h, h, bank(4 + g % 4), ALU.add).then_inc(dn_add.sem, 1)

                def down(j):
                    for g in range(2 * TT):
                        if g == 2:
                            split("g", j + 2)
                        if g == 10:
                            split("u", j + 2)
                        down_add(j, g)

                def segment(j, par):
                    split("d", j - 1)
                    gate(j, par)
                    down(j - 1)

                split("g", 1)
                gate(0, 0, True)
                split("u", 1)
                segment(1, 1)
                with dve.Fori(0, (FG - 3) // 2) as r:
                    segment(2 * r + 2, 0)
                    segment(2 * r + 3, 1)
                split("d", FG - 2)
                gate(FG - 1, 0)
                for g in range(2 * TT):
                    if g == 4:
                        split("d", FG - 1, ffn_slot("g"))
                    down_add(FG - 2, g)
                dve.wait_ge(gain3.sem, 16)

                def final(t):
                    s = t % 2
                    dve.wait_ge(e_root.sem, e_root.done(t + 1))
                    nc.vector.reciprocal(rstd[:, s:s + 1], std[:, s:s + 1]).then_inc(e_inv.sem, 1)
                    dve.wait_ge(e_inv.sem, e_inv.done(t + 1))
                    if t >= 2:
                        dve.wait_ge(stored[s].sem, 16 * (t // 2))
                    nc.vector.scalar_tensor_tensor(h_sq[:, s], h_res[:, t, :], rstd[:, s:s + 1], gain[:],
                                                   ALU.mult, ALU.mult).then_inc(e_norm.sem, 1)

                for t in range(TT):
                    down_add(FG - 1, 2 * t)
                    down_add(FG - 1, 2 * t + 1)
                    if t:
                        final(t - 1)
                final(TT - 1)

            @blk.tensor
            def _(pe):
                pe.sem_inc(n1.turned.sem, 2)
                pe.sem_inc(n2.turned.sem, 2)
                pe.wait_ge(filled.sem, 2)
                for step in (0, 1, 2, 3, "a0", 4, 5, "b0", 6, 7, "a1", 8, "b1", "a2", "b2"):
                    if isinstance(step, int):
                        n1.transposes(pe, step, step % 2, rows_of(step))
                    else:
                        tiles = min(TT + 1, -(-THIRDS[int(step[1])].stop // P))
                        pe.wait_ge(n1.lo.sem, n1.lo.done(2 * tiles))
                        project(pe, 0, step)
                recurrence_tensor(pe)
                attention_tensor(pe)

                order = [4, 5, 6, 7, 0, 1, 2, 3]

                def first_tile(n, c):
                    ft, th, g_bank, u_bank = ffn_tile(n, True)
                    last = turned_group(ffn_slot(c, True), ft, X_PARTS[th], bank(g_bank if c == "g" else u_bank))
                    if c == "u":
                        last.then_inc(gu_done.sem, 1)
                    elif n == 3:
                        last.then_inc(gates_used.sem, 1)

                def out_group(c, t):
                    n = TT * c + t
                    if c == 0 and t == 4:
                        pe.wait_ge(m_lo.sem, 16)
                    if t == 0:
                        pe.wait_ge(w_low.sem, w_low.done(CHUNK_NO["O", c] + 1))
                    if n >= 4:
                        pe.wait_ge(o_add.sem, o_add.done(n - 1 if c == 3 and t >= 2 else n - 3))
                    natural_group(c % 2, TOKEN_TILES[t], bank(out_bank(c, t), CW), order).then_inc(o_proj.sem, 1)

                pe.wait_ge(pt_even.sem, (NG + 1) // 2)
                pe.wait_ge(m_lo.sem, 15)
                pe.wait_ge(av_evac.sem, 8)
                for c in range(4):
                    for t in range(TT):
                        if c == 0 and t == 1:
                            head_norm_tensor(pe, 7, "sums")
                        if c == 0 and t == 3:
                            pe.wait_ge(s_mixed.sem, 8)
                        out_group(c, t)
                        if c == 0 and t == 1:
                            head_norm_tensor(pe, 7, "spread")
                        if c == 3 and t >= 2:
                            n2.transposes(pe, t - 2, t % 2)
                        if c == 3 and t == 6:
                            pe.wait_ge(low["g"].sem, 1)
                            pe.wait_ge(n2.lo.sem, n2.lo.done(8))
                            pe.wait_ge(o_add.sem, 3 * TT)
                            first_tile(0, "g")
                first_tile(1, "g")
                n2.transposes(pe, TT - 2, TT % 2)
                n2.transposes(pe, TT - 1, (TT - 1) % 2)
                pe.wait_ge(low["u"].sem, 1)
                pe.wait_ge(o_add.sem, 4 * TT)
                first_tile(0, "u")
                first_tile(1, "u")
                pe.wait_ge(n2.lo.sem, n2.lo.done(2 * TT))
                for n in (2, 3):
                    first_tile(n, "g")
                    first_tile(n, "u")

                def gate_up(j):
                    for n in range(4):
                        ft, th, g_bank, u_bank = ffn_tile(n)
                        if n == 0:
                            pe.wait_ge(low["g"].sem, low["g"].done(j + 1))
                        pe.wait_ge(hidden.sem, hidden.done(4 * j + (n - 1)))
                        turned_group(ffn_slot("g"), ft, X_PARTS[th], bank(g_bank))
                        if n == 0:
                            pe.wait_ge(low["u"].sem, low["u"].done(j + 1))
                        turned_group(ffn_slot("u"), ft, X_PARTS[th], bank(u_bank)).then_inc(gu_done.sem, 1)

                def down(j, par, weights=ffn_slot("d")):
                    dh, dl = weights
                    pe.wait_ge(low["d"].sem, low["d"].done(j + 1))
                    pe.wait_ge(f_low.sem, f_low.done(4 * j + 4))
                    for g in range(2 * TT):
                        t, half = g // 2, g % 2
                        if not (isinstance(j, int) and j == 0 and g < 4):
                            pe.wait_ge(dn_add.sem, dn_add.done(16 * j + (g - 3)))
                        for f in range(2):
                            w = slice(f * D + half * HALF, f * D + (half + 1) * HALF)
                            a = TOKEN_TILES[t]
                            for m, (fa, dw) in enumerate(((f_hi, dh), (f_hi, dl), (f_lo, dh))):
                                last = nc.tensor.matmul(bank(4 + g % 4), fa[:, par, f, a], dw[:, w],
                                                        start=f == 0 and m == 0, stop=f == 1 and m == 2)
                        last.then_inc(dn_done.sem, 1)

                gate_up(1)
                down(0, 0)
                with pe.Fori(0, (FG - 3) // 2) as r:
                    gate_up(2 * r + 2)
                    down(2 * r + 1, 1)
                    gate_up(2 * r + 3)
                    down(2 * r + 2, 0)
                gate_up(FG - 1)
                down(FG - 2, 1)
                down(FG - 1, 0, ffn_slot("g"))


_INS = ["x", "meta_tokens", "norm1_g", "w_in", "sb_norm_g", "hg_norm_g", "hg_lb_logits", "w_out",
        "norm2_g", "w_gate", "w_up", "w_down", "final_norm_g"]
_OUTS = [((1, SEQ, D), "float32")]


def kernel(**inputs):
    import numpy as _np
    import concourse.bacc as _bacc
    from concourse import mybir as _mybir
    from concourse.bass_utils import run_bass_kernel_spmd as _run

    nc = _bacc.Bacc("TRN2", target_bir_lowering=False, num_devices=1)
    arrays, args = {}, []
    for name in _INS:
        a = _np.ascontiguousarray(inputs[name])
        arrays[f"in_{name}_dram"] = a
        args.append(nc.dram_tensor(f"in_{name}_dram", a.shape, _mybir.dt.from_np(a.dtype), kind="ExternalInput").ap())
    for i, (shape, dtype) in enumerate(_OUTS):
        dt = _mybir.dt.from_np(_np.dtype(dtype))
        args.append(nc.dram_tensor(f"out_{i}_dram", shape, dt, kind="ExternalOutput").ap())
    hybrid_layer(nc, *args)
    r = _run(nc, [arrays], core_ids=[0])
    return r.results[0]["out_0_dram"]
```
